# Optimizing a Trainium2 kernel written in Bass

```python
import math
import jax, jax.numpy as jnp
from jax import lax
import numpy as np
import functools
import jax
import jax.numpy as jnp

D_MODEL = 1024
BATCH = 1
SEQ = 512
DEPTH = 1

SSD_D_INNER = 1024
SSD_HEAD_DIM = 64
SSD_HEADS = SSD_D_INNER // SSD_HEAD_DIM
SSD_GROUPS = 2
SSD_STATE = 128
SSD_CONV = 4
SSD_CHUNK = 128
SSD_CONV_DIM = SSD_D_INNER + 2 * SSD_GROUPS * SSD_STATE

ATTN_HEAD_DIM = 128
ATTN_HEADS_PER_GROUP = 4
DILATED_GROUPS = ((128, 1), (512, 4), (2048, 16))
ATTN_HEADS = ATTN_HEADS_PER_GROUP * len(DILATED_GROUPS)
ATTN_WIDTH = ATTN_HEADS * ATTN_HEAD_DIM
ATTN_OUT_WIDTH = ATTN_HEADS_PER_GROUP * ATTN_HEAD_DIM

POOL_WINDOWS = (2, 4, 8, 16)
POOL_WIDTH = 1024
POOL_GROUP_WIDTH = POOL_WIDTH // len(POOL_WINDOWS)

N_BRANCHES = 3
D_FF = 4 * D_MODEL
EPS = 1e-6
IN_SIZES = (SSD_D_INNER, SSD_CONV_DIM, SSD_HEADS, ATTN_WIDTH, ATTN_WIDTH, ATTN_WIDTH, POOL_WIDTH, N_BRANCHES * D_MODEL)
IN_WIDTH = SSD_D_INNER + SSD_CONV_DIM + SSD_HEADS + 3 * ATTN_WIDTH + POOL_WIDTH + N_BRANCHES * D_MODEL


def _rms(x, w):
    xf = x.astype(jnp.float32)
    y = xf * lax.rsqrt(jnp.mean(xf * xf, axis=-1, keepdims=True) + EPS)
    return (y * w.astype(jnp.float32)).astype(x.dtype)

def _alibi_slopes(n):
    def pow2(k):
        start = 2.0 ** (-8.0 / k)
        return [start ** (i + 1) for i in range(k)]
    if math.log2(n).is_integer():
        s = pow2(n)
    else:
        c = 2 ** math.floor(math.log2(n))
        s = pow2(c) + pow2(2 * c)[0::2][: n - c]
    return np.sort(np.asarray(s, np.float32))[::-1].copy()

def _causal_dwconv(x, w, bias):
    ch = x.shape[-1]
    y = lax.conv_general_dilated(x, w[:, None, :].astype(x.dtype), window_strides=(1,),
                                 padding=[(SSD_CONV - 1, 0)],
                                 dimension_numbers=('NWC', 'WIO', 'NWC'),
                                 feature_group_count=ch)
    return y + bias

def _ssd(xs, dt, A, B, C, D):
    b, S, H, P = xs.shape
    G, N, L = SSD_GROUPS, SSD_STATE, SSD_CHUNK
    J = H // G
    nc = S // L
    xc = xs.reshape(b, nc, L, G, J, P)
    X = xc * dt.reshape(b, nc, L, G, J)[..., None]
    a_cum = jnp.cumsum((dt * A).reshape(b, nc, L, G, J), axis=2)
    Bc = B.reshape(b, nc, L, G, N)
    Cc = C.reshape(b, nc, L, G, N)
    seg = a_cum[:, :, :, None] - a_cum[:, :, None, :]
    causal = jnp.tril(jnp.ones((L, L), bool))[:, :, None, None]
    decay = jnp.exp(jnp.where(causal, seg, -jnp.inf))
    cb = jnp.einsum('bclgn,bcsgn->bclsg', Cc, Bc)
    y_diag = jnp.einsum('bclsgj,bcsgjp->bclgjp', cb[..., None] * decay, X)
    Xd = X * jnp.exp(a_cum[:, :, -1:] - a_cum)[..., None]
    states = jnp.einsum('bclgn,bclgjp->bcgjpn', Bc, Xd)
    chunk_decay = jnp.exp(a_cum[:, :, -1])

    def step(h, inp):
        st, dec = inp
        return dec[..., None, None] * h + st, h

    h0 = jnp.zeros((b, G, J, P, N), X.dtype)
    _, prev = lax.scan(step, h0, (jnp.moveaxis(states, 1, 0), jnp.moveaxis(chunk_decay, 1, 0)))
    prev = jnp.moveaxis(prev, 0, 1)
    y_off = jnp.einsum('bclgn,bcgjpn->bclgjp', Cc, prev) * jnp.exp(a_cum)[..., None]
    y = y_diag + y_off + D.reshape(G, J)[:, :, None] * xc
    return y.reshape(b, S, H * P)

def _dilated_window_attn(q, k, v, steps, dilation, slopes):
    b, S, h, e = q.shape
    n = S // dilation
    nb = -(-n // steps)
    n_pad = nb * steps

    def to_sub(t):
        t = t.reshape(b, n, dilation, h, e).transpose(0, 3, 2, 1, 4)
        return jnp.pad(t, ((0, 0), (0, 0), (0, 0), (0, n_pad - n), (0, 0)))

    qs, ks, vs = to_sub(q), to_sub(k), to_sub(v)
    qb = qs.reshape(b, h, dilation, nb, steps, e)

    def band(t):
        tp = jnp.pad(t, ((0, 0), (0, 0), (0, 0), (steps, 0), (0, 0)))
        prev = tp[:, :, :, :n_pad].reshape(b, h, dilation, nb, steps, e)
        cur = t.reshape(b, h, dilation, nb, steps, e)
        return jnp.concatenate([prev, cur], axis=4)

    kb, vb = band(ks), band(vs)
    s = jnp.einsum('bhdnqe,bhdnke->bhdnqk', qb, kb) * (e ** -0.5)
    qi = jnp.arange(steps)[:, None]
    kj = jnp.arange(2 * steps)[None, :]
    rel = qi + steps - kj
    blk = jnp.arange(nb)[:, None, None]
    valid = (rel >= 0) & (rel <= steps) & (blk * steps + kj - steps >= 0)
    alibi = -slopes[:, None, None] * (rel * dilation).astype(jnp.float32)
    s = jnp.where(valid, s + alibi[:, None, None], -jnp.inf)
    lse = jax.nn.logsumexp(s, axis=-1)
    p = jnp.exp(s - lse[..., None])
    o = jnp.einsum('bhdnqk,bhdnke->bhdnqe', p, vb)
    o = o.reshape(b, h, dilation, n_pad, e)[:, :, :, :n].transpose(0, 3, 2, 1, 4).reshape(b, S, h, e)
    lse = lse.reshape(b, h, dilation, n_pad)[:, :, :, :n].transpose(0, 3, 2, 1).reshape(b, S, h)
    return o, lse

def _multi_scale_pool(u, w_mix):
    b, S, _ = u.shape
    ug = u.reshape(b, S, len(POOL_WINDOWS), POOL_GROUP_WIDTH)
    cs = jnp.cumsum(ug, axis=1)
    t = jnp.arange(S)
    outs = []
    for gi, w in enumerate(POOL_WINDOWS):
        csg = cs[:, :, gi]
        shifted = jnp.pad(csg, ((0, 0), (w, 0), (0, 0)))[:, :S]
        count = jnp.minimum(t + 1, w).astype(jnp.float32)[None, :, None]
        outs.append((csg - shifted) / count - ug[:, :, gi])
    pooled = jnp.stack(outs, axis=2)
    return jnp.einsum('bsgi,gio->bsgo', pooled, w_mix).reshape(b, S, POOL_WIDTH)

def _hybrid_mixer(h, w_in, conv_w, conv_b, dt_bias, a_log, d_skip, ssd_norm_w, w_ssd_out,
                  q_norm_w, k_norm_w, w_attn_out, w_pool_mix, pool_scale, w_pool_out, w_out, slopes):
    f32 = jnp.float32
    dtype = h.dtype
    b, S, _ = h.shape
    splits = np.cumsum(IN_SIZES)[:-1].tolist()
    z, xbc, dt_raw, q, k, v, u, gates = jnp.split(h @ w_in, splits, axis=-1)

    xbc = jax.nn.silu(_causal_dwconv(xbc, conv_w, conv_b)).astype(f32)
    xs, Bm, Cm = jnp.split(xbc, [SSD_D_INNER, SSD_D_INNER + SSD_GROUPS * SSD_STATE], axis=-1)
    dt = jax.nn.softplus(dt_raw.astype(f32) + dt_bias.astype(f32))
    A = -jnp.exp(a_log.astype(f32))
    y = _ssd(xs.reshape(b, S, SSD_HEADS, SSD_HEAD_DIM), dt, A,
             Bm.reshape(b, S, SSD_GROUPS, SSD_STATE), Cm.reshape(b, S, SSD_GROUPS, SSD_STATE),
             d_skip.astype(f32))
    y = (y * jax.nn.silu(z.astype(f32))).reshape(b, S, SSD_GROUPS, SSD_D_INNER // SSD_GROUPS)
    y = (y * lax.rsqrt(jnp.mean(y * y, axis=-1, keepdims=True) + EPS)).reshape(b, S, SSD_D_INNER)
    y_ssd = (y * ssd_norm_w.astype(f32)).astype(dtype) @ w_ssd_out

    qh = _rms(q.reshape(b, S, ATTN_HEADS, ATTN_HEAD_DIM).astype(f32), q_norm_w)
    kh = _rms(k.reshape(b, S, ATTN_HEADS, ATTN_HEAD_DIM).astype(f32), k_norm_w)
    vh = v.reshape(b, S, ATTN_HEADS, ATTN_HEAD_DIM).astype(f32)
    outs, lses = [], []
    for gi, (win, dil) in enumerate(DILATED_GROUPS):
        sl = slice(gi * ATTN_HEADS_PER_GROUP, (gi + 1) * ATTN_HEADS_PER_GROUP)
        o, lse = _dilated_window_attn(qh[:, :, sl], kh[:, :, sl], vh[:, :, sl], win // dil, dil, slopes[gi])
        outs.append(o)
        lses.append(lse)
    wts = jax.nn.softmax(jnp.stack(lses, axis=0), axis=0)
    o = jnp.sum(wts[..., None] * jnp.stack(outs, axis=0), axis=0).reshape(b, S, ATTN_OUT_WIDTH)
    y_attn = o.astype(dtype) @ w_attn_out

    y_pool = (_multi_scale_pool(u.astype(f32), w_pool_mix) * pool_scale).astype(dtype) @ w_pool_out

    g_ssd, g_attn, g_pool = jnp.split(jax.nn.sigmoid(gates.astype(f32)).astype(dtype), N_BRANCHES, axis=-1)
    return (g_ssd * y_ssd + g_attn * y_attn + g_pool * y_pool) @ w_out

def first_inputs(seed: int = 0) -> dict:
    key = jax.random.key(seed)
    ks = jax.random.split(key, 24)
    n = jax.random.normal
    L, D = DEPTH, D_MODEL
    u01 = jax.random.uniform(ks[9], (L, SSD_HEADS))
    dt0 = jnp.exp(u01 * (math.log(0.1) - math.log(0.001)) + math.log(0.001))
    return {
        "x": n(ks[0], (BATCH, SEQ, D), jnp.float32),
        "c": n(ks[1], (BATCH, D), jnp.float32),
        "w_ada": n(ks[2], (L, D, 6 * D)) * D ** -0.5,
        "b_ada": n(ks[3], (L, 6 * D)) * 0.01,
        "norm1_w": 1.0 + 0.05 * n(ks[4], (L, D)),
        "norm2_w": 1.0 + 0.05 * n(ks[5], (L, D)),
        "w_in": n(ks[6], (L, D, IN_WIDTH)) * D ** -0.5,
        "conv_w": n(ks[7], (L, SSD_CONV, SSD_CONV_DIM)) * SSD_CONV ** -0.5,
        "conv_b": n(ks[8], (L, SSD_CONV_DIM)) * 0.01,
        "dt_bias": dt0 + jnp.log(-jnp.expm1(-dt0)),
        "a_log": jnp.log(jax.random.uniform(ks[10], (L, SSD_HEADS), minval=1.0, maxval=16.0)),
        "d_skip": 1.0 + 0.05 * n(ks[11], (L, SSD_HEADS)),
        "ssd_norm_w": 1.0 + 0.05 * n(ks[12], (L, SSD_D_INNER)),
        "w_ssd_out": n(ks[13], (L, SSD_D_INNER, D)) * SSD_D_INNER ** -0.5,
        "q_norm_w": 1.0 + 0.05 * n(ks[14], (L, ATTN_HEAD_DIM)),
        "k_norm_w": 1.0 + 0.05 * n(ks[15], (L, ATTN_HEAD_DIM)),
        "w_attn_out": n(ks[16], (L, ATTN_OUT_WIDTH, D)) * ATTN_OUT_WIDTH ** -0.5,
        "w_pool_mix": n(ks[17], (L, len(POOL_WINDOWS), POOL_GROUP_WIDTH, POOL_GROUP_WIDTH)) * POOL_GROUP_WIDTH ** -0.5,
        "pool_scale": 1.0 + 0.05 * n(ks[18], (L, POOL_WIDTH)),
        "w_pool_out": n(ks[19], (L, POOL_WIDTH, D)) * POOL_WIDTH ** -0.5,
        "w_out": n(ks[20], (L, D, D)) * D ** -0.5,
        "w_ff1": n(ks[21], (L, D, D_FF)) * D ** -0.5,
        "w_ff2": n(ks[22], (L, D_FF, D)) * D_FF ** -0.5,
    }

def first_block(x, c, w_ada, b_ada, norm1_w, norm2_w, w_in, conv_w, conv_b, dt_bias, a_log, d_skip,
              ssd_norm_w, w_ssd_out, q_norm_w, k_norm_w, w_attn_out, w_pool_mix, pool_scale,
              w_pool_out, w_out, w_ff1, w_ff2):
    cond = jax.nn.silu(c)
    slopes = jnp.asarray(_alibi_slopes(ATTN_HEADS)).reshape(len(DILATED_GROUPS), ATTN_HEADS_PER_GROUP)
    for l in range(DEPTH):
        mod = (cond @ w_ada[l] + b_ada[l])[:, None, :]
        sh1, sc1, g1, sh2, sc2, g2 = jnp.split(mod, 6, axis=-1)
        h = _rms(x, norm1_w[l]) * (1 + sc1) + sh1
        x = x + g1 * _hybrid_mixer(h, w_in[l], conv_w[l], conv_b[l], dt_bias[l], a_log[l], d_skip[l],
                                   ssd_norm_w[l], w_ssd_out[l], q_norm_w[l], k_norm_w[l], w_attn_out[l],
                                   w_pool_mix[l], pool_scale[l], w_pool_out[l], w_out[l], slopes)
        h = _rms(x, norm2_w[l]) * (1 + sc2) + sh2
        x = x + g2 * (jnp.square(jax.nn.relu(h @ w_ff1[l])) @ w_ff2[l])
    return x


DEPTH_2 = 4

GRID_W = 64
CTX_LEN = 256
N_MIXERS = 3
NEG_INF = -1e30
ROPE_BASE = 10000.0
ADA_STD = 0.02

A_HEADS = 16
A_KV_HEADS = 4
A_HEAD_DIM = 64
A_WINDOW = 128
A_BLOCK = 128
A_WIDTH = A_HEADS * A_HEAD_DIM
A_KV_WIDTH = A_KV_HEADS * A_HEAD_DIM
A_IN = 2 * A_WIDTH + 2 * A_KV_WIDTH

B_HEADS = 8
B_NOPE = 128
B_ROPE = 64
B_VDIM = 128
B_Q_RANK = 256
B_KV_RANK = 128
B_BLOCK = 128
B_WIDTH = B_HEADS * B_VDIM
B_IN = B_Q_RANK + B_KV_RANK + B_ROPE + B_WIDTH

C_HEADS = 4
C_QK_DIM = 128
C_V_DIM = 256
C_QK_WIDTH = C_HEADS * C_QK_DIM
C_WIDTH = C_HEADS * C_V_DIM
C_CONV = 5
C_CHUNK = 128
C_IN = 2 * C_QK_WIDTH + 3 * C_WIDTH + 4 * C_HEADS
F_BIAS = 3.0


def rmsnorm(x, g):
    xf = x.astype(jnp.float32)
    y = xf * lax.rsqrt(jnp.mean(xf * xf, axis=-1, keepdims=True) + EPS)
    return (y * g.astype(jnp.float32)).astype(x.dtype)

def axial_rope(n_tok, rot_dim, dtype):
    rows = n_tok // GRID_W
    r, cidx = jnp.meshgrid(jnp.arange(rows), jnp.arange(GRID_W), indexing='ij')
    r = r.reshape(-1).astype(jnp.float32)
    cc = cidx.reshape(-1).astype(jnp.float32)
    n_freq = rot_dim // 4
    inv = ROPE_BASE ** (-jnp.arange(n_freq, dtype=jnp.float32) / n_freq)
    ang = jnp.concatenate([r[:, None] * inv, cc[:, None] * inv], axis=-1)
    return jnp.cos(ang).astype(dtype), jnp.sin(ang).astype(dtype)

def apply_rope(x, cos, sin):
    x1, x2 = x[..., 0::2], x[..., 1::2]
    cos, sin = cos[:, None, :], sin[:, None, :]
    return jnp.stack([x1 * cos - x2 * sin, x1 * sin + x2 * cos], axis=-1).reshape(x.shape)

def sink_softmax(logits, sink):
    m = jnp.maximum(jnp.max(logits, axis=-1, keepdims=True), sink)
    e = jnp.exp(logits - m)
    return e / (jnp.sum(e, axis=-1, keepdims=True) + jnp.exp(sink - m))

def centred_dwconv(x, w):
    k = w.shape[0]
    return lax.conv_general_dilated(x, w[:, None, :].astype(x.dtype), window_strides=(1,),
                                    padding=[(k // 2, k // 2)],
                                    dimension_numbers=('NWC', 'WIO', 'NWC'),
                                    feature_group_count=x.shape[-1])

def window_gqa_mixer(h_lat, h_ctx, need_ctx, w_in, sink, w_out):
    bsz, n_lat, _ = h_lat.shape
    n_ctx = h_ctx.shape[1]
    grp = A_HEADS // A_KV_HEADS
    scale = A_HEAD_DIM ** -0.5
    cuts = [A_WIDTH, A_WIDTH + A_KV_WIDTH, A_WIDTH + 2 * A_KV_WIDTH]
    sink_l = sink.astype(jnp.float32).reshape(A_KV_HEADS, grp, 1, 1)

    q_l, k_l, v_l, z_l = jnp.split(h_lat @ w_in, cuts, axis=-1)
    if need_ctx:
        q_c, k_c, v_c, z_c = jnp.split(h_ctx @ w_in, cuts, axis=-1)
    else:
        k_c, v_c = jnp.split(h_ctx @ w_in[:, A_WIDTH:A_WIDTH + 2 * A_KV_WIDTH], 2, axis=-1)
    k_c = k_c.reshape(bsz, n_ctx, A_KV_HEADS, A_HEAD_DIM)
    v_c = v_c.reshape(bsz, n_ctx, A_KV_HEADS, A_HEAD_DIM)

    cos, sin = axial_rope(n_lat, A_HEAD_DIM, h_lat.dtype)
    q_l = apply_rope(q_l.reshape(bsz, n_lat, A_HEADS, A_HEAD_DIM), cos, sin)
    q_l = q_l.reshape(bsz, n_lat, A_KV_HEADS, grp, A_HEAD_DIM)
    k_l = apply_rope(k_l.reshape(bsz, n_lat, A_KV_HEADS, A_HEAD_DIM), cos, sin)
    v_l = v_l.reshape(bsz, n_lat, A_KV_HEADS, A_HEAD_DIM)

    pad = ((0, 0), (A_BLOCK, A_BLOCK), (0, 0), (0, 0))
    k_pad, v_pad = jnp.pad(k_l, pad), jnp.pad(v_l, pad)
    band = 3 * A_BLOCK
    k_off = jnp.arange(band) - A_BLOCK
    in_window = jnp.abs(k_off[None, :] - jnp.arange(A_BLOCK)[:, None]) <= A_WINDOW
    ctx_ok = jnp.ones((A_BLOCK, n_ctx), dtype=bool)

    def block(n):
        start = n * A_BLOCK
        q_b = lax.dynamic_slice_in_dim(q_l, start, A_BLOCK, axis=1)
        k_b = jnp.concatenate([lax.dynamic_slice_in_dim(k_pad, start, band, axis=1), k_c], axis=1)
        v_b = jnp.concatenate([lax.dynamic_slice_in_dim(v_pad, start, band, axis=1), v_c], axis=1)
        kpos = start + k_off
        valid = in_window & ((kpos >= 0) & (kpos < n_lat))[None, :]
        mask = jnp.concatenate([valid, ctx_ok], axis=1)
        logits = jnp.einsum('bqkgd,bjkd->bkgqj', q_b, k_b).astype(jnp.float32) * scale
        p = sink_softmax(jnp.where(mask, logits, NEG_INF), sink_l)
        return jnp.einsum('bkgqj,bjkd->bqkgd', p.astype(v_b.dtype), v_b)

    o = lax.map(block, jnp.arange(n_lat // A_BLOCK))
    o_l = jnp.moveaxis(o, 0, 1).reshape(bsz, n_lat, A_WIDTH)
    y_l = (o_l * jax.nn.silu(z_l)) @ w_out

    y_c = None
    if need_ctx:
        q_c = q_c.reshape(bsz, n_ctx, A_KV_HEADS, grp, A_HEAD_DIM)
        logits = jnp.einsum('bqkgd,bjkd->bkgqj', q_c, k_c).astype(jnp.float32) * scale
        p = sink_softmax(logits, sink_l)
        o_c = jnp.einsum('bkgqj,bjkd->bqkgd', p.astype(v_c.dtype), v_c).reshape(bsz, n_ctx, A_WIDTH)
        y_c = (o_c * jax.nn.silu(z_c)) @ w_out
    return y_l, y_c

def mla_mixer(h_lat, h_ctx, need_ctx, w_in, g_qa, g_kva, w_uq, w_ukv, w_out):
    bsz, n_lat, _ = h_lat.shape
    n_ctx = h_ctx.shape[1]
    dqk = B_NOPE + B_ROPE
    scale = dqk ** -0.5
    cuts = [B_Q_RANK, B_Q_RANK + B_KV_RANK, B_Q_RANK + B_KV_RANK + B_ROPE]

    def queries(q_a):
        b, n, _ = q_a.shape
        return (rmsnorm(q_a, g_qa) @ w_uq).reshape(b, n, B_HEADS, dqk)

    def keys_values(kv_a, k_pe):
        b, n, _ = kv_a.shape
        kv = (rmsnorm(kv_a, g_kva) @ w_ukv).reshape(b, n, B_HEADS, B_NOPE + B_VDIM)
        k_nope, v = jnp.split(kv, [B_NOPE], axis=-1)
        k_pe = jnp.broadcast_to(k_pe[:, :, None, :], (b, n, B_HEADS, B_ROPE))
        return jnp.concatenate([k_nope, k_pe], axis=-1), v

    q_a_l, kv_a_l, kpe_l, z_l = jnp.split(h_lat @ w_in, cuts, axis=-1)
    if need_ctx:
        q_a_c, kv_a_c, kpe_c, z_c = jnp.split(h_ctx @ w_in, cuts, axis=-1)
    else:
        kv_a_c, kpe_c = jnp.split(h_ctx @ w_in[:, B_Q_RANK:cuts[2]], [B_KV_RANK], axis=-1)

    cos, sin = axial_rope(n_lat, B_ROPE, h_lat.dtype)
    q_l = queries(q_a_l)
    q_l = jnp.concatenate([q_l[..., :B_NOPE], apply_rope(q_l[..., B_NOPE:], cos, sin)], axis=-1)
    kpe_l = apply_rope(kpe_l[:, :, None, :], cos, sin)[:, :, 0]
    k_l, v_l = keys_values(kv_a_l, kpe_l)
    k_c, v_c = keys_values(kv_a_c, kpe_c)

    k_all = jnp.concatenate([k_c, k_l], axis=1)
    v_all = jnp.concatenate([v_c, v_l], axis=1)

    def block(q_b):
        logits = jnp.einsum('bqhd,bkhd->bhqk', q_b, k_all).astype(jnp.float32) * scale
        p = jax.nn.softmax(logits, axis=-1)
        return jnp.einsum('bhqk,bkhd->bqhd', p.astype(v_all.dtype), v_all)

    nb = n_lat // B_BLOCK
    q_blocks = jnp.moveaxis(q_l.reshape(bsz, nb, B_BLOCK, B_HEADS, dqk), 1, 0)
    o = lax.map(block, q_blocks)
    o_l = jnp.moveaxis(o, 0, 1).reshape(bsz, n_lat, B_WIDTH)
    y_l = (o_l * jax.nn.silu(z_l)) @ w_out

    y_c = None
    if need_ctx:
        q_c = queries(q_a_c)
        logits = jnp.einsum('bqhd,bkhd->bhqk', q_c, k_c).astype(jnp.float32) * scale
        p = jax.nn.softmax(logits, axis=-1)
        o_c = jnp.einsum('bhqk,bkhd->bqhd', p.astype(v_c.dtype), v_c).reshape(bsz, n_ctx, B_WIDTH)
        y_c = (o_c * jax.nn.silu(z_c)) @ w_out
    return y_l, y_c

def mlstm_chunkwise(q, k, v, i_pre, f_pre, state, need_out):
    b, h, t, dk = q.shape
    dv = v.shape[-1]
    nc = t // C_CHUNK
    q = q.reshape(b, h, nc, C_CHUNK, dk)
    k = k.reshape(b, h, nc, C_CHUNK, dk)
    v = v.reshape(b, h, nc, C_CHUNK, dv)
    ig = i_pre.reshape(b, h, nc, C_CHUNK)
    cum = jnp.cumsum(jax.nn.log_sigmoid(f_pre).reshape(b, h, nc, C_CHUNK), axis=-1)
    tot = cum[..., -1]

    w_end = tot[..., None] - cum + ig
    m_loc = jnp.max(w_end, axis=-1)
    e_end = jnp.exp(w_end - m_loc[..., None])
    c_loc = jnp.einsum('bhcs,bhcsv,bhcsk->bhcvk', e_end, v, k)
    n_loc = jnp.einsum('bhcs,bhcsk->bhck', e_end, k)

    def step(carry, inp):
        c_prev, n_prev, m_prev = carry
        tot_c, m_l, c_l, n_l = inp
        m_new = jnp.maximum(tot_c + m_prev, m_l)
        a = jnp.exp(tot_c + m_prev - m_new)
        bb = jnp.exp(m_l - m_new)
        new = (a[..., None, None] * c_prev + bb[..., None, None] * c_l,
               a[..., None] * n_prev + bb[..., None] * n_l, m_new)
        return new, carry

    to_front = lambda a: jnp.moveaxis(a, 2, 0)
    final, starts = lax.scan(step, state, (to_front(tot), to_front(m_loc), to_front(c_loc), to_front(n_loc)))
    if not need_out:
        return None, final
    c_st, n_st, m_st = (jnp.moveaxis(s, 0, 2) for s in starts)

    tri = jnp.tril(jnp.ones((C_CHUNK, C_CHUNK), dtype=bool))
    log_d = jnp.where(tri, cum[..., :, None] - cum[..., None, :] + ig[..., None, :], NEG_INF)
    inter = cum + m_st[..., None]
    m_t = jnp.maximum(inter, jnp.max(log_d, axis=-1))
    s_qk = jnp.einsum('bhctd,bhcsd->bhcts', q, k) * jnp.exp(log_d - m_t[..., None])
    a_t = jnp.exp(inter - m_t)
    num = (jnp.einsum('bhcts,bhcsv->bhctv', s_qk, v)
           + a_t[..., None] * jnp.einsum('bhcvk,bhctk->bhctv', c_st, q))
    den = jnp.sum(s_qk, axis=-1) + a_t * jnp.einsum('bhck,bhctk->bhct', n_st, q)
    out = num / jnp.maximum(jnp.abs(den), jnp.exp(-m_t))[..., None]
    return out.reshape(b, h, t, dv), final

def mlstm_mixer(h_lat, h_ctx, need_ctx, w_in, conv, b_gate, g_head, w_out):
    bsz = h_lat.shape[0]
    cuts = [2 * C_QK_WIDTH, 2 * C_QK_WIDTH + C_WIDTH, 2 * C_QK_WIDTH + 2 * C_WIDTH, 2 * C_QK_WIDTH + 3 * C_WIDTH]

    def prepare(h):
        b, n, _ = h.shape
        qk, v, o, z, gates = jnp.split(h @ w_in, cuts, axis=-1)
        qk = jax.nn.silu(centred_dwconv(qk, conv))
        q, k = jnp.split(qk, 2, axis=-1)
        heads = lambda a, d: jnp.moveaxis(a.reshape(b, n, C_HEADS, d), 2, 1).astype(jnp.float32)
        q = heads(q, C_QK_DIM)
        k = heads(k, C_QK_DIM) * (C_QK_DIM ** -0.5)
        v = heads(v, C_V_DIM)
        gates = jnp.moveaxis((gates + b_gate).astype(jnp.float32).reshape(b, n, 4, C_HEADS), 1, -1)
        return q, k, v, o, z, gates

    def finish(hsum, o, z):
        b, n, _ = o.shape
        hh = jnp.moveaxis(hsum, 1, 2).astype(o.dtype)
        hh = hh * jax.nn.sigmoid(o).reshape(b, n, C_HEADS, C_V_DIM)
        hh = rmsnorm(hh, g_head.reshape(C_HEADS, C_V_DIM)).reshape(b, n, C_WIDTH)
        return (hh * jax.nn.silu(z)) @ w_out

    q_c, k_c, v_c, o_c, z_c, g_c = prepare(h_ctx)
    q_l, k_l, v_l, o_l, z_l, g_l = prepare(h_lat)
    zero_state = (jnp.zeros((bsz, C_HEADS, C_V_DIM, C_QK_DIM), jnp.float32),
                  jnp.zeros((bsz, C_HEADS, C_QK_DIM), jnp.float32),
                  jnp.full((bsz, C_HEADS), NEG_INF, jnp.float32))
    flip = lambda a: jnp.flip(a, axis=2)

    hc_f, st_f = mlstm_chunkwise(q_c, k_c, v_c, g_c[:, 0], g_c[:, 1], zero_state, need_ctx)
    hl_f, _ = mlstm_chunkwise(q_l, k_l, v_l, g_l[:, 0], g_l[:, 1], st_f, True)
    hc_b, st_b = mlstm_chunkwise(flip(q_c), flip(k_c), flip(v_c), flip(g_c[:, 2]), flip(g_c[:, 3]), zero_state, need_ctx)
    hl_b, _ = mlstm_chunkwise(flip(q_l), flip(k_l), flip(v_l), flip(g_l[:, 2]), flip(g_l[:, 3]), st_b, True)

    y_l = finish(hl_f + flip(hl_b), o_l, z_l)
    y_c = finish(hc_f + flip(hc_b), o_c, z_c) if need_ctx else None
    return y_l, y_c

def _normal(key, shape, std):
    return std * jax.random.normal(key, shape, jnp.float32)

def _gain(key, n):
    return 1.0 + 0.1 * jax.random.normal(key, (n,), jnp.float32)

def _layer_params(key, kind):
    ks = jax.random.split(key, 10)
    p = {
        'w_ada': _normal(ks[0], (D_MODEL, 3 * D_MODEL), ADA_STD),
        'b_ada': _normal(ks[1], (3 * D_MODEL,), 0.02),
        'g_pre': _gain(ks[2], D_MODEL),
        'g_post': _gain(ks[3], D_MODEL),
    }
    if kind == 0:
        p['w_in'] = _normal(ks[4], (D_MODEL, A_IN), D_MODEL ** -0.5)
        p['sink'] = _normal(ks[5], (A_HEADS,), 0.5)
        p['w_out'] = _normal(ks[6], (A_WIDTH, D_MODEL), A_WIDTH ** -0.5)
    elif kind == 1:
        p['w_in'] = _normal(ks[4], (D_MODEL, B_IN), D_MODEL ** -0.5)
        p['g_qa'] = _gain(ks[5], B_Q_RANK)
        p['g_kva'] = _gain(ks[6], B_KV_RANK)
        p['w_uq'] = _normal(ks[7], (B_Q_RANK, B_HEADS * (B_NOPE + B_ROPE)), B_Q_RANK ** -0.5)
        p['w_ukv'] = _normal(ks[8], (B_KV_RANK, B_HEADS * (B_NOPE + B_VDIM)), B_KV_RANK ** -0.5)
        p['w_out'] = _normal(ks[9], (B_WIDTH, D_MODEL), B_WIDTH ** -0.5)
    else:
        offset = jnp.repeat(jnp.array([0.0, F_BIAS, 0.0, F_BIAS], jnp.float32), C_HEADS)
        p['w_in'] = _normal(ks[4], (D_MODEL, C_IN), D_MODEL ** -0.5)
        p['conv'] = _normal(ks[5], (C_CONV, 2 * C_QK_WIDTH), C_CONV ** -0.5)
        p['b_gate'] = offset + _normal(ks[6], (4 * C_HEADS,), 0.3)
        p['g_head'] = _gain(ks[7], C_WIDTH)
        p['w_out'] = _normal(ks[8], (C_WIDTH, D_MODEL), C_WIDTH ** -0.5)
    return p

def second_inputs(seed: int = 0) -> dict:
    key = jax.random.key(seed)
    k_x, k_c, k_ctx, k_cc, k_layers = jax.random.split(key, 5)
    inputs = {
        'x': jax.random.normal(k_x, (BATCH, SEQ, D_MODEL), jnp.float32),
        'c': jax.random.normal(k_c, (BATCH, D_MODEL), jnp.float32),
        'ctx': jax.random.normal(k_ctx, (BATCH, CTX_LEN, D_MODEL), jnp.float32),
        'c_ctx': jax.random.normal(k_cc, (D_MODEL,), jnp.float32),
    }
    for i, lk in enumerate(jax.random.split(k_layers, DEPTH_2)):
        for name, val in _layer_params(lk, i % N_MIXERS).items():
            inputs[f'l{i}_{name}'] = val
    return inputs

def modulation(cvec, w_ada, b_ada):
    return jnp.split(jax.nn.silu(cvec) @ w_ada + b_ada, 3, axis=-1)

def second_block(x, c, ctx, c_ctx,
              l0_w_ada, l0_b_ada, l0_g_pre, l0_g_post, l0_w_in, l0_sink, l0_w_out,
              l1_w_ada, l1_b_ada, l1_g_pre, l1_g_post, l1_w_in, l1_g_qa, l1_g_kva, l1_w_uq, l1_w_ukv, l1_w_out,
              l2_w_ada, l2_b_ada, l2_g_pre, l2_g_post, l2_w_in, l2_conv, l2_b_gate, l2_g_head, l2_w_out,
              l3_w_ada, l3_b_ada, l3_g_pre, l3_g_post, l3_w_in, l3_sink, l3_w_out):
    layers = [
        (l0_w_ada, l0_b_ada, l0_g_pre, l0_g_post,
         functools.partial(window_gqa_mixer, w_in=l0_w_in, sink=l0_sink, w_out=l0_w_out)),
        (l1_w_ada, l1_b_ada, l1_g_pre, l1_g_post,
         functools.partial(mla_mixer, w_in=l1_w_in, g_qa=l1_g_qa, g_kva=l1_g_kva,
                           w_uq=l1_w_uq, w_ukv=l1_w_ukv, w_out=l1_w_out)),
        (l2_w_ada, l2_b_ada, l2_g_pre, l2_g_post,
         functools.partial(mlstm_mixer, w_in=l2_w_in, conv=l2_conv, b_gate=l2_b_gate,
                           g_head=l2_g_head, w_out=l2_w_out)),
        (l3_w_ada, l3_b_ada, l3_g_pre, l3_g_post,
         functools.partial(window_gqa_mixer, w_in=l3_w_in, sink=l3_sink, w_out=l3_w_out)),
    ]
    x_lat, x_ctx = x, ctx
    for i in range(DEPTH_2):
        w_ada, b_ada, g_pre, g_post, mixer = layers[i]
        need_ctx = i < DEPTH_2 - 1
        sh_l, sc_l, gt_l = modulation(c, w_ada, b_ada)
        sh_c, sc_c, gt_c = modulation(c_ctx, w_ada, b_ada)
        h_l = rmsnorm(x_lat, g_pre) * (1.0 + sc_l[:, None, :]) + sh_l[:, None, :]
        h_c = rmsnorm(x_ctx, g_pre) * (1.0 + sc_c) + sh_c
        y_l, y_c = mixer(h_l, h_c, need_ctx=need_ctx)
        x_lat = x_lat + gt_l[:, None, :] * rmsnorm(y_l, g_post)
        if need_ctx:
            x_ctx = x_ctx + gt_c * rmsnorm(y_c, g_post)
    return x_lat


def setup_inputs(seed=0):
    out = dict(first_inputs(seed))
    for name, value in second_inputs(seed + 1).items():
        if name != "x":
            out[name + "_2"] = value
    return out


def reference(
    x, c, w_ada, b_ada, norm1_w, norm2_w, w_in, conv_w, conv_b, dt_bias, a_log, d_skip,
    ssd_norm_w, w_ssd_out, q_norm_w, k_norm_w, w_attn_out, w_pool_mix, pool_scale, w_pool_out,
    w_out, w_ff1, w_ff2, c_2, ctx_2, c_ctx_2, l0_w_ada_2, l0_b_ada_2, l0_g_pre_2, l0_g_post_2,
    l0_w_in_2, l0_sink_2, l0_w_out_2, l1_w_ada_2, l1_b_ada_2, l1_g_pre_2, l1_g_post_2,
    l1_w_in_2, l1_g_qa_2, l1_g_kva_2, l1_w_uq_2, l1_w_ukv_2, l1_w_out_2, l2_w_ada_2, l2_b_ada_2,
    l2_g_pre_2, l2_g_post_2, l2_w_in_2, l2_conv_2, l2_b_gate_2, l2_g_head_2, l2_w_out_2,
    l3_w_ada_2, l3_b_ada_2, l3_g_pre_2, l3_g_post_2, l3_w_in_2, l3_sink_2, l3_w_out_2,
):
    x = first_block(
        x, c, w_ada, b_ada, norm1_w, norm2_w, w_in, conv_w, conv_b, dt_bias, a_log, d_skip,
        ssd_norm_w, w_ssd_out, q_norm_w, k_norm_w, w_attn_out, w_pool_mix, pool_scale,
        w_pool_out, w_out, w_ff1, w_ff2,
    )
    return second_block(
        x, c_2, ctx_2, c_ctx_2, l0_w_ada_2, l0_b_ada_2, l0_g_pre_2, l0_g_post_2, l0_w_in_2,
        l0_sink_2, l0_w_out_2, l1_w_ada_2, l1_b_ada_2, l1_g_pre_2, l1_g_post_2, l1_w_in_2,
        l1_g_qa_2, l1_g_kva_2, l1_w_uq_2, l1_w_ukv_2, l1_w_out_2, l2_w_ada_2, l2_b_ada_2,
        l2_g_pre_2, l2_g_post_2, l2_w_in_2, l2_conv_2, l2_b_gate_2, l2_g_head_2, l2_w_out_2,
        l3_w_ada_2, l3_b_ada_2, l3_g_pre_2, l3_g_post_2, l3_w_in_2, l3_sink_2, l3_w_out_2,
    )


_drawn_inputs = setup_inputs


def setup_inputs(seed=0):
    import zlib

    import numpy as np

    out = dict(_drawn_inputs(seed))
    spreads = {}
    factors = {'b_ada': 2.855,
     'conv_b': 8.0,
     'd_skip': 7.369,
     'ssd_norm_w': 3.772,
     'q_norm_w': 8.0,
     'k_norm_w': 8.0,
     'pool_scale': 3.692,
     'l0_b_ada_2': 2.694,
     'l0_sink_2': 21.485,
     'l1_b_ada_2': 3.04,
     'l1_g_qa_2': 7.459,
     'l2_b_ada_2': 3.45,
     'l3_b_ada_2': 3.664,
     'l3_sink_2': 64.0,
     'l0_g_post_2': 2.718,
     'l1_g_post_2': 3.461,
     'l2_g_post_2': 3.478,
     'l2_g_head_2': 3.384,
     'l3_g_pre_2': 2.908,
     'l3_g_post_2': 3.638}
    for name, (base, spread) in spreads.items():
        noise = np.random.default_rng([zlib.crc32(name.encode()), seed]).standard_normal(out[name].shape)
        drawn = base * np.exp(spread * noise) if base else spread * noise
        out[name] = jnp.asarray(drawn.astype(out[name].dtype))
    for name, factor in factors.items():
        out[name] = (out[name] * factor).astype(out[name].dtype)
    return out
```

```python
import math
from contextlib import ExitStack

import numpy as np
import concourse.bass as bass
from concourse import mybir

F32 = mybir.dt.float32
F32R = mybir.dt.float32r
ACT = mybir.ActivationFunctionType
ALU = mybir.AluOpType
AX = mybir.AxisListType

P = 128
D = 1024
KC = D // P
S = 512
SC = 256
T2 = S + SC
SLOT = 2048
EPS = 1e-6
NEG = -1.0e30

SSD_HEADS, SSD_P, SSD_N = 16, 64, 128
A_SCALE = 64 ** -0.5
B_SCALE = 192 ** -0.5
FF = 4096



HEAD_ORDER = [h for c in range(2) for i in range(4) for h in (8 * c + i, 8 * c + 4 + i)]
HEAD_COLS = [h * 64 + e for h in HEAD_ORDER for e in range(64)]


def slot_plan():
    plan = []

    def slots(section, name, rows, cols):
        kc = (rows[1] - rows[0]) // P
        width = SLOT // kc
        first = len(plan)
        for c in range(0, len(cols), width):
            plan.append((name, rows[0], rows[1], tuple(cols[c:c + width])))
        sections[section] = (first, len(plan) - first)

    sections = {}
    R = lambda a, n: list(range(a, a + n))
    full = (0, D)
    z0, xbc0, dt0 = 0, 1024, 2560
    q0 = 2576
    k0, v0, u0, g0 = q0 + 1536, q0 + 3072, q0 + 4608, q0 + 5632
    slots("z", "w_in", full, R(z0, 1024))
    slots("xbc", "w_in", full, R(xbc0, 1536))
    slots("dt", "w_in", full, R(dt0, 16))
    slots("_dt", "w_in", full, R(dt0, 16))
    for c in range(4):
        slots(f"g_ssd{c}", "w_in", full, R(g0 + 256 * c, 256))
        slots(f"ssd_out{c}", "w_ssd_out", full, R(256 * c, 256))
    for j in range(4):
        cols = []
        for base in (q0, k0, v0):
            for g in range(3):
                cols += R(base + (4 * g + j) * P, P)
        slots(f"qkv{j}", "w_in", full, cols)
    for c in range(2):
        slots(f"attn_out{c}", "w_attn_out", (0, 512), R(512 * c, 512))
        slots(f"g_attn{c}", "w_in", full, R(g0 + 1024 + 512 * c, 512))
    slots("u", "w_in", full, R(u0, 1024))
    slots("mix", "mix", (0, 1024), R(0, 256))
    slots("_mix", "w_in", full, R(dt0, 16))
    for c in range(4):
        slots(f"g_pool{c}", "w_in", full, R(g0 + 2048 + 256 * c, 256))
        slots(f"pool_out{c}", "w_pool_out", full, R(256 * c, 256))
    slots("out", "w_out", full, R(0, 1024))
    for b in range(4):
        slots(f"ff1_{b}", "w_ff1", full, R(1024 * b, 1024))
        slots(f"ff2_{b}", "w_ff2", (1024 * b, 1024 * b + 1024), R(0, 1024))

    hcols = HEAD_COLS
    for l in (0, 3):
        w = f"l{l}_w_in_2"
        slots(f"A{l}q", w, full, hcols)
        slots(f"A{l}k", w, full, R(1024, 256))
        slots(f"A{l}v", w, full, R(1280, 256))
        slots(f"A{l}z", w, full, [1536 + c for c in hcols])
        slots(f"A{l}o", f"l{l}_w_out_2", full, R(0, 1024))
        if l == 0:
            w = "l1_w_in_2"
            slots("Bin", w, full, R(0, 256) + R(256, 128) + R(384, 64) + R(384, 64))
            slots("Bz", w, full, R(448, 1024))
            slots("Bq", "l1_w_uq_2", (0, 256),
                  [h * 192 + e for h in range(8) for e in range(128)]
                  + [h * 192 + 128 + e for h in range(8) for e in range(64)])
            slots("Bk", "l1_w_ukv_2", (0, 128), [h * 256 + e for h in range(8) for e in range(128)]
                  + [h * 256 + 128 + e for h in range(8) for e in range(128)])
            slots("_Bk", w, full, R(0, 16))
            slots("Bo", "l1_w_out_2", full, R(0, 1024))
            w = "l2_w_in_2"
            slots("Cqk", w, full, R(0, 1024))
            slots("Cv", w, full, R(1024, 1024))
            slots("Cg", w, full, R(4096, 16))
            slots("_Cg", w, full, R(4096, 16))
            slots("Cog", w, full, R(2048, 1024))
            slots("Cz", w, full, R(3072, 1024))
            slots("Co", "l2_w_out_2", full, R(0, 1024))
    return plan, sections


PLAN, SECTIONS = slot_plan()


def ada_plan():
    return [("w_ada", c) for c in range(24)] + [(f"l{l}_w_ada_2", c) for l in range(4) for c in range(12)]


COLS = {"c": 8, "c_2": 8, "c_ctx_2": 8, "b_ada": 48, "norm1_w": 8, "norm2_w": 8, "conv_w": 48,
        "conv_b": 12, "d_skip": 8, "ssd_norm_w": 8, "q_norm_w": 1, "k_norm_w": 1, "pool_scale": 8,
        "l1_g_qa_2": 2, "l1_g_kva_2": 1, "l2_conv_2": 40}
for _l in range(4):
    COLS |= {f"l{_l}_b_ada_2": 24, f"l{_l}_g_pre_2": 8, f"l{_l}_g_post_2": 8}
COL_AT, _n = {}, 0
for _k, _w in COLS.items():
    COL_AT[_k] = _n
    _n += _w
N_COLS = _n

ROWS = {"dt_bias": 16, "a_log": 16, "l2_b_gate_2": 16, "l0_sink_2": 16, "l3_sink_2": 16, "l2_g_head_2": 1024}
ROW_AT, _n = {}, 0
for _k, _w in ROWS.items():
    ROW_AT[_k] = _n
    _n += _w
N_ROWS = _n

CONSTS = {"ident": 128, "ones": 128, "tri": 128, "triT": 128, "mask_le": 128, "mask_ge": 128,
          "swap": 128, "cos": 512, "sin": 512, "negd": 512, "mask0": 512, "mask1": 512, "mask2": 512,
          "pool_inv": 64}
CONST_AT, _n = {}, 0
for _k, _w in CONSTS.items():
    CONST_AT[_k] = _n
    _n += _w
N_CONSTS = _n


def constants():
    out = np.zeros((P, N_CONSTS), np.float32)
    p = np.arange(P)[:, None]
    f = np.arange(P)[None, :]

    def put(name, a):
        out[:, CONST_AT[name]:CONST_AT[name] + CONSTS[name]] = a

    put("ident", p == f)
    put("ones", 1.0)
    put("tri", p <= f)
    put("triT", p >= f)
    put("mask_le", np.where(p <= f, 0.0, NEG))
    put("mask_ge", np.where(p >= f, 0.0, NEG))
    sw = np.zeros((P, P), np.float32)
    for i in range(0, P, 2):
        sw[i + 1, i] = -1.0
        sw[i, i + 1] = 1.0
    put("swap", sw)
    t = np.arange(S)
    n_freq = 16
    inv = (np.float32(10000.0) ** (-np.arange(n_freq, dtype=np.float32) / np.float32(n_freq))).astype(np.float32)
    ang = np.concatenate([(t // 64).astype(np.float32)[:, None] * inv,
                          (t % 64).astype(np.float32)[:, None] * inv], axis=1)
    ang = np.repeat(ang, 2, axis=1).T
    ang = np.concatenate([ang, ang], axis=0)
    put("cos", np.cos(ang))
    put("sin", np.sin(ang))
    c = np.arange(512)[None, :]
    dist = p + 384 - c
    put("negd", -dist.astype(np.float32))
    for g, (win, dil) in enumerate(((128, 1), (512, 4), (2048, 16))):
        ok = (dist >= 0) & (dist % dil == 0) & (dist <= win)
        put(f"mask{g}", np.where(ok, 0.0, NEG))
    inv_count = np.concatenate([1.0 / np.minimum(np.arange(16) + 1, w) for w in (2, 4, 8, 16)])
    put("pool_inv", inv_count[None, :].astype(np.float32))
    return out


def alibi_slopes(n):
    def pow2(k):
        start = 2.0 ** (-8.0 / k)
        return [start ** (i + 1) for i in range(k)]
    c = 2 ** math.floor(math.log2(n))
    s = pow2(n) if c == n else pow2(c) + pow2(2 * c)[0::2][: n - c]
    return sorted((float(np.float32(x)) for x in s), reverse=True)



class Signal:

    def __init__(self, handle):
        self.sem = handle
        self.base = 0

    def at(self, n):
        return self.base + n

    def stage_over(self, n):
        self.base += n


class Chain:

    def __init__(self, handle):
        self.sem = handle
        self.count = 0
        self.loop = 0

    def __call__(self, eng, ins):
        ins.then_inc(self.sem, 1)
        self.count += 1
        eng.wait_ge(self.sem, self.loop + self.count)


class Kernel:

    RING, CONST, ARENA, TOP = 0, 49152, 69632, 212832

    def __init__(self, nc, ctx, io):
        self.nc, self.ctx, self.io = nc, ctx, io
        sem = lambda name: ctx.enter_context(nc.semaphore(name))
        self.raw_loaded = [sem("raw_loaded0"), sem("raw_loaded1")]
        self.hi_ready = sem("hi_ready")
        self.lo_ready = sem("lo_ready")
        self.stage_end = sem("stage_end")
        self.stages = 0
        self.tile_done = Signal(sem("tile_done"))
        self.tile_free = Signal(sem("tile_free"))
        self.tile_free.base = 8
        self.staged = Signal(sem("staged"))
        self.finished = Signal(sem("finished"))
        self.signals = {}
        self.dve_chain = Chain(sem("dve_chain"))
        self.act_chain = Chain(sem("act_chain"))
        self.dma_n = {}
        self.tensors = {}
        self.first_byte = (nc.sbuf_base + 31) // 32 * 32

        at = self.at
        self.raw = at("raw", 0, [P, 2, SLOT])
        self.w_hi = at("w_hi", 16384, [P, 2, SLOT], F32R)
        self.w_lo = at("w_lo", 32768, [P, 2, SLOT], F32R)
        o = self.CONST
        self.const = at("const", o, [P, N_COMMON])
        o += 4 * N_COMMON
        self.cols = at("cols", o, [P, N_COLS])
        o += 4 * N_COLS
        self.rows = at("rows", o, [P, N_ROWS])
        o += 4 * N_ROWS
        self.cond = at("cond", o, [P, 2, KC, 2])
        o += 4 * 32
        self.mod1 = at("mod1", o, [P, 48])
        o += 4 * 48
        self.mod2 = at("mod2", o, [P, 4, 24, 2])
        o += 4 * 192
        self.coef = at("coef", o, [P, 2, KC])
        o += 4 * 16
        self.coef2 = at("coef2", o, [P, 4, KC, 2])
        o += 4 * 64
        self.gate2 = at("gate2", o, [P, 4, KC, 2])
        o += 4 * 64
        self.eps = at("eps", o, [P, 1])
        o += 4
        assert o <= self.ARENA, o
        self.psum = ctx.enter_context(nc.psum_tensor("psum", [P, 8, 512], F32))

    def sem_named(self, name):
        if name not in self.signals:
            self.signals[name] = Signal(self.ctx.enter_context(self.nc.semaphore(name)))
        return self.signals[name]

    def at(self, name, offset, shape, dtype=F32):
        size = 4 * int(np.prod(shape[1:]))
        assert offset + size <= self.TOP, (name, offset + size)
        key = (name, offset, tuple(shape), str(dtype))
        if key not in self.tensors:
            self.tensors[key] = self.nc.alloc_sbuf_tensor_at(f"{name}_{len(self.tensors)}", shape, dtype,
                                                             offset=self.first_byte + (offset + 31) // 32 * 32)
        return self.tensors[key]

    def col(self, name, i=0, n=1):
        return self.cols[:, COL_AT[name] + i:COL_AT[name] + i + n]

    def row(self, name):
        return self.rows[:, ROW_AT[name]:ROW_AT[name] + ROWS[name]]

    def cst(self, name):
        return self.const[:, CONST_AT[name]:CONST_AT[name] + CONSTS[name]]

    def end_stage(self, block):
        self.stages += 1
        n = 3 * self.stages

        @block.tensor
        def _(pe):
            pe.drain().then_inc(self.stage_end, 1)
            pe.wait_ge(self.stage_end, n)

        @block.vector
        def _(dve):
            dve.drain().then_inc(self.stage_end, 1)
            dve.wait_ge(self.stage_end, n)

        @block.scalar
        def _(act):
            act.drain().then_inc(self.stage_end, 1)
            act.wait_ge(self.stage_end, n)


N_COMMON = CONST_AT["negd"]
N_SLOTS = len(PLAN)
assert N_SLOTS % 2 == 0


def weight_stream(k, block):
    stream = k.io["stream"]

    @block.sync
    def _(sp):
        for s in range(2):
            sp.dma_start(k.raw[:, s], stream[s]).then_inc(k.raw_loaded[s], 16)
        with sp.Fori(1, N_SLOTS // 2) as i:
            for s in range(2):
                sp.wait_ge(k.lo_ready, i * 2 - 1 + s)
                sp.dma_start(k.raw[:, s], stream[bass.ds(i * 2 + s, 1)].rearrange("a p n -> p (a n)")) \
                    .then_inc(k.raw_loaded[s], 16)

    @block.gpsimd
    def _(pool):
        with pool.Fori(0, N_SLOTS // 2) as i:
            for s in range(2):
                pool.wait_ge(k.hi_ready, i * 2 + s + 1)
                pool.tensor_tensor(k.w_lo[:, s], k.raw[:, s], k.w_hi[:, s].bitcast(F32), ALU.subtract) \
                    .then_inc(k.lo_ready, 1)


def refill_hi(k, act, s, turn):
    act.wait_ge(k.raw_loaded[s], turn * 16 + 16)
    act.activation(k.w_hi[:, s], k.raw[:, s], ACT.Copy).then_inc(k.hi_ready, 1)


def skip_slot(k, block, slot):
    @block.scalar
    def _(act):
        act.wait_ge(k.lo_ready, slot + 1)
        if slot + 2 < N_SLOTS:
            refill_hi(k, act, slot % 2, (slot + 2) // 2)


def products(pe, out, lhs, rhs, start, stop):
    pe.matmul(out, lhs[0], rhs[0], start=start, stop=False)
    pe.matmul(out, lhs[0], rhs[1], start=False, stop=False)
    return pe.matmul(out, lhs[1], rhs[0], start=False, stop=stop)


def dense(k, block, sections, tiles, act_tile=None, dve_tile=None, act_last=None, loop=False,
          dve_chained=0):
    first = SECTIONS[sections[0]][0]
    count = sum(SECTIONS[x][1] for x in sections)
    n_slots = 2 if loop else count
    per = [len(tiles(s, k.w_hi[:, 0], k.w_lo[:, 0])) for s in range(n_slots)]
    at = [sum(per[:s]) for s in range(n_slots + 1)]
    turns = count // 2 if loop else 1
    ring = 4 if max(per) <= 2 else 6 if max(per) % 3 == 0 else 8
    n_t = at[-1]
    assert not loop or (n_t % ring == 0 and first % 2 == 0 and count % 2 == 0)

    @block.tensor
    def _(pe):
        def turn(i):
            for s in range(n_slots):
                par = (first + s) % 2
                pe.wait_ge(k.lo_ready, i * 2 + (first + s + 1))
                for n, (cut, pairs) in enumerate(tiles(s, k.w_hi[:, par], k.w_lo[:, par])):
                    t = at[s] + n
                    pe.wait_ge(k.tile_free.sem, i * n_t + k.tile_free.at(t + 1 - ring))
                    out = cut(k.psum[:, t % ring])
                    for j, (lhs, rhs) in enumerate(pairs):
                        last = products(pe, out, lhs, rhs, j == 0, j == len(pairs) - 1)
                    last.then_inc(k.tile_done.sem, 1)

        if loop:
            with pe.Fori(0, turns) as i:
                turn(i)
        else:
            turn(0)

    @block.scalar
    def _(act):
        def finish(i, t):
            act.wait_ge(k.finished.sem, i * n_t + k.finished.at(t + 1))
            act_last(act, i, t).then_inc(k.tile_free.sem, 1)

        def turn(i, refill=True):
            for s in range(n_slots):
                for t in range(at[s], at[s + 1]):
                    if act_tile is not None:
                        act.wait_ge(k.tile_done.sem, i * n_t + k.tile_done.at(t + 1))
                        done = act_tile(act, i, t, k.psum[:, t % ring])
                        done.then_inc((k.tile_free if dve_tile is None else k.staged).sem, 1)
                    if act_last is not None and t > 0:
                        finish(i, t - 1)
                if per[s]:
                    act.wait_ge(k.tile_done.sem, i * n_t + k.tile_done.at(at[s + 1]))
                else:
                    act.wait_ge(k.lo_ready, i * 2 + (first + s + 1))
                if refill if loop else first + s + 2 < N_SLOTS:
                    refill_hi(k, act, (first + s) % 2, i + (first + s + 2) // 2)
            if act_last is not None:
                finish(i, n_t - 1)

        if loop and first + count == N_SLOTS:
            with act.Fori(0, turns - 1) as i:
                turn(i)
            turn(turns - 1, refill=False)
        elif loop:
            with act.Fori(0, turns) as i:
                turn(i)
        else:
            turn(0)

    if dve_tile is not None:
        @block.vector
        def _(dve):
            def turn(i):
                k.dve_chain.loop = i * dve_chained
                for t in range(n_t):
                    source = k.tile_done if act_tile is None else k.staged
                    dve.wait_ge(source.sem, i * n_t + source.at(t + 1))
                    done = dve_tile(dve, i, t, k.psum[:, t % ring])
                    done.then_inc((k.tile_free if act_last is None else k.finished).sem, 1)

            before = k.dve_chain.count
            if loop:
                with dve.Fori(0, turns) as i:
                    turn(i)
                assert k.dve_chain.count - before == dve_chained, k.dve_chain.count - before
                k.dve_chain.count = before + dve_chained * turns
            else:
                turn(0)
            k.dve_chain.loop = 0

    k.tile_done.stage_over(n_t * turns)
    k.tile_free.stage_over(n_t * turns)
    if act_tile is not None and dve_tile is not None:
        k.staged.stage_over(n_t * turns)
    if act_last is not None:
        k.finished.stage_over(n_t * turns)
    k.end_stage(block)


def feature_major(a, kc, parts, slot_cols=None, chunks=(0, 1)):
    width = SLOT // kc

    def tiles(s, hi, lo):
        hi = hi.rearrange("p (k n) -> p k n", k=kc)
        lo = lo.rearrange("p (k n) -> p k n", k=kc)
        out = []
        use = chunks(s) if callable(chunks) else chunks
        for c in use:
            for t0, t1 in parts:
                out.append((lambda bank, n=t1 - t0: bank[:, 0:n],
                            [((hi[:, j, c * P:(c + 1) * P], lo[:, j, c * P:(c + 1) * P]),
                              (a[0][:, j, t0:t1], a[1][:, j, t0:t1])) for j in range(kc)]))
        return out

    return tiles


def split(k, dve, hi, lo, x):
    k.dve_chain(dve, dve.tensor_copy(hi, x))
    return dve.tensor_tensor(lo, x, hi.bitcast(F32), ALU.subtract)



def setup(k, block):
    loaded = k.sem_named("consts_loaded")

    @block.scalar
    def _(act):
        act.dma_start(k.const[:], k.io["consts"][:, 0:N_COMMON]).then_inc(loaded.sem, 16)
        act.dma_start(k.cols[:], k.io["cols"]).then_inc(loaded.sem, 16)
        act.dma_start(k.rows[:], k.io["rows"]).then_inc(loaded.sem, 16)
        for s in range(2):
            refill_hi(k, act, s, 0)
        act.wait_ge(loaded.sem, 48)
        for b, (own, other) in enumerate((("c", "c"), ("c_2", "c_ctx_2"))):
            act.activation(k.cond[:, b, :, 0], k.col(own, 0, KC), ACT.Silu)
            act.activation(k.cond[:, b, :, 1], k.col(other, 0, KC), ACT.Silu)

    @block.vector
    def _(dve):
        dve.nop().then_inc(k.tile_free.sem, 8)
        dve.memset(k.eps[:], EPS)

    k.end_stage(block)


def modulation(k, block):
    ada = k.io["ada"]
    ring = k.at("ada_ring", k.ARENA, [P, 4, KC, 256])
    loaded = [k.ctx.enter_context(k.nc.semaphore(f"ada_loaded{s}")) for s in range(4)]
    used = k.ctx.enter_context(k.nc.semaphore("ada_used"))
    out1 = k.psum[:, 0, 0:48]
    out2 = k.psum[:, 1, 0:192].rearrange("p (n two) -> p n two", two=2)
    n_first, n_all = 24, 72

    @block.scalar
    def _(act):
        for s in range(4):
            act.dma_start(ring[:, s], ada[s].rearrange("p (k n) -> p k n", k=KC)).then_inc(loaded[s], 16)
        with act.Fori(1, n_all // 4) as i:
            for s in range(4):
                act.wait_ge(used, i * 4 - 3 + s)
                act.dma_start(ring[:, s], ada[bass.ds(i * 4 + s, 1)].rearrange("a p (k n) -> p (a k) n", k=KC)) \
                    .then_inc(loaded[s], 16)

    @block.tensor
    def _(pe):
        def slots(i, base, n, out, rhs):
            for s in range(4):
                pe.wait_ge(loaded[s], i * 16 + 16)
                for c in range(2):
                    for j in range(KC):
                        last = pe.matmul(out(i, 2 * s + c), ring[:, s, j, c * P:(c + 1) * P], rhs(j),
                                         start=j == 0, stop=j == KC - 1)
                last.then_inc(used, 1)

        with pe.Fori(0, n_first // 4) as i:
            slots(i, 0, n_first, lambda i, c: out1[:, bass.ds(i * 8 + c, 1)], lambda j: k.cond[:, 0, j, 0:1])
        with pe.Fori(n_first // 4, n_all // 4) as i:
            slots(i, n_first, n_all, lambda i, c: out2[:, bass.ds(i * 8 + (c - 48), 1), :].rearrange("p a b -> p (a b)"),
                  lambda j: k.cond[:, 1, j, :])

    @block.vector
    def _(dve):
        dve.wait_ge(used, n_all)
        dve.tensor_tensor(k.mod1[:], out1, k.col("b_ada", 0, 48), ALU.add).then_inc(k.dve_chain.sem, 1)
        k.dve_chain.count += 1
        for l in range(4):
            bias = k.col(f"l{l}_b_ada_2", 0, 24).unsqueeze(2).broadcast_to([P, 24, 2])
            k.dve_chain(dve, dve.tensor_tensor(k.mod2[:, l], out2[:, 24 * l:24 * l + 24, :], bias, ALU.add))
        for n, name in enumerate(("norm1_w", "norm2_w")):
            dve.scalar_tensor_tensor(k.coef[:, n], k.mod1[:, 24 * n + 8:24 * n + 16], 1.0, k.col(name, 0, KC),
                                     ALU.add, ALU.mult)
        for l in range(4):
            for w in range(2):
                dve.scalar_tensor_tensor(k.coef2[:, l, :, w], k.mod2[:, l, 8:16, w], 1.0,
                                         k.col(f"l{l}_g_pre_2", 0, KC), ALU.add, ALU.mult)
                dve.tensor_tensor(k.gate2[:, l, :, w], k.mod2[:, l, 16:24, w], k.col(f"l{l}_g_post_2", 0, KC),
                                  ALU.mult)

    k.end_stage(block)


def rms_scale(k, block, x, n_chunks, parts, width, rstd, squares, load=None, banks=(0, 1)):
    sq = k.sem_named("square_ready")
    summed = k.sem_named("square_summed")

    @block.scalar
    def _(act):
        if load is not None:
            load(act)
        for c in range(n_chunks):
            if c >= 2:
                act.wait_ge(summed.sem, summed.at(c - 1))
            act.activation(squares[:, c % 2, 0:x.shape[2]], x[:, c, :], ACT.Square).then_inc(sq.sem, 1)
        act.wait_ge(summed.sem, summed.at(n_chunks))
        for n, (t0, t1) in enumerate(parts):
            k.act_chain(act, act.activation(rstd[:, t0:t1], k.psum[:, banks[n], 0:t1 - t0], ACT.Ln,
                                            bias=k.eps[:], scale=1.0 / width))
        for n, (t0, t1) in enumerate(parts):
            k.act_chain(act, act.activation(rstd[:, t0:t1], rstd[:, t0:t1], ACT.Exp, scale=-0.5))

    @block.tensor
    def _(pe):
        for c in range(n_chunks):
            pe.wait_ge(sq.sem, sq.at(c + 1))
            for n, (t0, t1) in enumerate(parts):
                last = pe.matmul(k.psum[:, banks[n], 0:t1 - t0], k.cst("ones"), squares[:, c % 2, t0:t1],
                                 start=c == 0, stop=c == n_chunks - 1)
            last.then_inc(summed.sem, 1)

    sq.stage_over(n_chunks)
    summed.stage_over(n_chunks)


def load_residual(k, x, sources):
    loaded = k.sem_named("residual_loaded")

    def load(act):
        for dst, src in sources:
            act.dma_start(dst, src).then_inc(loaded.sem, 16)
        act.wait_ge(loaded.sem, loaded.at(16 * len(sources)))
        loaded.stage_over(16 * len(sources))

    return load


def pre_norm(k, block, x, sources, a, parts, coef, shift, temp):
    w = x.shape[2]
    squares = k.at("squares", temp, [P, 2, w])
    rstd = k.at("rstd", temp + 8 * w, [P, w])
    h = k.at("h", temp + 12 * w, [P, 2, w])
    rms_scale(k, block, x, KC, parts, D, rstd, squares, load_residual(k, x, sources) if sources else None)
    ready = k.sem_named("rstd_ready")

    @block.scalar
    def _(act):
        act.nop().then_inc(ready.sem, 1)

    @block.vector
    def _(dve):
        dve.wait_ge(ready.sem, ready.at(1))
        for c in range(KC):
            for n, (t0, t1) in enumerate(parts):
                hh = h[:, c % 2, t0:t1]
                k.dve_chain(dve, dve.scalar_tensor_tensor(hh, x[:, c, t0:t1], coef(n, c), rstd[:, t0:t1],
                                                          ALU.mult, ALU.mult))
                k.dve_chain(dve, dve.tensor_scalar(a[0][:, c, t0:t1], hh, shift(n, c), None, ALU.add))
                dve.scalar_tensor_tensor(a[1][:, c, t0:t1], hh, shift(n, c), a[0][:, c, t0:t1].bitcast(F32),
                                         ALU.add, ALU.subtract)

    ready.stage_over(1)
    k.end_stage(block)



def ssd_branch(k, block, a, acc):
    B0 = k.ARENA + 49152
    z = k.at("z", B0, [P, 8, S])
    xbc = k.at("xbc", B0 + 16384, [P, 12, S])
    x_tok = k.at("x_tok", B0 + 40960, [P, 4, 1024])
    b_tok = k.at("b_tok", B0 + 57344, [P, 4, 256])
    h_prev = k.at("h_prev", B0 + 61440, [P, 3, 1024])
    small = B0 + 73728
    full = [(0, S)]

    dense(k, block, ["z"], feature_major(a, KC, full), loop=True,
          act_tile=lambda act, i, t, ps: act.activation(
              z[:, bass.ds(i * 4 + t, 1), :].rearrange("p a n -> p (a n)"), ps, ACT.Silu))

    pad = k.at("pad", small, [P, 4, S + 3])
    conv = k.at("conv", small + 16 * (S + 3) + 32, [P, 2, S])

    @block.vector
    def _(dve):
        for t in range(4):
            dve.memset(pad[:, t, 0:3], 0.0)
        dve.nop().then_inc(k.dve_chain.sem, 1)
        k.dve_chain.count += 1

    def conv_tile(dve, i, t, ps):
        src, dst = pad[:, t % 4], conv[:, t % 2]
        tap = lambda j: k.col("conv_w", 12 * j + t)
        if t >= 2:
            dve.wait_ge(k.tile_free.sem, k.tile_free.at(t - 1))
        k.dve_chain(dve, dve.tensor_scalar(dst, src[:, 3:3 + S], tap(3), k.col("conv_b", t), ALU.mult, ALU.add))
        for j in (2, 1):
            k.dve_chain(dve, dve.scalar_tensor_tensor(dst, src[:, j:j + S], tap(j), dst, ALU.mult, ALU.add))
        return dve.scalar_tensor_tensor(dst, src[:, 0:S], tap(0), dst, ALU.mult, ALU.add)

    dense(k, block, ["xbc"], feature_major(a, KC, full),
          act_tile=lambda act, i, t, ps: act.activation(pad[:, t % 4, 3:3 + S], ps, ACT.Copy),
          dve_tile=conv_tile,
          act_last=lambda act, i, t: act.activation(xbc[:, t, :], conv[:, t % 2], ACT.Silu))

    dt = k.at("dt", small, [P, 9, 64])
    raw, e, u, dts, da, acum, nacum, wend, dec = (dt[:, j] for j in range(9))
    c4 = lambda x: x.rearrange("p (c h) -> p c h", c=4)
    bias = lambda name: k.row(name).unsqueeze(1).broadcast_to([P, 4, 16])

    def dt_tiles(s, hi, lo):
        hi = hi.rearrange("p (k n) -> p k n", k=KC)
        lo = lo.rearrange("p (k n) -> p k n", k=KC)
        return [] if s else [
            (lambda bank: bank[:, 0:16],
             [((a[0][:, j, c * P:(c + 1) * P], a[1][:, j, c * P:(c + 1) * P]), (hi[:, j, 0:16], lo[:, j, 0:16]))
              for j in range(KC)]) for c in range(4)]

    def softplus_in(dve, i, t, ps):
        return dve.tensor_tensor(raw[:, 16 * t:16 * t + 16], ps[:, 0:16], k.row("dt_bias"), ALU.add)

    dense(k, block, ["dt", "_dt"], dt_tiles, dve_tile=softplus_in)

    ssd_to_act, ssd_to_dve, ssd_to_pe = (k.sem_named(f"ssd_to_{x}") for x in ("act", "dve", "pe"))

    @block.vector
    def _(dve):
        ch = k.dve_chain
        ch(dve, dve.tensor_scalar(e, raw, -1.0, None, ALU.mult))
        dve.tensor_tensor(e, raw, e, ALU.min).then_inc(ssd_to_act.sem, 1)
        dve.wait_ge(ssd_to_dve.sem, ssd_to_dve.at(1))
        ch(dve, dve.tensor_scalar(u, e, 1.0, None, ALU.add))
        dve.nop().then_inc(ssd_to_act.sem, 1)
        ch(dve, dve.scalar_tensor_tensor(dec, u, -1.0, e, ALU.add, ALU.subtract))
        ch(dve, dve.reciprocal(wend, u))
        ch(dve, dve.tensor_tensor(dec, dec, wend, ALU.mult))
        dve.wait_ge(ssd_to_dve.sem, ssd_to_dve.at(2))
        ch(dve, dve.tensor_tensor(dec, da, dec, ALU.subtract))
        ch(dve, dve.scalar_tensor_tensor(dts, raw, 0.0, dec, ALU.max, ALU.add))
        ch(dve, dve.scalar_tensor_tensor(c4(da), c4(dts), -1.0, bias("a_log"), ALU.mult, ALU.mult))
        dve.nop().then_inc(ssd_to_pe.sem, 1)
        dve.wait_ge(ssd_to_dve.sem, ssd_to_dve.at(3))
        ch(dve, dve.tensor_copy(acum, k.psum[:, 0, 0:64]))
        ch(dve, dve.tensor_scalar(nacum, acum, -1.0, None, ALU.mult))
        dve.tensor_tensor(wend, k.psum[:, 1, 0:64], acum, ALU.subtract).then_inc(ssd_to_act.sem, 1)

    @block.scalar
    def _(act):
        act.wait_ge(ssd_to_act.sem, ssd_to_act.at(1))
        k.act_chain(act, act.activation(e, e, ACT.Exp))
        act.activation(k.row("a_log"), k.row("a_log"), ACT.Exp).then_inc(ssd_to_dve.sem, 1)
        act.wait_ge(ssd_to_act.sem, ssd_to_act.at(2))
        act.activation(da, u, ACT.Ln).then_inc(ssd_to_dve.sem, 1)
        act.wait_ge(ssd_to_act.sem, ssd_to_act.at(3))
        act.activation(wend, wend, ACT.Exp)
        act.activation(dec, k.psum[:, 1, 0:64], ACT.Exp)

    @block.tensor
    def _(pe):
        pe.wait_ge(ssd_to_pe.sem, ssd_to_pe.at(1))
        pe.matmul(k.psum[:, 0, 0:64], k.cst("tri"), da, start=True, stop=True)
        pe.matmul(k.psum[:, 1, 0:64], k.cst("ones"), da, start=True, stop=True).then_inc(ssd_to_dve.sem, 1)

    ssd_to_act.stage_over(3)
    ssd_to_dve.stage_over(3)
    ssd_to_pe.stage_over(1)
    k.end_stage(block)

    turned, taken = k.sem_named("turned"), k.sem_named("turned_taken")
    groups = [(f0, c) for c in range(4) for f0 in (0, 4, 8)]

    @block.tensor
    def _(pe):
        for n, (f0, c) in enumerate(groups):
            if n >= 4:
                pe.wait_ge(taken.sem, taken.at(n - 3))
            for f in range(f0, min(f0 + 4, 10)):
                last = pe.transpose(k.psum[:, n % 4, (f - f0) * P:(f - f0 + 1) * P], xbc[:, f, c * P:(c + 1) * P],
                                    k.cst("ident"))
            last.then_inc(turned.sem, 1)

    @block.vector
    def _(dve):
        for n, (f0, c) in enumerate(groups):
            dve.wait_ge(turned.sem, turned.at(n + 1))
            if f0 == 8:
                dve.tensor_copy(b_tok[:, c, :], k.psum[:, n % 4, 0:256]).then_inc(taken.sem, 1)
            else:
                heads = c4(dts)[:, c, 2 * f0:2 * f0 + 8].unsqueeze(2).broadcast_to([P, 8, 64])
                dve.tensor_tensor(x_tok[:, c, f0 * P:f0 * P + 512].rearrange("p (h e) -> p h e", h=8),
                                  k.psum[:, n % 4, :].rearrange("p (h e) -> p h e", h=8), heads,
                                  ALU.mult).then_inc(taken.sem, 1)

    turned.stage_over(len(groups))
    taken.stage_over(len(groups))
    k.end_stage(block)

    xd = k.at("xd", small + 4096, [P, 2, 1024])
    ready, summed = k.sem_named("xd_ready"), k.sem_named("state_summed")

    @block.vector
    def _(dve):
        def scaled(c):
            w = c4(wend)[:, c, :].unsqueeze(2).broadcast_to([P, 16, 64])
            if c >= 2:
                dve.wait_ge(summed.sem, summed.at(c - 1))
            dve.tensor_tensor(xd[:, c % 2].rearrange("p (h e) -> p h e", h=16),
                              x_tok[:, c, :].rearrange("p (h e) -> p h e", h=16), w, ALU.mult).then_inc(ready.sem, 1)

        def state(c):
            dve.wait_ge(summed.sem, summed.at(c + 1))
            ps = k.psum[:, 2 * c:2 * c + 2, :].rearrange("p g n -> p (g n)")
            if c == 0:
                k.dve_chain(dve, dve.tensor_copy(h_prev[:, 0, :], ps))
            else:
                d = c4(dec)[:, c, :].unsqueeze(2).broadcast_to([P, 16, 64])
                k.dve_chain(dve, dve.tensor_tensor(h_prev[:, c, :].rearrange("p (h e) -> p h e", h=16),
                                                   h_prev[:, c - 1, :].rearrange("p (h e) -> p h e", h=16), d,
                                                   ALU.mult))
                k.dve_chain(dve, dve.tensor_tensor(h_prev[:, c, :], ps, h_prev[:, c, :], ALU.add))

        scaled(0)
        scaled(1)
        state(0)
        scaled(2)
        state(1)
        state(2)

    @block.tensor
    def _(pe):
        for c in range(3):
            pe.wait_ge(ready.sem, ready.at(c + 1))
            for g in range(2):
                last = pe.matmul(k.psum[:, 2 * c + g, :], b_tok[:, c, g * P:(g + 1) * P],
                                 xd[:, c % 2, g * 512:(g + 1) * 512], start=True, stop=True)
            last.then_inc(summed.sem, 1)
        for g in range(2):
            for c in range(4):
                last = pe.matmul(k.psum[:, 6 + g, c * P:(c + 1) * P], xbc[:, 8 + g, c * P:(c + 1) * P],
                                 xbc[:, 10 + g, c * P:(c + 1) * P], start=True, stop=True)

    ready.stage_over(3)
    summed.stage_over(3)
    k.end_stage(block)

    cb = k.at("cb", B0 + 57344, [P, 2, 512])
    o = small + 4096
    tri_a = k.at("tri_a", o, [P, 2, 512])
    seg = k.at("seg", o + 4096, [P, 2, 512])
    ea = k.at("ea", o + 8192, [P, 2, 512])
    cs = lambda x: x.rearrange("p (c l) -> p c l", c=4)
    rows_in, rows_out, seg_ready, dec_ready, m_ready, y_used = (
        k.sem_named(n) for n in ("ssd_rows_in", "ssd_rows_out", "ssd_seg_ready", "ssd_decay_ready",
                                 "ssd_m_ready", "ssd_y_used"))

    heads_out = k.sem_named("ssd_heads_out")

    @block.vector
    def _(dve):
        for g in range(2):
            k.dve_chain(dve, dve.tensor_copy(cb[:, g, :], k.psum[:, 6 + g, :]))
        tri = k.cst("tri").unsqueeze(1).broadcast_to([P, 4, P])
        mask = k.cst("mask_le").unsqueeze(1).broadcast_to([P, 4, P])

        def rows(h):
            if h >= 2:
                dve.wait_ge(rows_out.sem, rows_out.at(h - 1))
            d = c4(da)[:, :, h:h + 1].broadcast_to([P, 4, P])
            dve.tensor_tensor(cs(tri_a[:, h % 2]), tri, d, ALU.mult).then_inc(rows_in.sem, 1)

        def segment(h):
            dve.wait_ge(rows_out.sem, rows_out.at(h + 1))
            nac = c4(nacum)[:, :, h:h + 1].broadcast_to([P, 4, P])
            k.dve_chain(dve, dve.tensor_tensor(cs(seg[:, h % 2]), cs(k.psum[:, h % 2, :]), mask, ALU.add))
            dve.tensor_tensor(cs(seg[:, h % 2]), cs(seg[:, h % 2]), nac, ALU.add).then_inc(seg_ready.sem, 1)

        def combine(h):
            g = h // 8
            dve.wait_ge(dec_ready.sem, dec_ready.at(h + 1))
            dve.tensor_tensor(seg[:, h % 2], seg[:, h % 2], cb[:, g, :], ALU.mult)
            dve.tensor_tensor(ea[:, h % 2], ea[:, h % 2], xbc[:, 10 + g, :], ALU.mult).then_inc(m_ready.sem, 1)

        def finish(f):
            dve.wait_ge(heads_out.sem, heads_out.at(2 * f + 2))
            ps = k.psum[:, 2 + f % 2, :]
            k.dve_chain(dve, dve.scalar_tensor_tensor(xbc[:, f, :], xbc[:, f, :], k.col("d_skip", f), ps,
                                                      ALU.mult, ALU.add))
            dve.tensor_tensor(z[:, f, :], z[:, f, :], xbc[:, f, :], ALU.mult).then_inc(y_used.sem, 1)

        rows(0)
        rows(1)
        segment(0)
        for h in range(SSD_HEADS):
            if h + 2 < SSD_HEADS:
                rows(h + 2)
            if h + 1 < SSD_HEADS:
                if h >= 1:
                    dve.wait_ge(heads_out.sem, heads_out.at(h))
                segment(h + 1)
            combine(h)
            if h % 2 == 1 and h >= 3:
                finish(h // 2 - 1)
        finish(7)

    @block.scalar
    def _(act):
        for h in range(SSD_HEADS):
            act.wait_ge(seg_ready.sem, seg_ready.at(h + 1))
            act.activation(seg[:, h % 2], seg[:, h % 2], ACT.Exp)
            act.activation(ea[:, h % 2], k.psum[:, h % 2, :], ACT.Exp).then_inc(dec_ready.sem, 1)

    @block.tensor
    def _(pe):
        def rows(h):
            if h >= 2:
                pe.wait_ge(dec_ready.sem, dec_ready.at(h - 1))
            pe.wait_ge(rows_in.sem, rows_in.at(h + 1))
            pe.matmul(k.psum[:, h % 2, :], k.cst("ones"), tri_a[:, h % 2], start=True, stop=True) \
                .then_inc(rows_out.sem, 1)

        rows(0)
        rows(1)
        for h in range(SSD_HEADS):
            f, off = h // 2, 64 * (h % 2)
            pe.wait_ge(m_ready.sem, m_ready.at(h + 1))
            if f >= 2 and off == 0:
                pe.wait_ge(y_used.sem, y_used.at(f - 1))
            for c in range(4):
                out = k.psum[off:off + 64, 2 + f % 2, c * P:(c + 1) * P]
                last = pe.matmul(out, x_tok[:, c, h * 64:(h + 1) * 64], seg[:, h % 2, c * P:(c + 1) * P],
                                 start=True, stop=c == 0)
                if c:
                    last = pe.matmul(out, h_prev[:, c - 1, h * 64:(h + 1) * 64], ea[:, h % 2, c * P:(c + 1) * P],
                                     start=False, stop=True)
            last.then_inc(heads_out.sem, 1)
            if h + 2 < SSD_HEADS:
                rows(h + 2)

    for s_, n in ((rows_in, 16), (rows_out, 16), (seg_ready, 16), (dec_ready, 16), (m_ready, 16),
                  (y_used, 8), (heads_out, 16)):
        s_.stage_over(n)
    k.end_stage(block)


def gated(k, block, a, b, kb, gate, proj, acc, temp, first):
    sig = k.at("sig", temp, [P, 8, S])
    n_g = 2 if kb == KC else 4

    def tiles_of(x, kc, n):
        f = feature_major(x, kc, [(0, S)], chunks=range(min(2, n) if kc == KC else n))
        return f

    for c in range(len(gate)):
        dense(k, block, [gate[c]], tiles_of(a, KC, 2),
              act_tile=lambda act, i, t, ps: act.activation(sig[:, t, :], ps, ACT.Sigmoid))

        def project(dve, i, t, ps, c=c):
            f = n_g * c + t
            if first:
                return dve.tensor_tensor(acc[:, f, :], ps, sig[:, t, :], ALU.mult)
            k.dve_chain(dve, dve.tensor_tensor(sig[:, t, :], ps, sig[:, t, :], ALU.mult))
            return dve.tensor_tensor(acc[:, f, :], acc[:, f, :], sig[:, t, :], ALU.add)

        dense(k, block, [proj[c]], tiles_of(b, kb, n_g), dve_tile=project)


def ssd_out(k, block, a, acc):
    B0 = k.ARENA + 49152
    z = k.at("z", B0, [P, 8, S])
    rstd = k.at("rstd", B0 + 73728, [P, 2, S])
    squares = k.at("squares", B0 + 73728 + 4096, [P, 2, S])
    y = (k.at("y_hi", B0 + 16384, [P, 8, S], F32R), k.at("y_lo", B0 + 32768, [P, 8, S], F32R))
    for g in range(2):
        rms_scale(k, block, z[:, 4 * g:4 * g + 4, :], 4, [(0, S)], 512, rstd[:, g], squares, banks=(g,))
    k.end_stage(block)

    @block.vector
    def _(dve):
        for f in range(8):
            k.dve_chain(dve, dve.scalar_tensor_tensor(z[:, f, :], z[:, f, :], k.col("ssd_norm_w", f),
                                                      rstd[:, f // 4], ALU.mult, ALU.mult))
            split(k, dve, y[0][:, f, :], y[1][:, f, :], z[:, f, :])

    k.end_stage(block)
    gated(k, block, a, y, KC, [f"g_ssd{c}" for c in range(4)], [f"ssd_out{c}" for c in range(4)], acc, B0, True)


def attention(k, block, units, temp, width):
    scores_done, masked, exp_done, scaled, turned, copied, out_done, out_used = (
        k.sem_named(f"att_{x}") for x in ("scores_done", "max_ready", "exp_done", "scaled", "turned", "copied",
                                          "out_done", "out_used"))
    n = len(units)
    wide = 3 if width > 1024 else 2
    prob = k.at("prob", temp, [P, 2, width])
    prob_t = k.at("prob_t", temp + 8 * width, [P, 2, width])
    stat = k.at("stat", temp + 16 * width, [P, 2, 16])
    t_bank = 2 * wide if wide == 2 else 3
    t_banks = 2 if wide == 2 else 3
    o_bank = t_bank + t_banks
    s_bufs = 2 if wide == 2 else 1

    def score(u):
        b = wide * (u % s_bufs)
        return k.psum[:, b:b + wide, :].rearrange("p b n -> p (b n)")

    turned_bank = k.psum[:, t_bank:t_bank + t_banks, :].rearrange("p b n -> p (b n)")

    def out_bank(u):
        return k.psum[:, o_bank + u % 2, :] if wide == 2 else k.psum[:, o_bank + u % 2, :]

    @block.tensor
    def _(pe):
        def scores(u):
            if u >= s_bufs:
                pe.wait_ge(exp_done.sem, exp_done.at(u - s_bufs + 1))
            if "ready" in units[u]:
                pe.wait_ge(*units[u]["ready"])
            ps = score(u)
            for col, cols, pairs in units[u]["qk"]:
                for j, (lhs, rhs) in enumerate(pairs):
                    last = pe.matmul(ps[:, col:col + cols], lhs, rhs, start=j == 0, stop=j == len(pairs) - 1)
            last.then_inc(scores_done.sem, 1)

        def turn(u):
            pe.wait_ge(scaled.sem, scaled.at(u + 1))
            if u:
                pe.wait_ge(copied.sem, copied.at(u))
            for j in range(len(units[u]["pv"])):
                last = pe.transpose(turned_bank[:, j * P:(j + 1) * P], prob[:, u % 2, j * P:(j + 1) * P],
                                    k.cst("ident"))
            last.then_inc(turned.sem, 1)

        def values(u):
            pe.wait_ge(copied.sem, copied.at(u + 1))
            if u >= 2:
                pe.wait_ge(out_used.sem, out_used.at(u - 1))
            pv, r = units[u]["pv"], units[u]["rows"]
            for j, v in enumerate(pv):
                last = pe.matmul(out_bank(u)[r[0]:r[1], 0:P], v, prob_t[:, u % 2, j * P:(j + 1) * P],
                                 start=j == 0, stop=j == len(pv) - 1)
            last.then_inc(out_done.sem, 1)

        for u in range(n + 2):
            if u < n:
                scores(u)
            if 1 <= u <= n:
                turn(u - 1)
            if u >= 2:
                values(u - 2)

    @block.vector
    def _(dve):
        def maxima(u):
            un, ps, st = units[u], score(u), stat[:, u % 2]
            dve.wait_ge(scores_done.sem, scores_done.at(u + 1))
            for col, cols, mask in un["masks"]:
                last = dve.tensor_tensor(ps[:, col:col + cols], ps[:, col:col + cols], mask, ALU.add)
            if un["masks"]:
                k.dve_chain(dve, last)
            for j, (r0, r1) in enumerate(un["ranges"]):
                last = dve.tensor_reduce(st[:, j:j + 1], ps[:, r0:r1], AX.X, ALU.max)
            k.dve_chain(dve, last)
            m = st[:, 0:1]
            if len(un["ranges"]) > 1:
                k.dve_chain(dve, dve.tensor_reduce(st[:, 4:5], st[:, 0:len(un["ranges"])], AX.X, ALU.max))
                m = st[:, 4:5]
            if un["sink"] is None:
                dve.tensor_scalar(st[:, 5:6], m, -un["scale"], None, ALU.mult).then_inc(masked.sem, 1)
            else:
                k.dve_chain(dve, dve.tensor_scalar(st[:, 6:7], m, un["scale"], un["sink"], ALU.mult, ALU.max))
                dve.tensor_scalar(st[:, 5:6], st[:, 6:7], -1.0, None, ALU.mult)
                dve.tensor_tensor(st[:, 7:8], un["sink"], st[:, 6:7], ALU.subtract).then_inc(masked.sem, 1)

        def scale(u):
            un, st = units[u], stat[:, u % 2]
            dve.wait_ge(exp_done.sem, exp_done.at(u + 1))
            total = 8 + len(un["ranges"]) + (un["sink"] is not None)
            k.dve_chain(dve, dve.tensor_reduce(st[:, 14:15], st[:, 8:total], AX.X, ALU.add))
            k.dve_chain(dve, dve.reciprocal(st[:, 15:16], st[:, 14:15]))
            w = sum(b - a for a, b in un["ranges"])
            dve.tensor_scalar(prob[:, u % 2, 0:w], prob[:, u % 2, 0:w], st[:, 15:16], None, ALU.mult) \
                .then_inc(scaled.sem, 1)

        for u in range(n + 1):
            if u < n:
                if u >= 2:
                    dve.wait_ge(turned.sem, turned.at(u - 1))
                maxima(u)
            if u >= 1:
                scale(u - 1)

    @block.scalar
    def _(act):
        def exps(u):
            un, ps, st = units[u], score(u), stat[:, u % 2]
            act.wait_ge(masked.sem, masked.at(u + 1))
            at = 0
            if un["sink"] is not None:
                act.activation(st[:, 8 + len(un["ranges"]):9 + len(un["ranges"])], st[:, 7:8], ACT.Exp)
            for j, (r0, r1) in enumerate(un["ranges"]):
                last = act.activation(prob[:, u % 2, at:at + r1 - r0], ps[:, r0:r1], ACT.Exp, bias=st[:, 5:6],
                                      scale=un["scale"], accum_out=st[:, 8 + j:9 + j])
                at += r1 - r0
            last.then_inc(exp_done.sem, 1)

        def copy(u):
            act.wait_ge(turned.sem, turned.at(u + 1))
            if u >= 2:
                act.wait_ge(out_done.sem, out_done.at(u - 1))
            w = P * len(units[u]["pv"])
            act.activation(prob_t[:, u % 2, 0:w], turned_bank[:, 0:w], ACT.Copy).then_inc(copied.sem, 1)

        def take(u):
            act.wait_ge(out_done.sem, out_done.at(u + 1))
            r = units[u]["rows"]
            act.activation(units[u]["out"], out_bank(u)[r[0]:r[1], 0:P], ACT.Copy).then_inc(out_used.sem, 1)

        for u in range(n + 2):
            if u < n:
                exps(u)
            if 1 <= u <= n:
                copy(u - 1)
            if u >= 2:
                take(u - 2)

    for s_ in (scores_done, masked, exp_done, scaled, turned, copied, out_done, out_used):
        s_.stage_over(n)
    k.end_stage(block)


def dilated_attention(k, block, a, acc):
    B0 = k.ARENA + 49152
    qkv = k.at("qkv", B0, [P, 9, S])
    v = qkv[:, 6:9, :].rearrange("p a n -> p (a n)").rearrange("p (b n) -> p b n", b=4)
    o = k.at("o", B0 + 18432, [P, 4, S])
    o_s = (k.at("o_hi", B0 + 26624, [P, 4, S], F32R), k.at("o_lo", B0 + 34816, [P, 4, S], F32R))
    tables = k.at("tables", B0 + 43008, [P, 4, 512])
    bias = k.at("bias", B0 + 51200, [P, 3, 512])
    temp = B0 + 57344
    squares = k.at("squares", temp, [P, 2, S])
    rstd = k.at("rstd", temp + 4096, [P, 2, S])
    slopes = alibi_slopes(12)
    scale = float(P) ** -0.5
    loaded = k.sem_named("tables_loaded")
    normed, sq, summed = (k.sem_named(x) for x in ("qk_normed", "square_ready", "square_summed"))

    @block.scalar
    def _(act):
        n0 = CONST_AT["negd"]
        act.dma_start(tables[:], k.io["consts"][:, n0:n0 + 2048].rearrange("p (a n) -> p a n", a=4)) \
            .then_inc(loaded.sem, 16)

    for j in range(4):
        def tiles(s, hi, lo):
            if s < 3:
                return feature_major(a, KC, [(0, S)])(s, hi, lo)
            hi = hi.rearrange("p (k n) -> p k n", k=KC)
            lo = lo.rearrange("p (k n) -> p k n", k=KC)
            n0, n1 = (0, 256) if s == 3 else (0, 128)
            return [(lambda bank, n=n1: bank[:, 0:n],
                     [((a[0][:, c, b * P:(b + 1) * P], a[1][:, c, b * P:(b + 1) * P]),
                       (hi[:, c, 0:n1], lo[:, c, 0:n1])) for c in range(KC)]) for b in range(4)]

        def take(act, i, t, ps):
            if t < 6:
                return act.activation(qkv[:, t, :], ps, ACT.Copy)
            b, s = (t - 6) % 4, (t - 6) // 4
            return act.activation(v[:, b, 256 * s:256 * s + (128 if s else 256)], ps[:, 0:128 if s else 256],
                                  ACT.Copy)

        dense(k, block, [f"qkv{j}"], tiles, act_tile=take)

        def root(act, t):
            act.wait_ge(summed.sem, summed.at(t + 1))
            if t >= 2:
                act.wait_ge(k.finished.sem, k.finished.at(t - 1))
            k.act_chain(act, act.activation(rstd[:, t % 2], k.psum[:, t % 2, :], ACT.Ln, bias=k.eps[:],
                                            scale=1.0 / P))
            act.activation(rstd[:, t % 2], rstd[:, t % 2], ACT.Exp, scale=-0.5).then_inc(normed.sem, 1)

        @block.scalar
        def _(act):
            for t in range(6):
                if t >= 2:
                    act.wait_ge(summed.sem, summed.at(t - 1))
                act.activation(squares[:, t % 2], qkv[:, t, :], ACT.Square).then_inc(sq.sem, 1)
                if t >= 1:
                    root(act, t - 1)
            root(act, 5)

        @block.tensor
        def _(pe):
            for t in range(6):
                pe.wait_ge(sq.sem, sq.at(t + 1))
                if t >= 2:
                    pe.wait_ge(normed.sem, normed.at(t - 1))
                pe.matmul(k.psum[:, t % 2, :], k.cst("ones"), squares[:, t % 2], start=True, stop=True) \
                    .then_inc(summed.sem, 1)

        @block.vector
        def _(dve):
            if j == 0:
                dve.wait_ge(loaded.sem, loaded.at(16))
            for g in range(3):
                dve.scalar_tensor_tensor(bias[:, g], tables[:, 0], slopes[4 * g + j] / scale, tables[:, 1 + g],
                                         ALU.mult, ALU.add)
            for t in range(6):
                dve.wait_ge(normed.sem, normed.at(t + 1))
                dve.scalar_tensor_tensor(qkv[:, t, :], qkv[:, t, :], k.col("q_norm_w" if t < 3 else "k_norm_w"),
                                         rstd[:, t % 2], ALU.mult, ALU.mult).then_inc(k.finished.sem, 1)

        sq.stage_over(6)
        summed.stage_over(6)
        normed.stage_over(6)
        k.finished.stage_over(6)
        if j == 0:
            loaded.stage_over(16)
        k.end_stage(block)

        units = []
        for b in range(4):
            q = lambda g: qkv[:, g, b * P:(b + 1) * P]
            lo0 = max(0, b - 1)
            k0s = [lo0, 0, 0]
            qk, masks, ranges, pv = [], [], [], []
            for g in range(3):
                n = (b + 1 - k0s[g]) * P
                qk.append((512 * g, n, [(q(g), qkv[:, 3 + g, k0s[g] * P:(b + 1) * P])]))
                masks.append((512 * g, n, bias[:, g, 512 - n:512]))
                ranges.append((512 * g, 512 * g + n))
                pv += [v[:, kb, g * P:(g + 1) * P] for kb in range(k0s[g], b + 1)]
            units.append(dict(qk=qk, masks=masks, ranges=ranges, scale=scale, sink=None, pv=pv, rows=(0, P),
                              out=o[:, j, b * P:(b + 1) * P]))
        attention(k, block, units, temp, 1280)

    @block.vector
    def _(dve):
        for j in range(4):
            split(k, dve, o_s[0][:, j, :], o_s[1][:, j, :], o[:, j, :])

    k.end_stage(block)
    gated_wide(k, block, a, o_s, acc, B0 + 43008)


def gated_wide(k, block, a, b, acc, temp):
    y = k.at("y_part", temp, [P, 4, S])
    sig = k.at("sig", temp + 8192, [P, 4, S])
    for c in range(2):
        dense(k, block, [f"attn_out{c}"], feature_major(b, 4, [(0, S)], chunks=range(4)),
              act_tile=lambda act, i, t, ps: act.activation(y[:, t, :], ps, ACT.Copy))

        def gate(dve, i, t, ps, c=c):
            s = sig[:, t, :]
            k.dve_chain(dve, dve.tensor_tensor(s, s, y[:, t, :], ALU.mult))
            return dve.tensor_tensor(acc[:, 4 * c + t, :], acc[:, 4 * c + t, :], s, ALU.add)

        dense(k, block, [f"g_attn{c}"], feature_major(a, KC, [(0, S)]),
              act_tile=lambda act, i, t, ps: act.activation(sig[:, t, :], ps, ACT.Sigmoid), dve_tile=gate)


def pool_branch(k, block, a, acc):
    B0 = k.ARENA + 49152
    PAD = 16
    u = k.at("u", B0, [P, 8, S + PAD])
    win = k.at("win", B0 + 17408, [P, 2, 2, S + PAD])
    m = (k.at("m_hi", B0 + 26112, [P, 8, S], F32R), k.at("m_lo", B0 + 42496, [P, 8, S], F32R))
    inv = k.at("inv", B0 + 58880, [P, 64])
    x = (k.at("x_hi", B0 + 59392, [P, 8, S], F32R), k.at("x_lo", B0, [P, 8, S], F32R))
    loaded = k.sem_named("tables_loaded")

    @block.vector
    def _(dve):
        k.dve_chain(dve, dve.memset(u[:, :, 0:PAD], 0.0))
        k.dve_chain(dve, dve.memset(win[:, :, :, 0:PAD], 0.0))

    @block.scalar
    def _(act):
        n0 = CONST_AT["pool_inv"]
        act.dma_start(inv[:], k.io["consts"][:, n0:n0 + 64]).then_inc(loaded.sem, 16)

    dense(k, block, ["u"], feature_major(a, KC, [(0, S)]), loop=True,
          act_tile=lambda act, i, t, ps: act.activation(
              u[:, bass.ds(i * 4 + t, 1), PAD:].rearrange("p a n -> p (a n)"), ps, ACT.Copy))

    @block.vector
    def _(dve):
        ch = k.dve_chain
        dve.wait_ge(loaded.sem, loaded.at(16))
        for f in range(8):
            g = f // 2
            w = 2 << g
            src = u[:, f]
            for d in range(g + 1):
                step = 1 << d
                dst = win[:, f % 2, d % 2]
                ch(dve, dve.tensor_tensor(dst[:, PAD:], src[:, PAD:], src[:, PAD - step:PAD + S - step], ALU.add))
                src = dst
            cur = u[:, f, PAD:]
            mean = win[:, f % 2, (g + 1) % 2]
            ch(dve, dve.tensor_tensor(mean[:, PAD:PAD + 16], src[:, PAD:PAD + 16], inv[:, 16 * g:16 * g + 16],
                                      ALU.mult))
            ch(dve, dve.tensor_scalar(mean[:, PAD + 16:], src[:, PAD + 16:], 1.0 / w, None, ALU.mult))
            ch(dve, dve.tensor_tensor(cur, mean[:, PAD:], cur, ALU.subtract))
            split(k, dve, m[0][:, f, :], m[1][:, f, :], cur)

    loaded.stage_over(16)
    k.end_stage(block)

    def mix_tiles(s, hi, lo):
        if s:
            return []
        hi = hi.rearrange("p (k n) -> p k n", k=KC)
        lo = lo.rearrange("p (k n) -> p k n", k=KC)
        return [(lambda bank: bank,
                 [((hi[:, 2 * g + j, c * P:(c + 1) * P], lo[:, 2 * g + j, c * P:(c + 1) * P]),
                   (m[0][:, 2 * g + j, :], m[1][:, 2 * g + j, :])) for j in range(2)])
                for g in range(4) for c in range(2)]

    mixed = k.at("mixed", B0 + 17408, [P, 4, S])

    def scaled(dve, i, t, ps):
        y = mixed[:, t % 4, :]
        k.dve_chain(dve, dve.tensor_scalar(y, ps, k.col("pool_scale", t), None, ALU.mult))
        return split(k, dve, x[0][:, t, :], x[1][:, t, :], y)

    dense(k, block, ["mix", "_mix"], mix_tiles, dve_tile=scaled)
    gated(k, block, a, x, KC, [f"g_pool{c}" for c in range(4)], [f"pool_out{c}" for c in range(4)], acc,
          B0 + 26112, False)


def first_block(k, block, stop=None):
    A0 = k.ARENA
    B0 = A0 + 49152
    full = [(0, S)]
    a = (k.at("a_hi", A0, [P, KC, S], F32R), k.at("a_lo", A0 + 16384, [P, KC, S], F32R))
    acc = k.at("acc", A0 + 32768, [P, KC, S])
    x_in = k.io["xT"].rearrange("(c p) t -> p c t", p=P)
    x1 = k.at("x1", B0, [P, KC, S])
    pre_norm(k, block, x1, [(x1[:], x_in)], a, full, lambda n, c: k.coef[:, 0, c:c + 1],
             lambda n, c: k.mod1[:, c:c + 1], B0 + 16384)
    k.dump("h", a[0][:].bitcast(F32))
    ssd_branch(k, block, a, acc)
    k.dump("z", k.at("z", B0, [P, 8, S])[:])
    ssd_out(k, block, a, acc)
    k.dump("acc1", acc[:])
    dilated_attention(k, block, a, acc)
    k.dump("acc2", acc[:])
    pool_branch(k, block, a, acc)
    k.dump("acc3", acc[:])

    m = (k.at("m_hi", B0, [P, KC, S], F32R), k.at("m_lo", B0 + 16384, [P, KC, S], F32R))
    x = k.at("x", A0 + 32768, [P, KC, S])

    @block.vector
    def _(dve):
        for c in range(KC):
            split(k, dve, m[0][:, c, :], m[1][:, c, :], acc[:, c, :])

    k.end_stage(block)
    loaded = k.sem_named("residual_loaded")

    @block.scalar
    def _(act):
        act.dma_start(x[:], x_in).then_inc(loaded.sem, 16)

    @block.vector
    def _(dve):
        dve.wait_ge(loaded.sem, loaded.at(16))

    def add(dve, i, t, ps):
        return dve.scalar_tensor_tensor(x[:, t, :], ps, k.mod1[:, 16 + t:17 + t], x[:, t, :], ALU.mult, ALU.add)

    dense(k, block, ["out"], feature_major(m, KC, full), dve_tile=add)
    loaded.stage_over(16)
    k.dump("x1", x[:])

    pre_norm(k, block, x, None, a, full, lambda n, c: k.coef[:, 1, c:c + 1],
             lambda n, c: k.mod1[:, 24 + c:25 + c], B0)

    hid = (k.at("hid_hi", B0, [P, KC, S], F32R), k.at("hid_lo", B0 + 16384, [P, KC, S], F32R))
    f_acc = k.at("f_acc", B0 + 32768, [P, KC, S])
    r = k.at("r", B0 + 49152, [P, 4, S])
    for b in range(4):
        def square(dve, i, t, ps):
            y = r[:, t % 4, :]
            k.dve_chain(dve, dve.tensor_tensor(y, y, y, ALU.mult))
            return split(k, dve, hid[0][:, t, :], hid[1][:, t, :], y)

        dense(k, block, [f"ff1_{b}"], feature_major(a, KC, full),
              act_tile=lambda act, i, t, ps: act.activation(r[:, t % 4, :], ps, ACT.Relu), dve_tile=square)

        def total(dve, i, t, ps, b=b):
            f = f_acc[:, t, :]
            if b == 0:
                return dve.tensor_copy(f, ps)
            if b < 3:
                return dve.tensor_tensor(f, ps, f, ALU.add)
            k.dve_chain(dve, dve.tensor_tensor(f, ps, f, ALU.add))
            return dve.scalar_tensor_tensor(x[:, t, :], f, k.mod1[:, 40 + t:41 + t], x[:, t, :], ALU.mult,
                                            ALU.add)

        dense(k, block, [f"ff2_{b}"], feature_major(hid, KC, full), dve_tile=total)
    store(k, block, [(k.io["xres"][:, 0:S].rearrange("(c p) t -> p c t", p=P), x[:])])
    k.dump("x2", x[:])


def store(k, block, pairs):
    stored = k.sem_named("stored")

    @block.scalar
    def _(act):
        for dst, src in pairs:
            act.dma_start(dst, src).then_inc(stored.sem, 16)
        act.wait_ge(stored.sem, stored.at(16 * len(pairs)))

    stored.stage_over(16 * len(pairs))
    k.end_stage(block)



LAT, CTX = (0, S), (S, T2)


def rotate(k, block, chunks, temp):
    t_sin = k.at("t_sin", temp, [P, 2, S])
    swapped, done = k.sem_named("swapped"), k.sem_named("swap_used")

    @block.tensor
    def _(pe):
        for n, c in enumerate(chunks):
            if n >= 2:
                pe.wait_ge(done.sem, done.at(n - 1))
            pe.matmul(k.psum[:, n % 2, :], k.cst("swap"), c, start=True, stop=True).then_inc(swapped.sem, 1)

    @block.vector
    def _(dve):
        for n, c in enumerate(chunks):
            dve.wait_ge(swapped.sem, swapped.at(n + 1))
            dve.tensor_tensor(c, c, k.cst("cos"), ALU.mult)
            k.dve_chain(dve, dve.tensor_tensor(t_sin[:, n % 2], k.psum[:, n % 2, :], k.cst("sin"), ALU.mult))
            dve.tensor_tensor(c, c, t_sin[:, n % 2], ALU.add).then_inc(done.sem, 1)

    swapped.stage_over(len(chunks))
    done.stage_over(len(chunks))
    k.end_stage(block)


def token_major(a, blocks, slot_cols, width):
    def tiles(s, hi, lo):
        hi = hi.rearrange("p (k n) -> p k n", k=KC)
        lo = lo.rearrange("p (k n) -> p k n", k=KC)
        return [(lambda bank: bank[:, 0:slot_cols],
                 [((a[0][:, j, b * P:(b + 1) * P], a[1][:, j, b * P:(b + 1) * P]),
                   (hi[:, j, 0:slot_cols], lo[:, j, 0:slot_cols])) for j in range(KC)]) for b in blocks]
    return tiles


def layer_norm_in(k, block, l, a, x_at, both=True):
    xres = k.io["xres"].rearrange("(c p) t -> p c t", p=P)
    x = k.at("x_in", x_at, [P, KC, T2])
    ctx = k.io["ctxT"].rearrange("(c p) t -> p c t", p=P) if l == 0 else xres[:, :, S:T2]
    pre_norm(k, block, x, [(x[:, :, 0:S], xres[:, :, 0:S]), (x[:, :, S:T2], ctx)], a, [LAT, CTX],
             lambda n, c: k.coef2[:, l, c, n:n + 1], lambda n, c: k.mod2[:, l, c, n:n + 1], x_at + 24576)


def layer_out(k, block, l, section, b, parts, y_at, x_at, temp, out):
    w = parts[-1][1]
    y = k.at("y", y_at, [P, KC, w])
    x = k.at("x_out", x_at, [P, KC, w])
    squares = k.at("squares", temp, [P, 2, w])
    rstd = k.at("rstd", temp + 8 * w, [P, w])
    n_parts = len(parts)

    dense(k, block, [section], feature_major(b, KC, parts), loop=True,
          act_tile=lambda act, i, t, ps: act.activation(
              y[:, bass.ds(i * 4 + t // n_parts, 1), parts[t % n_parts][0]:parts[t % n_parts][1]]
              .rearrange("p a n -> p (a n)"), ps[:, 0:parts[t % n_parts][1] - parts[t % n_parts][0]], ACT.Copy))
    xres = k.io["xres"].rearrange("(c p) t -> p c t", p=P)
    ctx = k.io["ctxT"].rearrange("(c p) t -> p c t", p=P) if l == 0 else xres[:, :, S:T2]
    sources = [(x[:, :, 0:S], xres[:, :, 0:S])] + ([(x[:, :, S:T2], ctx)] if n_parts == 2 else [])
    rms_scale(k, block, y, KC, parts, D, rstd, squares, load_residual(k, x, sources))
    ready = k.sem_named("rstd_ready")

    @block.scalar
    def _(act):
        act.nop().then_inc(ready.sem, 1)

    @block.vector
    def _(dve):
        dve.wait_ge(ready.sem, ready.at(1))
        for c in range(KC):
            for n, (t0, t1) in enumerate(parts):
                k.dve_chain(dve, dve.scalar_tensor_tensor(y[:, c, t0:t1], y[:, c, t0:t1], k.gate2[:, l, c, n:n + 1],
                                                          rstd[:, t0:t1], ALU.mult, ALU.mult))
            dve.tensor_tensor(x[:, c, :], x[:, c, :], y[:, c, :], ALU.add)

    ready.stage_over(1)
    k.end_stage(block)
    store(k, block, [(out, x[:])])


def times_and_split(k, block, o, z, b, w):
    @block.vector
    def _(dve):
        for c in range(KC):
            k.dve_chain(dve, dve.tensor_tensor(o[:, c, 0:w], o[:, c, 0:w], z[:, c, 0:w], ALU.mult))
            split(k, dve, b[0][:, c, 0:w], b[1][:, c, 0:w], o[:, c, 0:w])

    k.end_stage(block)


def gqa_layer(k, block, l):
    A0, R0 = k.ARENA, k.ARENA + 49152
    a = (k.at("a2_hi", A0, [P, KC, T2], F32R), k.at("a2_lo", A0 + 24576, [P, KC, T2], F32R))
    both = l < 3
    parts = [LAT, CTX] if both else [LAT]
    w = parts[-1][1]
    np_ = len(parts)
    q = k.at("gq", R0, [P, 8, T2])
    kk = k.at("gk", R0 + 24576, [P, 2, T2])
    v = k.at("gv", R0 + 30720, [P, 6, 256])
    z = k.at("gz", R0 + 36864, [P, 8, T2])
    temp = R0 + 61440
    layer_norm_in(k, block, l, a, R0)
    k.dump(f"H{l}", a[0][:].bitcast(F32))

    def into(dst, func, parts):
        n = len(parts)
        return lambda act, i, t, ps: act.activation(
            dst[:, bass.ds(i * 4 + t // n, 1), parts[t % n][0]:parts[t % n][1]].rearrange("p a n -> p (a n)"),
            ps[:, 0:parts[t % n][1] - parts[t % n][0]], func)

    dense(k, block, [f"A{l}q"], feature_major(a, KC, parts), loop=True, act_tile=into(q, ACT.Copy, parts))
    dense(k, block, [f"A{l}k"], feature_major(a, KC, [LAT, CTX]), act_tile=into(kk, ACT.Copy, [LAT, CTX]))
    dense(k, block, [f"A{l}v"], token_major(a, range(6), 256, 256),
          act_tile=lambda act, i, t, ps: act.activation(v[:, t, :], ps[:, 0:256], ACT.Copy))
    dense(k, block, [f"A{l}z"], feature_major(a, KC, parts), loop=True, act_tile=into(z, ACT.Silu, parts))
    rotate(k, block, [q[:, c, 0:S] for c in range(8)] + [kk[:, c, 0:S] for c in range(2)], temp)
    if l == 0:
        k.dump("q0", q[:])
        k.dump("k0", kk[:])
        k.dump("v0", v[:])
        k.dump("z0", z[:])

    sinks = k.row(f"l{l}_sink_2")
    units = []
    for pos, h in enumerate(HEAD_ORDER):
        r0, kv = 64 * (pos % 2), h // 4
        qs = q[r0:r0 + 64, pos // 2]
        ks = kk[r0:r0 + 64, kv // 2]
        vs = lambda b: v[:, b, kv * 64:kv * 64 + 64]
        for b in range(6 if both else 4):
            qb = qs[:, b * P:(b + 1) * P]
            unit = dict(qk=[(0, 256, [(qb, ks[:, S:T2])])], masks=[], scale=A_SCALE, sink=sinks[:, h:h + 1],
                        pv=[vs(4), vs(5)], rows=(r0, r0 + 64), out=qb)
            if b < 4:
                near = range(max(0, b - 1), min(3, b + 1) + 1)
                for n, kb in enumerate(near):
                    unit["qk"].append((256 + n * P, P, [(qb, ks[:, kb * P:(kb + 1) * P])]))
                    if kb != b:
                        unit["masks"].append((256 + n * P, P, k.cst("mask_le" if kb < b else "mask_ge")))
                    unit["pv"].append(vs(kb))
            unit["ranges"] = [(0, P * len(unit["pv"]))]
            units.append(unit)
    attention(k, block, units, temp, 640)
    times_and_split(k, block, q, z, a, w)
    xres = k.io["xres"].rearrange("(c p) t -> p c t", p=P)
    out = xres if both else k.io["outT"].rearrange("(c p) t -> p c t", p=P)
    layer_out(k, block, l, f"A{l}o", a, parts, R0, R0 + 24576, R0 + 49152, out)


def mla_layer(k, block):
    l = 1
    A0, R0 = k.ARENA, k.ARENA + 49152
    a = (k.at("a2_hi", A0, [P, KC, T2], F32R), k.at("a2_lo", A0 + 24576, [P, KC, T2], F32R))
    both = [LAT, CTX]
    layer_norm_in(k, block, l, a, R0)
    z = k.at("mz", R0, [P, 8, T2])
    raw = k.at("m_raw", R0 + 24576, [P, 4, T2])
    low = (k.at("low_hi", R0 + 73728, [P, 3, T2], F32R), k.at("low_lo", R0 + 82944, [P, 3, T2], F32R))
    q = k.at("mq", A0, [P, 8, T2])
    qr = k.at("mqr", A0 + 24576, [P, 4, T2])
    kpe = k.at("kpe", A0 + 36864, [P, T2])
    kn = k.at("mk", R0 + 24576, [P, 8, T2])
    v = k.at("mv", R0 + 49152, [P, 6, 1024])

    def into(dst, func, base=0):
        return lambda act, i, t, ps: act.activation(
            dst[:, base + t // 2, both[t % 2][0]:both[t % 2][1]], ps[:, 0:both[t % 2][1] - both[t % 2][0]], func)

    dense(k, block, ["Bin"], feature_major(a, KC, both), act_tile=into(raw, ACT.Copy))
    dense(k, block, ["Bz"], feature_major(a, KC, both), act_tile=into(z, ACT.Silu))

    squares = k.at("squares", A0 + 40960, [P, 2, T2])
    rstd = k.at("rstd2", R0 + 36864, [P, 2, T2])
    rms_scale(k, block, raw[:, 0:2, :], 2, both, 256, rstd[:, 0], squares, banks=(0, 1))
    rms_scale(k, block, raw[:, 2:3, :], 1, both, 128, rstd[:, 1], squares, banks=(2, 3))
    k.end_stage(block)

    @block.vector
    def _(dve):
        for c in range(3):
            g = k.col("l1_g_qa_2", c) if c < 2 else k.col("l1_g_kva_2")
            k.dve_chain(dve, dve.scalar_tensor_tensor(raw[:, c, :], raw[:, c, :], g, rstd[:, c // 2], ALU.mult,
                                                      ALU.mult))
            split(k, dve, low[0][:, c, :], low[1][:, c, :], raw[:, c, :])
        dve.tensor_copy(kpe[:], raw[:, 3, :])

    k.end_stage(block)
    rotate(k, block, [kpe[:, 0:S]], A0 + 40960)

    dense(k, block, ["Bq"],
          lambda s, hi, lo: feature_major([x[:, 0:2, :] for x in low], 2, both,
                                          chunks=range(8 if s == 0 else 4))(s, hi, lo),
          act_tile=lambda act, i, t, ps: (into(q, ACT.Copy) if t < 16 else into(qr, ACT.Copy, -8))(act, i, t, ps))

    kv = [x[:, 2:3, :] for x in low]

    def kv_tiles(s, hi, lo):
        if s:
            return []
        out = feature_major(kv, 1, both, chunks=range(8))(s, hi, lo)
        for b in range(6):
            for c in range(2):
                cols = slice(1024 + 512 * c, 1536 + 512 * c)
                out.append((lambda bank: bank,
                            [((kv[0][:, 0, b * P:(b + 1) * P], kv[1][:, 0, b * P:(b + 1) * P]),
                              (hi[:, cols], lo[:, cols]))]))
        return out

    def take(act, i, t, ps):
        if t < 16:
            return into(kn, ACT.Copy)(act, i, t, ps)
        b, c = divmod(t - 16, 2)
        return act.activation(v[:, b, 512 * c:512 * c + 512], ps, ACT.Copy)

    dense(k, block, ["Bk", "_Bk"], kv_tiles, act_tile=take)
    rotate(k, block, [qr[:, c, 0:S] for c in range(4)], R0 + 73728)

    units = []
    for h in range(8):
        r0 = 64 * (h % 2)
        for b in range(6):
            t = slice(b * P, (b + 1) * P)
            keys = [LAT, CTX] if b < 4 else [CTX]
            qk = [(512 * n, k1 - k0, [(q[:, h, t], kn[:, h, k0:k1]), (qr[r0:r0 + 64, h // 2, t],
                                                                     kpe[r0:r0 + 64, k0:k1])])
                  for n, (k0, k1) in enumerate(keys)]
            blocks = range(6) if b < 4 else (4, 5)
            units.append(dict(qk=qk, masks=[], ranges=[(0, P * len(blocks))], scale=B_SCALE, sink=None,
                              pv=[v[:, kb, h * P:(h + 1) * P] for kb in blocks], rows=(0, P), out=q[:, h, t]))
    attention(k, block, units, R0 + 73728, 768)
    b2 = (k.at("b2_hi", R0 + 24576, [P, KC, T2], F32R), k.at("b2_lo", R0 + 49152, [P, KC, T2], F32R))
    times_and_split(k, block, q, z, b2, T2)
    layer_out(k, block, l, "Bo", b2, both, A0, A0 + 24576, R0, k.io["xres"].rearrange("(c p) t -> p c t", p=P))


def second_block(k, block):
    gqa_layer(k, block, 0)
    k.dump("Y0", k.at("y", k.ARENA + 49152, [P, KC, T2])[:])
    k.dump("X0", k.at("x_out", k.ARENA + 49152+24576, [P, KC, T2])[:])
    mla_layer(k, block)
    k.dump("X1", k.at("x_out", k.ARENA + 24576, [P, KC, T2])[:])
    mlstm_layer(k, block)
    k.dump("X2", k.at("x_out", k.ARENA + 24576, [P, KC, T2])[:])
    gqa_layer(k, block, 3)


def mlstm_layer(k, block):
    l = 2
    A0, R0 = k.ARENA, k.ARENA + 49152
    a = (k.at("a2_hi", A0, [P, KC, T2], F32R), k.at("a2_lo", A0 + 24576, [P, KC, T2], F32R))
    both = [LAT, CTX]
    H, KS = 4, P ** -0.5
    qk = k.at("cqk", R0, [P, 8, T2])
    v = k.at("cv", R0 + 24576, [P, 6, 1024])
    k_tok = k.at("ck_tok", R0 + 49152, [P, 6, 512])
    hsum = k.at("hsum", R0 + 61440, [P, 6, 1024])
    gates = k.at("c_gates", R0 + 86016, [P, 6, 16])
    layer_norm_in(k, block, l, a, R0)

    pad = k.at("c_pad", R0 + 49152, [P, 8, S + 4])
    conv = k.at("c_conv", R0 + 49152 + 32 * (S + 4), [P, 2, S])

    @block.vector
    def _(dve):
        for t in range(8):
            n = S if t % 2 == 0 else SC
            dve.memset(pad[:, t, 0:2], 0.0)
            k.dve_chain(dve, dve.memset(pad[:, t, 2 + n:4 + n], 0.0))

    def conv_tile(dve, i, t, ps):
        c, n = t // 2, (S if t % 2 == 0 else SC)
        src, dst = pad[:, t % 8], conv[:, t % 2, 0:n]
        tap = lambda j: k.col("l2_conv_2", 8 * j + c)
        if t >= 2:
            dve.wait_ge(k.tile_free.sem, k.tile_free.at(t - 1))
        k.dve_chain(dve, dve.tensor_scalar(dst, src[:, 0:n], tap(0), None, ALU.mult))
        for j in (1, 2, 3):
            k.dve_chain(dve, dve.scalar_tensor_tensor(dst, src[:, j:j + n], tap(j), dst, ALU.mult, ALU.add))
        return dve.scalar_tensor_tensor(dst, src[:, 4:4 + n], tap(4), dst, ALU.mult, ALU.add)

    def span(t):
        n = S if t % 2 == 0 else SC
        return n, (S if t % 2 else 0)

    dense(k, block, ["Cqk"], feature_major(a, KC, both),
          act_tile=lambda act, i, t, ps: act.activation(pad[:, t % 8, 2:2 + span(t)[0]], ps[:, 0:span(t)[0]],
                                                        ACT.Copy),
          dve_tile=conv_tile,
          act_last=lambda act, i, t: act.activation(qk[:, t // 2, span(t)[1]:span(t)[1] + span(t)[0]],
                                                    conv[:, t % 2, 0:span(t)[0]], ACT.Silu))
    dense(k, block, ["Cv"], token_major(a, range(6), 256, 256),
          act_tile=lambda act, i, t, ps: act.activation(v[:, t % 6, 256 * (t // 6):256 * (t // 6) + 256],
                                                        ps[:, 0:256], ACT.Copy))
    dense(k, block, ["Cg", "_Cg"],
          lambda s, hi, lo: token_major(a, range(6), 16, 16)(s, hi, lo) if s == 0 else [],
          dve_tile=lambda dve, i, t, ps: dve.tensor_tensor(gates[:, t, :], ps[:, 0:16], k.row("l2_b_gate_2"),
                                                           ALU.add))

    turned, taken = k.sem_named("turned"), k.sem_named("turned_taken")

    @block.tensor
    def _(pe):
        for b in range(6):
            if b >= 2:
                pe.wait_ge(taken.sem, taken.at(b - 1))
            for h in range(H):
                last = pe.transpose(k.psum[:, b % 2, h * P:(h + 1) * P], qk[:, 4 + h, b * P:(b + 1) * P],
                                    k.cst("ident"))
            last.then_inc(turned.sem, 1)

    o = A0
    g48 = lambda name, n: k.at(name, o + 192 * n, [P, 2, 6, H])
    ig, f, e, u, t1, cum, g = (g48(f"c_{x}", n) for n, x in enumerate(("ig", "f", "e", "u", "t1", "cum", "g")))
    tot = g48("c_tot", 7)
    flat = lambda x: x[:].rearrange("p d b h -> p (d b h)")
    to_act, to_dve, to_pe = (k.sem_named(f"ssd_to_{x}") for x in ("act", "dve", "pe"))

    @block.vector
    def _(dve):
        ch = k.dve_chain
        for b in range(6):
            dve.wait_ge(turned.sem, turned.at(b + 1))
            dve.tensor_scalar(k_tok[:, b, :], k.psum[:, b % 2, :], KS, None, ALU.mult).then_inc(taken.sem, 1)
        for d in range(2):
            dve.tensor_copy(ig[:, d], gates[:, :, 8 * d:8 * d + 4])
            ch(dve, dve.tensor_copy(f[:, d], gates[:, :, 8 * d + 4:8 * d + 8]))
        ch(dve, dve.tensor_scalar(flat(e), flat(f), -1.0, None, ALU.mult))
        dve.tensor_tensor(flat(e), flat(f), flat(e), ALU.min).then_inc(to_act.sem, 1)
        dve.wait_ge(to_dve.sem, to_dve.at(1))
        ch(dve, dve.tensor_scalar(flat(u), flat(e), 1.0, None, ALU.add))
        dve.nop().then_inc(to_act.sem, 1)
        ch(dve, dve.scalar_tensor_tensor(flat(g), flat(u), -1.0, flat(e), ALU.add, ALU.subtract))
        ch(dve, dve.reciprocal(flat(t1), flat(u)))
        ch(dve, dve.tensor_tensor(flat(g), flat(g), flat(t1), ALU.mult))
        dve.wait_ge(to_dve.sem, to_dve.at(2))
        ch(dve, dve.tensor_tensor(flat(g), flat(cum), flat(g), ALU.subtract))
        ch(dve, dve.scalar_tensor_tensor(flat(f), flat(f), 0.0, flat(g), ALU.min, ALU.subtract))
        dve.nop().then_inc(to_pe.sem, 1)
        dve.wait_ge(to_dve.sem, to_dve.at(3))
        ch(dve, dve.tensor_copy(flat(cum), k.psum[:, 2, 0:48]))
        dve.tensor_copy(flat(tot), k.psum[:, 3, 0:48])
        dve.tensor_tensor(flat(g), flat(ig), flat(cum), ALU.subtract)

    @block.scalar
    def _(act):
        act.wait_ge(to_act.sem, to_act.at(1))
        act.activation(flat(e), flat(e), ACT.Exp).then_inc(to_dve.sem, 1)
        act.wait_ge(to_act.sem, to_act.at(2))
        act.activation(flat(cum), flat(u), ACT.Ln).then_inc(to_dve.sem, 1)

    @block.tensor
    def _(pe):
        pe.wait_ge(to_pe.sem, to_pe.at(1))
        pe.matmul(k.psum[:, 2, 0:24], k.cst("tri"), f[:, 0].rearrange("p b h -> p (b h)"), start=True, stop=True)
        pe.matmul(k.psum[:, 2, 24:48], k.cst("triT"), f[:, 1].rearrange("p b h -> p (b h)"), start=True, stop=True)
        pe.matmul(k.psum[:, 3, 0:48], k.cst("ones"), flat(f), start=True, stop=True).then_inc(to_dve.sem, 1)

    turned.stage_over(6)
    taken.stage_over(6)
    to_act.stage_over(2)
    to_dve.stage_over(3)
    to_pe.stage_over(1)
    k.end_stage(block)

    o = A0 + 2048
    diag = k.at("c_diag", o, [P, 2, H, P])
    gm = k.at("c_gm", o + 4096, [P, 2, H, P])
    prob = k.at("c_prob", o + 8192, [P, 2, H, P])
    prob_t = k.at("c_prob_t", o + 12288, [P, 2, H * P])
    ke = k.at("c_ke", o + 16384, [P, 2, H, P])
    state = k.at("c_state", o + 20480, [P, 2, H, 256])
    norm = k.at("c_norm", o + 28672, [P, 2, H])
    m_st = k.at("c_m", o + 28704, [P, 2, H])
    st = k.at("c_small", o + 28736, [P, 2, 16, H])
    order = [[4, 5, 0, 1, 2, 3], [5, 4, 3, 2, 1, 0]]
    steps = [(j, d, order[d][j]) for j in range(6) for d in range(2)]
    N = len(steps)
    names = ("diag_in", "scores", "sub_in", "exp_out", "ke_in", "prob_in", "turn", "turn_copied", "num2", "num1",
             "outs_taken", "local", "state_new", "nq_read")
    (diag_in, scores, sub_in, exp_out, ke_in, prob_in, turn, turn_copied, num2, num1, outs_taken, local,
     state_new, nq_read) = (k.sem_named(f"c_{x}") for x in names)
    bc = lambda x: x.unsqueeze(2).broadcast_to([P, H, P])
    ident4 = k.cst("ident").unsqueeze(1).broadcast_to([P, H, P])
    heads = lambda x: x.rearrange("p (h n) -> p h n", h=H)
    n2 = lambda h: k.psum[:, 4 + h // 2, 256 * (h % 2):256 * (h % 2) + 256]
    n1 = lambda h: k.psum[:, 3 if h < 2 else 6, 256 * (h % 2):256 * (h % 2) + 256]
    lc = lambda h: k.psum[:, h // 2, 256 * (h % 2):256 * (h % 2) + 256]

    @block.tensor
    def _(pe):
        for s, (j, d, b) in enumerate(steps):
            t = slice(b * P, (b + 1) * P)
            if s:
                pe.wait_ge(state_new.sem, state_new.at(s))
            for h in range(H):
                pe.matmul(k.psum[:, 0, h * P:(h + 1) * P], qk[:, h, t], qk[:, 4 + h, t], start=True, stop=True)
            pe.wait_ge(diag_in.sem, diag_in.at(s + 1))
            pe.matmul(k.psum[:, 1, :], k.cst("ones"), diag[:, s % 2].rearrange("p h n -> p (h n)"), start=True,
                      stop=True).then_inc(scores.sem, 1)
            if s:
                pe.wait_ge(outs_taken.sem, outs_taken.at(s))
            for h in range(H):
                pe.matmul(n2(h), qk[:, h, t], state[:, d, h, :], start=True, stop=True)
            for h in range(H):
                last = pe.matmul(k.psum[:, 7, h:h + 1], qk[:, h, t], norm[:, d, h:h + 1], start=True, stop=True)
            last.then_inc(num2.sem, 1)
            pe.wait_ge(prob_in.sem, prob_in.at(s + 1))
            for h in range(H):
                last = pe.transpose(k.psum[:, 2, h * P:(h + 1) * P], prob[:, s % 2, h, :], k.cst("ident"))
            last.then_inc(turn.sem, 1)
            pe.wait_ge(ke_in.sem, ke_in.at(s + 1))
            for h in range(H):
                pe.matmul(lc(h), ke[:, s % 2, h, :], v[:, b, 256 * h:256 * h + 256], start=True, stop=True)
            pe.wait_ge(nq_read.sem, nq_read.at(s + 1))
            for h in range(H):
                last = pe.matmul(k.psum[:, 7, 8 + h:9 + h], ke[:, s % 2, h, :], k.cst("ones")[:, 0:1], start=True,
                                 stop=True)
            last.then_inc(local.sem, 1)
            pe.wait_ge(turn_copied.sem, turn_copied.at(s + 1))
            for h in range(H):
                last = pe.matmul(n1(h), prob_t[:, s % 2, h * P:(h + 1) * P], v[:, b, 256 * h:256 * h + 256],
                                 start=True, stop=True)
            last.then_inc(num1.sem, 1)

    @block.scalar
    def _(act):
        for s, (j, d, b) in enumerate(steps):
            act.wait_ge(sub_in.sem, sub_in.at(s + 1))
            act.activation(gm[:, s % 2], gm[:, s % 2], ACT.Exp)
            act.activation(st[:, s % 2, 0:5], st[:, s % 2, 0:5], ACT.Exp).then_inc(exp_out.sem, 1)
            act.wait_ge(turn.sem, turn.at(s + 1))
            act.activation(prob_t[:, s % 2], k.psum[:, 2, :], ACT.Copy).then_inc(turn_copied.sem, 1)

    @block.vector
    def _(dve):
        ch = k.dve_chain
        ch(dve, dve.memset(m_st[:], NEG))
        ch(dve, dve.memset(norm[:], 0.0))
        ch(dve, dve.memset(state[:], 0.0))
        ch(dve, dve.memset(hsum[:], 0.0))

        def diagonal(s):
            j, d, b = steps[s]
            if s >= 2:
                dve.wait_ge(scores.sem, scores.at(s - 1))
            dve.tensor_tensor(diag[:, s % 2], ident4, bc(g[:, d, b, :]), ALU.mult).then_inc(diag_in.sem, 1)

        diagonal(0)
        for s, (j, d, b) in enumerate(steps):
            S_ = lambda n: st[:, s % 2, n]
            if s + 1 < N:
                diagonal(s + 1)
            mask = k.cst("mask_ge" if d == 0 else "mask_le").unsqueeze(1).broadcast_to([P, H, P])
            dve.wait_ge(scores.sem, scores.at(s + 1))
            rows = heads(k.psum[:, 1, :])
            ch(dve, dve.tensor_tensor(gm[:, s % 2], rows, mask, ALU.add))
            dve.tensor_reduce(S_(8), gm[:, s % 2], AX.X, ALU.max)
            ch(dve, dve.tensor_reduce(S_(9), rows, AX.X, ALU.max))
            m = m_st[:, d, :]
            ch(dve, dve.tensor_tensor(S_(10), S_(8), m, ALU.max))
            ch(dve, dve.tensor_tensor(S_(11), S_(9), m, ALU.max))
            dve.tensor_tensor(gm[:, s % 2], gm[:, s % 2], bc(S_(10)), ALU.subtract)
            dve.tensor_tensor(S_(0), m, S_(10), ALU.subtract)
            dve.scalar_tensor_tensor(S_(1), cum[:, d, b, :], -1.0, S_(10), ALU.mult, ALU.subtract)
            dve.tensor_tensor(S_(2), g[:, d, b, :], S_(9), ALU.subtract)
            dve.tensor_tensor(S_(3), m, S_(11), ALU.subtract)
            ch(dve, dve.tensor_tensor(S_(4), S_(9), S_(11), ALU.subtract))
            ch(dve, dve.tensor_tensor(m, tot[:, d, b, :], S_(11), ALU.add))
            dve.nop().then_inc(sub_in.sem, 1)

            dve.wait_ge(exp_out.sem, exp_out.at(s + 1))
            ch(dve, dve.scalar_tensor_tensor(prob[:, s % 2], heads(k.psum[:, 0, :]), KS, gm[:, s % 2], ALU.mult,
                                             ALU.mult))
            dve.nop().then_inc(prob_in.sem, 1)
            dve.tensor_tensor(ke[:, s % 2], heads(k_tok[:, b, :]), bc(S_(2)), ALU.mult).then_inc(ke_in.sem, 1)
            ch(dve, dve.tensor_reduce(S_(12), prob[:, s % 2], AX.X, ALU.add))
            dve.wait_ge(num2.sem, num2.at(s + 1))
            ch(dve, dve.tensor_tensor(S_(13), k.psum[:, 7, 0:H], S_(0), ALU.mult))
            dve.nop().then_inc(nq_read.sem, 1)
            ch(dve, dve.tensor_tensor(S_(12), S_(12), S_(13), ALU.add))
            ch(dve, dve.tensor_scalar(S_(13), S_(12), -1.0, None, ALU.mult))
            ch(dve, dve.tensor_tensor(S_(12), S_(12), S_(13), ALU.max))
            ch(dve, dve.tensor_tensor(S_(12), S_(12), S_(1), ALU.max))
            ch(dve, dve.reciprocal(S_(14), S_(12)))
            ch(dve, dve.tensor_tensor(S_(15), S_(14), S_(0), ALU.mult))
            dve.wait_ge(num1.sem, num1.at(s + 1))
            for part, src, col in ((0, n2, 15), (1, n1, 14)):
                for h in range(H):
                    hs = hsum[:, b, 256 * h:256 * h + 256]
                    last = dve.scalar_tensor_tensor(hs, src(h), S_(col)[:, h:h + 1], hs, ALU.mult, ALU.add)
                ch(dve, last)
            dve.wait_ge(local.sem, local.at(s + 1))
            for h in range(H):
                last = dve.tensor_scalar(state[:, d, h, :], state[:, d, h, :], S_(3)[:, h:h + 1], None, ALU.mult)
            ch(dve, last)
            for h in range(H):
                dve.scalar_tensor_tensor(state[:, d, h, :], lc(h), S_(4)[:, h:h + 1], state[:, d, h, :], ALU.mult,
                                         ALU.add)
            ch(dve, dve.tensor_tensor(norm[:, d, :], norm[:, d, :], S_(3), ALU.mult))
            ch(dve, dve.tensor_tensor(S_(13), k.psum[:, 7, 8:8 + H], S_(4), ALU.mult))
            ch(dve, dve.tensor_tensor(norm[:, d, :], norm[:, d, :], S_(13), ALU.add))
            dve.nop().then_inc(state_new.sem, 1)
            dve.nop().then_inc(outs_taken.sem, 1)

    for x in (diag_in, scores, sub_in, exp_out, ke_in, prob_in, turn, turn_copied, num2, num1, outs_taken, local,
              state_new, nq_read):
        x.stage_over(N)
    k.end_stage(block)

    layer_norm_in(k, block, l, a, R0)
    part = k.at("c_part", R0, [P, 6, 256])

    def gate(dve, i, t, ps):
        hs = hsum[:, t % 6, 256 * (t // 6):256 * (t // 6) + 256]
        return dve.tensor_tensor(hs, hs, part[:, t % 6, :], ALU.mult)

    dense(k, block, ["Cog"], token_major(a, range(6), 256, 256),
          act_tile=lambda act, i, t, ps: act.activation(part[:, t % 6, :], ps[:, 0:256], ACT.Sigmoid),
          dve_tile=gate)

    sq = k.at("c_sq", R0 + 8192, [P, 256])
    ms = k.at("c_ms", R0 + 9216, [P, 24])
    ready = k.sem_named("rstd_ready")

    @block.scalar
    def _(act):
        for n in range(24):
            b, h = divmod(n, H)
            k.act_chain(act, act.activation(sq[:], hsum[:, b, 256 * h:256 * h + 256], ACT.Square,
                                            accum_out=ms[:, n:n + 1]))
        k.act_chain(act, act.activation(ms[:], ms[:], ACT.Ln, bias=k.eps[:], scale=1.0 / 256))
        act.activation(ms[:], ms[:], ACT.Exp, scale=-0.5).then_inc(ready.sem, 1)

    @block.vector
    def _(dve):
        dve.wait_ge(ready.sem, ready.at(1))
        for n in range(24):
            b, h = divmod(n, H)
            hs = hsum[:, b, 256 * h:256 * h + 256]
            dve.scalar_tensor_tensor(hs, hs, ms[:, n:n + 1], k.row("l2_g_head_2")[:, 256 * h:256 * h + 256],
                                     ALU.mult, ALU.mult)

    ready.stage_over(1)
    k.end_stage(block)
    dense(k, block, ["Cz"], token_major(a, range(6), 256, 256),
          act_tile=lambda act, i, t, ps: act.activation(part[:, t % 6, :], ps[:, 0:256], ACT.Silu),
          dve_tile=gate)

    b2 = (k.at("b3_hi", R0, [P, KC, T2], F32R), k.at("b3_lo", R0 + 24576, [P, KC, T2], F32R))

    @block.tensor
    def _(pe):
        for n in range(16):
            c, half = divmod(n, 2)
            if n >= 4:
                pe.wait_ge(taken.sem, taken.at(n - 3))
            for j, b in enumerate((0, 1, 2, 3) if half == 0 else (4, 5)):
                last = pe.transpose(k.psum[:, n % 4, j * P:(j + 1) * P], hsum[:, b, c * P:(c + 1) * P],
                                    k.cst("ident"))
            last.then_inc(turned.sem, 1)

    @block.vector
    def _(dve):
        for n in range(16):
            c, half = divmod(n, 2)
            t0, t1 = both[half]
            dve.wait_ge(turned.sem, turned.at(n + 1))
            ps = k.psum[:, n % 4, 0:t1 - t0]
            k.dve_chain(dve, dve.tensor_copy(b2[0][:, c, t0:t1], ps))
            dve.tensor_tensor(b2[1][:, c, t0:t1], ps, b2[0][:, c, t0:t1].bitcast(F32), ALU.subtract) \
                .then_inc(taken.sem, 1)

    turned.stage_over(16)
    taken.stage_over(16)
    k.end_stage(block)
    layer_out(k, block, l, "Co", b2, both, A0, A0 + 24576, R0, k.io["xres"].rearrange("(c p) t -> p c t", p=P))


def build(nc, io, debug=None):
    with ExitStack() as ctx:
        k = Kernel(nc, ctx, io)
        block = ctx.enter_context(nc.Block())
        k.debug = debug

        def dump(name, ap):
            if debug is None:
                return
            shape = [int(x) for x in ap.shape]
            if name in debug or debug == ["all"]:
                d = nc.dram_tensor(f"dbg_{name}", shape, F32, kind="ExternalOutput").ap()
                store(k, block, [(d, ap)])
        k.dump = dump
        weight_stream(k, block)
        setup(k, block)
        modulation(k, block)
        first_block(k, block)
        second_block(k, block)



def layout(inputs):
    f = lambda name: np.asarray(inputs[name])
    w = {}
    for name, _, _, _ in PLAN:
        if name not in w:
            w[name] = f("w_pool_mix").reshape(1024, 256) if name == "mix" else \
                f(name)[0] if f(name).ndim == 3 else f(name)
    for name in ("l0_w_out_2", "l3_w_out_2"):
        w[name] = w[name][np.asarray(HEAD_COLS)]
    stream = np.zeros((N_SLOTS, P, SLOT), np.float32)
    for s, (name, r0, r1, cols) in enumerate(PLAN):
        kc = (r1 - r0) // P
        part = w[name][r0:r1][:, np.asarray(cols)]
        if kc * len(cols) <= SLOT:
            width = SLOT // kc
            stream[s].reshape(P, kc, width)[:, :, :len(cols)] = part.reshape(kc, P, len(cols)).transpose(1, 0, 2)
    ada = np.zeros((72, P, SLOT), np.float32)
    for s, (name, c) in enumerate(ada_plan()):
        m = f(name)[0] if f(name).ndim == 3 else f(name)
        ada[s] = m[:, 256 * c:256 * c + 256].reshape(KC, P, 256).transpose(1, 0, 2).reshape(P, SLOT)
    cols = np.zeros((P, N_COLS), np.float32)
    for name, n in COLS.items():
        v = f(name)
        if name == "d_skip":
            v = np.repeat(v, SSD_P)
        if name == "l2_conv_2" or name == "conv_w":
            v = v.reshape(-1)
        cols[:, COL_AT[name]:COL_AT[name] + n] = v.reshape(n, P).T
    rows = np.zeros((P, N_ROWS), np.float32)
    for name, n in ROWS.items():
        rows[:, ROW_AT[name]:ROW_AT[name] + n] = f(name).reshape(1, n)
    return {"stream": stream, "ada": ada, "cols": cols, "rows": rows, "consts": constants(),
            "xT": np.ascontiguousarray(f("x")[0].T), "ctxT": np.ascontiguousarray(f("ctx_2")[0].T)}


def kernel(**inputs):
    import concourse.bacc as bacc
    from concourse.bass_utils import run_bass_kernel_spmd

    nc = bacc.Bacc("TRN2", target_bir_lowering=False, num_devices=1)
    arrays = layout(inputs)
    io = {name: nc.dram_tensor(name, a.shape, F32, kind="ExternalInput").ap() for name, a in arrays.items()}
    io["outT"] = nc.dram_tensor("outT", (D, S), F32, kind="ExternalOutput").ap()
    io["xres"] = nc.dram_tensor("xres", (D, T2), F32).ap()
    build(nc, io)
    result = run_bass_kernel_spmd(nc, [arrays], core_ids=[0])
    return np.ascontiguousarray(result.results[0]["outT"].T)[None]
```

```python
import math
from contextlib import ExitStack

import numpy as np
import concourse.bass as bass
from concourse import mybir

F32 = mybir.dt.float32
F32R = mybir.dt.float32r
ACT = mybir.ActivationFunctionType
ALU = mybir.AluOpType
AX = mybir.AxisListType

P = 128
D = 1024
KC = D // P
S = 512
SC = 256
T2 = S + SC
SLOT = 2048
EPS = 1e-6
NEG = -1.0e30

SSD_HEADS, SSD_P, SSD_N = 16, 64, 128
A_SCALE = 64 ** -0.5
B_SCALE = 192 ** -0.5
FF = 4096



HEAD_ORDER = [h for c in range(2) for i in range(4) for h in (8 * c + i, 8 * c + 4 + i)]
HEAD_COLS = [h * 64 + e for h in HEAD_ORDER for e in range(64)]


def slot_plan():
    plan = []

    def slots(section, name, rows, cols):
        kc = (rows[1] - rows[0]) // P
        width = SLOT // kc
        first = len(plan)
        for c in range(0, len(cols), width):
            plan.append((name, rows[0], rows[1], tuple(cols[c:c + width])))
        sections[section] = (first, len(plan) - first)

    sections = {}
    R = lambda a, n: list(range(a, a + n))
    full = (0, D)
    z0, xbc0, dt0 = 0, 1024, 2560
    q0 = 2576
    k0, v0, u0, g0 = q0 + 1536, q0 + 3072, q0 + 4608, q0 + 5632
    slots("z", "w_in", full, R(z0, 1024))
    slots("xbc", "w_in", full, R(xbc0, 1536))
    slots("dt", "w_in", full, R(dt0, 16))
    for c in range(4):
        slots(f"g_ssd{c}", "w_in", full, R(g0 + 256 * c, 256))
        slots(f"ssd_out{c}", "w_ssd_out", full, R(256 * c, 256))
    for j in range(4):
        cols = []
        for base in (q0, k0, v0):
            for g in range(3):
                cols += R(base + (4 * g + j) * P, P)
        slots(f"qkv{j}", "w_in", full, cols)
    for c in range(2):
        slots(f"attn_out{c}", "w_attn_out", (0, 512), R(512 * c, 512))
        slots(f"g_attn{c}", "w_in", full, R(g0 + 1024 + 512 * c, 512))
    slots("u", "w_in", full, R(u0, 1024))
    slots("mix", "mix", (0, 1024), R(0, 256))
    for c in range(4):
        slots(f"g_pool{c}", "w_in", full, R(g0 + 2048 + 256 * c, 256))
        slots(f"pool_out{c}", "w_pool_out", full, R(256 * c, 256))
    slots("out", "w_out", full, R(0, 1024))
    for b in range(4):
        slots(f"ff1_{b}", "w_ff1", full, R(1024 * b, 1024))
        slots(f"ff2_{b}", "w_ff2", (1024 * b, 1024 * b + 1024), R(0, 1024))

    hcols = HEAD_COLS
    for l in (0, 3):
        w = f"l{l}_w_in_2"
        slots(f"A{l}q", w, full, hcols)
        slots(f"A{l}k", w, full, R(1024, 256))
        slots(f"A{l}v", w, full, R(1280, 256))
        slots(f"A{l}z", w, full, [1536 + c for c in hcols])
        slots(f"A{l}o", f"l{l}_w_out_2", full, R(0, 1024))
        if l == 0:
            w = "l1_w_in_2"
            slots("Bin", w, full, R(0, 256) + R(256, 128) + R(384, 64) + R(384, 64))
            slots("Bz", w, full, R(448, 1024))
            slots("Bq", "l1_w_uq_2", (0, 256),
                  [h * 192 + e for h in range(8) for e in range(128)]
                  + [h * 192 + 128 + e for h in range(8) for e in range(64)])
            slots("Bk", "l1_w_ukv_2", (0, 128), [h * 256 + e for h in range(8) for e in range(128)]
                  + [h * 256 + 128 + e for h in range(8) for e in range(128)])
            slots("Bo", "l1_w_out_2", full, R(0, 1024))
            w = "l2_w_in_2"
            slots("Cqk", w, full, R(0, 1024))
            slots("Cv", w, full, R(1024, 1024))
            slots("Cg", w, full, R(4096, 16))
            slots("Cog", w, full, R(2048, 1024))
            slots("Cz", w, full, R(3072, 1024))
            slots("Co", "l2_w_out_2", full, R(0, 1024))
    return plan, sections


PLAN, SECTIONS = slot_plan()


def ada_plan():
    return [("w_ada", c) for c in range(24)] + [(f"l{l}_w_ada_2", c) for l in range(4) for c in range(12)]


COLS = {"c": 8, "c_2": 8, "c_ctx_2": 8, "b_ada": 48, "norm1_w": 8, "norm2_w": 8, "conv_w": 48,
        "conv_b": 12, "d_skip": 8, "ssd_norm_w": 8, "q_norm_w": 1, "k_norm_w": 1, "pool_scale": 8,
        "l1_g_qa_2": 2, "l1_g_kva_2": 1, "l2_conv_2": 40}
for _l in range(4):
    COLS |= {f"l{_l}_b_ada_2": 24, f"l{_l}_g_pre_2": 8, f"l{_l}_g_post_2": 8}
COL_AT, _n = {}, 0
for _k, _w in COLS.items():
    COL_AT[_k] = _n
    _n += _w
N_COLS = _n

ROWS = {"dt_bias": 16, "a_log": 16, "l2_b_gate_2": 16, "l0_sink_2": 16, "l3_sink_2": 16, "l2_g_head_2": 1024}
ROW_AT, _n = {}, 0
for _k, _w in ROWS.items():
    ROW_AT[_k] = _n
    _n += _w
N_ROWS = _n

CONSTS = {"ident": 128, "ones": 128, "tri": 128, "triT": 128, "mask_le": 128, "mask_ge": 128,
          "swap": 128, "cos": 512, "sin": 512, "negd": 512, "mask0": 512, "mask1": 512, "mask2": 512,
          "pool_inv": 64}
CONST_AT, _n = {}, 0
for _k, _w in CONSTS.items():
    CONST_AT[_k] = _n
    _n += _w
N_CONSTS = _n


def constants():
    out = np.zeros((P, N_CONSTS), np.float32)
    p = np.arange(P)[:, None]
    f = np.arange(P)[None, :]

    def put(name, a):
        out[:, CONST_AT[name]:CONST_AT[name] + CONSTS[name]] = a

    put("ident", p == f)
    put("ones", 1.0)
    put("tri", p <= f)
    put("triT", p >= f)
    put("mask_le", np.where(p <= f, 0.0, NEG))
    put("mask_ge", np.where(p >= f, 0.0, NEG))
    sw = np.zeros((P, P), np.float32)
    for i in range(0, P, 2):
        sw[i + 1, i] = -1.0
        sw[i, i + 1] = 1.0
    put("swap", sw)
    t = np.arange(S)
    n_freq = 16
    inv = (np.float32(10000.0) ** (-np.arange(n_freq, dtype=np.float32) / np.float32(n_freq))).astype(np.float32)
    ang = np.concatenate([(t // 64).astype(np.float32)[:, None] * inv,
                          (t % 64).astype(np.float32)[:, None] * inv], axis=1)
    ang = np.repeat(ang, 2, axis=1).T
    ang = np.concatenate([ang, ang], axis=0)
    put("cos", np.cos(ang))
    put("sin", np.sin(ang))
    c = np.arange(512)[None, :]
    dist = p + 384 - c
    put("negd", -dist.astype(np.float32))
    for g, (win, dil) in enumerate(((128, 1), (512, 4), (2048, 16))):
        ok = (dist >= 0) & (dist % dil == 0) & (dist <= win)
        put(f"mask{g}", np.where(ok, 0.0, NEG))
    inv_count = np.concatenate([1.0 / np.minimum(np.arange(16) + 1, w) for w in (2, 4, 8, 16)])
    put("pool_inv", inv_count[None, :].astype(np.float32))
    return out


def alibi_slopes(n):
    def pow2(k):
        start = 2.0 ** (-8.0 / k)
        return [start ** (i + 1) for i in range(k)]
    c = 2 ** math.floor(math.log2(n))
    s = pow2(n) if c == n else pow2(c) + pow2(2 * c)[0::2][: n - c]
    return sorted((float(np.float32(x)) for x in s), reverse=True)



class Signal:

    def __init__(self, handle):
        self.sem = handle
        self.base = 0

    def at(self, n):
        return self.base + n

    def stage_over(self, n):
        self.base += n


class Chain:

    def __init__(self, handle):
        self.sem = handle
        self.count = 0
        self.loop = 0

    def __call__(self, eng, ins):
        ins.then_inc(self.sem, 1)
        self.count += 1
        eng.wait_ge(self.sem, self.loop + self.count)

    def mark(self, ins):
        ins.then_inc(self.sem, 1)
        self.count += 1
        return self.count

    def behind(self, eng, ins, lag):
        ins.then_inc(self.sem, 1)
        self.count += 1
        eng.wait_ge(self.sem, self.loop + self.count - lag)


class Kernel:

    RING, CONST, ARENA, TOP = 0, 49152, 69632, 212832

    def __init__(self, nc, ctx, io):
        self.nc, self.ctx, self.io = nc, ctx, io
        sem = lambda name: ctx.enter_context(nc.semaphore(name))
        self.raw_loaded = [sem("raw_loaded0"), sem("raw_loaded1")]
        self.hi_ready = sem("hi_ready")
        self.lo_ready = sem("lo_ready")
        self.stage_end = sem("stage_end")
        self.stages = 0
        self.tile_done = Signal(sem("tile_done"))
        self.tile_free = Signal(sem("tile_free"))
        self.tile_free.base = 8
        self.staged = Signal(sem("staged"))
        self.finished = Signal(sem("finished"))
        self.signals = {}
        self.dve_chain = Chain(sem("dve_chain"))
        self.act_chain = Chain(sem("act_chain"))
        self.dma_n = {}
        self.tensors = {}
        self.rhs_ready = None
        self.first_byte = (nc.sbuf_base + 31) // 32 * 32

        at = self.at
        self.raw = at("raw", 0, [P, 2, SLOT])
        self.w_hi = at("w_hi", 16384, [P, 2, SLOT], F32R)
        self.w_lo = at("w_lo", 32768, [P, 2, SLOT], F32R)
        o = self.CONST
        self.const = at("const", o, [P, N_COMMON])
        o += 4 * N_COMMON
        self.cols = at("cols", o, [P, N_COLS])
        o += 4 * N_COLS
        self.rows = at("rows", o, [P, N_ROWS])
        o += 4 * N_ROWS
        self.cond = at("cond", o, [P, 2, KC, 2])
        o += 4 * 32
        self.mod1 = at("mod1", o, [P, 48])
        o += 4 * 48
        self.mod2 = at("mod2", o, [P, 4, 24, 2])
        o += 4 * 192
        self.coef = at("coef", o, [P, 2, KC])
        o += 4 * 16
        self.coef2 = at("coef2", o, [P, 4, KC, 2])
        o += 4 * 64
        self.gate2 = at("gate2", o, [P, 4, KC, 2])
        o += 4 * 64
        self.eps = at("eps", o, [P, 1])
        o += 4
        assert o <= self.ARENA, o
        self.psum = ctx.enter_context(nc.psum_tensor("psum", [P, 8, 512], F32))

    def sem_named(self, name):
        if name not in self.signals:
            self.signals[name] = Signal(self.ctx.enter_context(self.nc.semaphore(name)))
        return self.signals[name]

    def at(self, name, offset, shape, dtype=F32):
        size = 4 * int(np.prod(shape[1:]))
        assert offset + size <= self.TOP, (name, offset + size)
        key = (name, offset, tuple(shape), str(dtype))
        if key not in self.tensors:
            self.tensors[key] = self.nc.alloc_sbuf_tensor_at(f"{name}_{len(self.tensors)}", shape, dtype,
                                                             offset=self.first_byte + (offset + 31) // 32 * 32)
        return self.tensors[key]

    def col(self, name, i=0, n=1):
        return self.cols[:, COL_AT[name] + i:COL_AT[name] + i + n]

    def row(self, name):
        return self.rows[:, ROW_AT[name]:ROW_AT[name] + ROWS[name]]

    def cst(self, name):
        return self.const[:, CONST_AT[name]:CONST_AT[name] + CONSTS[name]]

    def context_in(self, block):
        @block.scalar
        def _(act):
            act.wait_ge(self.sem_named("context_loaded").sem, 16)

    def end_stage(self, block):
        self.stages += 1
        n = 3 * self.stages

        @block.tensor
        def _(pe):
            pe.drain().then_inc(self.stage_end, 1)
            pe.wait_ge(self.stage_end, n)

        @block.vector
        def _(dve):
            dve.drain().then_inc(self.stage_end, 1)
            dve.wait_ge(self.stage_end, n)

        @block.scalar
        def _(act):
            act.drain().then_inc(self.stage_end, 1)
            act.wait_ge(self.stage_end, n)


N_COMMON = CONST_AT["negd"]
N_SLOTS = len(PLAN)
assert N_SLOTS % 2 == 0


def weight_stream(k, block):
    stream = k.io["stream"]

    @block.sync
    def _(sp):
        for s in range(2):
            sp.dma_start(k.raw[:, s], stream[s]).then_inc(k.raw_loaded[s], 16)
        with sp.Fori(1, N_SLOTS // 2) as i:
            for s in range(2):
                sp.wait_ge(k.lo_ready, i * 2 - 1 + s)
                sp.dma_start(k.raw[:, s], stream[bass.ds(i * 2 + s, 1)].rearrange("a p n -> p (a n)")) \
                    .then_inc(k.raw_loaded[s], 16)

    @block.gpsimd
    def _(pool):
        with pool.Fori(0, N_SLOTS // 2) as i:
            for s in range(2):
                pool.wait_ge(k.hi_ready, i * 2 + s + 1)
                pool.tensor_tensor(k.w_lo[:, s], k.raw[:, s], k.w_hi[:, s].bitcast(F32), ALU.subtract) \
                    .then_inc(k.lo_ready, 1)


def refill_hi(k, act, s, turn):
    act.wait_ge(k.raw_loaded[s], turn * 16 + 16)
    act.activation(k.w_hi[:, s], k.raw[:, s], ACT.Copy).then_inc(k.hi_ready, 1)


def products(pe, out, lhs, rhs, start, stop):
    pe.matmul(out, lhs[0], rhs[0], start=start, stop=False)
    pe.matmul(out, lhs[0], rhs[1], start=False, stop=False)
    return pe.matmul(out, lhs[1], rhs[0], start=False, stop=stop)


def dense(k, block, sections, tiles, act_tile=None, dve_tile=None, act_last=None, loop=False,
          dve_chained=0, ada=None):
    first = SECTIONS[sections[0]][0]
    count = sum(SECTIONS[x][1] for x in sections)
    n_slots = 2 if loop else count
    per = [len(tiles(s, k.w_hi[:, 0], k.w_lo[:, 0])) for s in range(n_slots)]
    at = [sum(per[:s]) for s in range(n_slots + 1)]
    turns = count // 2 if loop else 1
    ring = 4 if max(per) <= 2 else 6 if max(per) % 3 == 0 else 8
    n_t = at[-1]
    assert not loop or (n_t % ring == 0 and count % 2 == 0)
    assert not (loop and ada)
    share = ada.share(n_t) if ada else None
    rhs_ready, k.rhs_ready = k.rhs_ready, None

    @block.tensor
    def _(pe):
        def turn(i):
            for s in range(n_slots):
                par = (first + s) % 2
                pe.wait_ge(k.lo_ready, i * 2 + (first + s + 1))
                for n, (cut, pairs) in enumerate(tiles(s, k.w_hi[:, par], k.w_lo[:, par])):
                    t = at[s] + n
                    pe.wait_ge(k.tile_free.sem, i * n_t + k.tile_free.at(t + 1 - ring))
                    out = cut(k.psum[:, t % ring])
                    for j, (lhs, rhs) in enumerate(pairs):
                        if rhs_ready and (j, t) in rhs_ready:
                            pe.wait_ge(k.dve_chain.sem, rhs_ready[j, t])
                        last = products(pe, out, lhs, rhs, j == 0, j == len(pairs) - 1)
                    last.then_inc(k.tile_done.sem, 1)

        if loop:
            with pe.Fori(0, turns) as i:
                turn(i)
        else:
            turn(0)
            if ada:
                pe.wait_ge(k.tile_free.sem, k.tile_free.at(n_t - ring + 1))
                ada.column_sums(pe, k.psum[:, n_t % ring])

    @block.scalar
    def _(act):
        def finish(i, t):
            act.wait_ge(k.finished.sem, i * n_t + k.finished.at(t + 1))
            act_last(act, i, t).then_inc(k.tile_free.sem, 1)

        def turn(i, refill=True):
            if ada:
                ada.first_loads(act)
            for s in range(n_slots):
                for t in range(at[s], at[s + 1]):
                    if ada and t:
                        ada.loads(act, share[t - 1])
                    if act_tile is not None:
                        act.wait_ge(k.tile_done.sem, i * n_t + k.tile_done.at(t + 1))
                        done = act_tile(act, i, t, k.psum[:, t % ring])
                        done.then_inc((k.tile_free if dve_tile is None else k.staged).sem, 1)
                    if act_last is not None and t > 0:
                        finish(i, t - 1)
                act.wait_ge(k.tile_done.sem, i * n_t + k.tile_done.at(at[s + 1]))
                if refill if loop else first + s + 2 < N_SLOTS:
                    refill_hi(k, act, (first + s) % 2, i + (first + s + 2) // 2)
            if act_last is not None:
                finish(i, n_t - 1)
        if loop and first + count == N_SLOTS:
            with act.Fori(0, turns - 1) as i:
                turn(i)
            turn(turns - 1, refill=False)
        elif loop:
            with act.Fori(0, turns) as i:
                turn(i)
        else:
            turn(0)

    if ada and dve_tile is None:
        @block.vector
        def _(dve):
            for t in range(n_t):
                ada.multiply(dve, share[t])
            ada.take(dve, k.psum[:, n_t % ring])

    if dve_tile is not None:
        @block.vector
        def _(dve):
            def turn(i):
                k.dve_chain.loop = i * dve_chained
                for t in range(n_t):
                    if ada:
                        ada.multiply(dve, share[t])
                    source = k.tile_done if act_tile is None else k.staged
                    dve.wait_ge(source.sem, i * n_t + source.at(t + 1))
                    done = dve_tile(dve, i, t, k.psum[:, t % ring])
                    done.then_inc((k.tile_free if act_last is None else k.finished).sem, 1)

            before = k.dve_chain.count
            if loop:
                with dve.Fori(0, turns) as i:
                    turn(i)
                assert k.dve_chain.count - before == dve_chained, k.dve_chain.count - before
                k.dve_chain.count = before + dve_chained * turns
            else:
                turn(0)
                if ada:
                    ada.take(dve, k.psum[:, n_t % ring])
            k.dve_chain.loop = 0

    k.tile_done.stage_over(n_t * turns)
    k.tile_free.stage_over(n_t * turns)
    if act_tile is not None and dve_tile is not None:
        k.staged.stage_over(n_t * turns)
    if act_last is not None:
        k.finished.stage_over(n_t * turns)
    k.end_stage(block)


def feature_major(a, kc, parts, slot_cols=None, chunks=(0, 1)):
    width = SLOT // kc

    def tiles(s, hi, lo):
        hi = hi.rearrange("p (k n) -> p k n", k=kc)
        lo = lo.rearrange("p (k n) -> p k n", k=kc)
        out = []
        use = chunks(s) if callable(chunks) else chunks
        for c in use:
            for t0, t1 in parts:
                out.append((lambda bank, n=t1 - t0: bank[:, 0:n],
                            [((hi[:, j, c * P:(c + 1) * P], lo[:, j, c * P:(c + 1) * P]),
                              (a[0][:, j, t0:t1], a[1][:, j, t0:t1])) for j in range(kc)]))
        return out

    return tiles


def few_rows(a, n, parts):
    def tiles(s, hi, lo):
        hi = hi.rearrange("p (k n) -> p k n", k=KC)
        lo = lo.rearrange("p (k n) -> p k n", k=KC)
        return [(lambda bank, w=t1 - t0: bank[0:n, 0:w],
                 [((hi[:, j, 0:n], lo[:, j, 0:n]), (a[0][:, j, t0:t1], a[1][:, j, t0:t1])) for j in range(KC)])
                for t0, t1 in parts]
    return tiles


def split(k, dve, hi, lo, x):
    k.dve_chain(dve, dve.tensor_copy(hi, x))
    return dve.tensor_tensor(lo, x, hi.bitcast(F32), ALU.subtract)



def setup(k, block):
    loaded = k.sem_named("consts_loaded")
    first_ada = k.ada.group(8, k.ARENA + 65536, k.ARENA + 32768, 7).of(8)
    x1 = k.at("x1", k.ARENA + 49152, [P, KC, S])

    @block.scalar
    def _(act):
        act.dma_start(k.const[:], k.io["consts"][:, 0:N_COMMON]).then_inc(loaded.sem, 16)
        act.dma_start(k.cols[:], k.io["cols"]).then_inc(loaded.sem, 16)
        act.dma_start(k.rows[:], k.io["rows"]).then_inc(loaded.sem, 16)
        for _ in range(4):
            first_ada.load(act)
        act.dma_start(x1[:], k.io["xT"].rearrange("(c p) t -> p c t", p=P)) \
            .then_inc(k.sem_named("residual_loaded").sem, 16)
        for _ in range(3):
            first_ada.load(act)
        for s in range(2):
            refill_hi(k, act, s, 0)
        act.wait_ge(loaded.sem, 48)
        for b, (own, other) in enumerate((("c", "c"), ("c_2", "c_ctx_2"))):
            act.activation(k.cond[:, b, :, 0], k.col(own, 0, KC), ACT.Silu)
            act.activation(k.cond[:, b, :, 1], k.col(other, 0, KC), ACT.Silu)

    @block.vector
    def _(dve):
        dve.nop().then_inc(k.tile_free.sem, 8)
        dve.memset(k.eps[:], EPS)

    k.end_stage(block)
    return first_ada


N_ADA = 72


class Modulation:

    def __init__(self, k):
        self.k = k
        self.loaded = [k.ctx.enter_context(k.nc.semaphore(f"ada_loaded{s}")) for s in range(7)]
        self.place_count = [0] * 7
        self.used = k.ctx.enter_context(k.nc.semaphore("ada_used"))
        self.summed = k.ctx.enter_context(k.nc.semaphore("ada_summed"))
        self.shares = 0
        self.next = 0

    def group(self, slots, ring_at, part_at, places):
        k = self.k
        self.first, self.end, self.places = self.next, self.next + slots, places
        self.next += slots
        self.ring = k.at("ada_ring", ring_at, [P, places, KC, 256])
        self.part_at = part_at
        self.done = self.first
        self.loads_made = self.first
        self.loaded_base = list(self.place_count)
        for j in range(slots):
            self.place_count[j % places] += 16
        return self

    def of(self, slots):
        self.lo, self.hi = self.done, self.done + slots
        assert self.hi <= self.end
        self.done = self.hi
        self.conds = 1 if self.lo < 24 else 2
        self.part = self.k.at("ada_part", self.part_at, [P, slots, 2, 256])
        return self

    def share(self, n_tiles):
        n, at = self.hi - self.lo, [[] for _ in range(n_tiles)]
        for s in range(n):
            at[s * (n_tiles - 2) // n].append(self.lo + s)
        return at

    def load(self, act):
        s = self.loads_made
        place = (s - self.first) % self.places
        act.dma_start(self.ring[:, place], self.k.io["ada"][s].rearrange("p (k n) -> p k n", k=KC)) \
            .then_inc(self.loaded[place], 16)
        self.loads_made += 1

    def first_loads(self, act):
        if self.loads_made == self.first:
            for _ in range(min(self.places, self.end - self.first)):
                self.load(act)

    def loads(self, act, slots):
        for s in slots:
            if self.loads_made < self.end and s + self.places >= self.loads_made:
                act.wait_ge(self.used, s + 1)
                self.load(act)

    def multiply(self, dve, slots):
        k = self.k
        for s in slots:
            place, turn = (s - self.first) % self.places, (s - self.first) // self.places
            dve.wait_ge(self.loaded[place], self.loaded_base[place] + 16 * (turn + 1))
            for j in range(KC):
                for w in range(2) if self.conds == 2 else (j % 2,):
                    out = self.part[:, s - self.lo, w, :]
                    c = k.cond[:, self.conds - 1, j, w:w + 1]
                    x = self.ring[:, place, j, :]
                    if j < (1 if self.conds == 2 else 2):
                        ins = dve.tensor_scalar(out, x, c, None, ALU.mult)
                    else:
                        ins = dve.scalar_tensor_tensor(out, x, c, out, ALU.mult, ALU.add)
                    k.dve_chain.behind(dve, ins, 1)
            dve.wait_ge(k.dve_chain.sem, k.dve_chain.count)
            if self.conds == 1:
                both = self.part[:, s - self.lo]
                k.dve_chain(dve, dve.tensor_tensor(both[:, 0], both[:, 0], both[:, 1], ALU.add))
            dve.nop().then_inc(self.used, 1)

    def column_sums(self, pe, bank):
        pe.wait_ge(self.used, self.hi)
        for s in range(self.hi - self.lo):
            for c in range(2):
                for w in range(self.conds):
                    n = (2 * s + c) * self.conds + w
                    last = pe.matmul(bank[:, n:n + 1], self.part[:, s, w, c * P:(c + 1) * P],
                                     self.k.cst("ones")[:, 0:1], start=True, stop=True)
        last.then_inc(self.summed, 1)
        self.shares += 1

    def take(self, dve, bank):
        k = self.k
        dve.wait_ge(self.summed, self.shares)
        if self.conds == 1:
            c0, c1 = 2 * self.lo, 2 * self.hi
            k.dve_chain(dve, dve.tensor_tensor(k.mod1[:, c0:c1], bank[:, 0:c1 - c0],
                                               k.col("b_ada", c0, c1 - c0), ALU.add))
            return
        c0, c1 = 2 * (self.lo - 24), 2 * (self.hi - 24)
        sums = bank[:, 0:2 * (c1 - c0)].rearrange("p (n w) -> p n w", w=2)
        mod = k.mod2[:].rearrange("p l n w -> p (l n) w")
        for l in range(c0 // 24, (c1 - 1) // 24 + 1):
            a, b = max(c0, 24 * l), min(c1, 24 * l + 24)
            bias = k.col(f"l{l}_b_ada_2", a - 24 * l, b - a).unsqueeze(2).broadcast_to([P, b - a, 2])
            k.dve_chain(dve, dve.tensor_tensor(mod[:, a:b], sums[:, a - c0:b - c0], bias, ALU.add))


def modulation_start(k, block, ada):

    @block.vector
    def _(dve):
        ada.multiply(dve, range(8))

    def last_load():
        @block.scalar
        def _(act):
            ada.loads(act, range(1))

    def finish():
        @block.tensor
        def _(pe):
            ada.column_sums(pe, k.psum[:, 2])

        @block.vector
        def _(dve):
            ada.take(dve, k.psum[:, 2])
            norm_coef(k, dve, 0, "norm1_w")

    return last_load, finish


def norm_coef(k, dve, n, name):
    k.dve_chain(dve, dve.scalar_tensor_tensor(k.coef[:, n], k.mod1[:, 24 * n + 8:24 * n + 16], 1.0,
                                              k.col(name, 0, KC), ALU.add, ALU.mult))


def modulation_end(k, block):
    @block.vector
    def _(dve):
        for l in range(4):
            for w in range(2):
                dve.scalar_tensor_tensor(k.coef2[:, l, :, w], k.mod2[:, l, 8:16, w], 1.0,
                                         k.col(f"l{l}_g_pre_2", 0, KC), ALU.add, ALU.mult)
                ins = dve.tensor_tensor(k.gate2[:, l, :, w], k.mod2[:, l, 16:24, w],
                                        k.col(f"l{l}_g_post_2", 0, KC), ALU.mult)
        k.dve_chain(dve, ins)


def rms_scale(k, block, x, n_chunks, parts, width, rstd, squares, banks=(0, 1)):
    sq = k.sem_named("square_ready")
    summed = k.sem_named("square_summed")

    @block.scalar
    def _(act):
        for c in range(n_chunks):
            if c >= 2:
                act.wait_ge(summed.sem, summed.at(c - 1))
            act.activation(squares[:, c % 2, 0:x.shape[2]], x[:, c, :], ACT.Square).then_inc(sq.sem, 1)
        act.wait_ge(summed.sem, summed.at(n_chunks))
        root_rows(k, act, rstd, parts, width, banks)

    @block.tensor
    def _(pe):
        for c in range(n_chunks):
            pe.wait_ge(sq.sem, sq.at(c + 1))
            for n, (t0, t1) in enumerate(parts):
                last = pe.matmul(k.psum[:, banks[n], 0:t1 - t0], k.cst("ones"), squares[:, c % 2, t0:t1],
                                 start=c == 0, stop=c == n_chunks - 1)
            last.then_inc(summed.sem, 1)

    sq.stage_over(n_chunks)
    summed.stage_over(n_chunks)


def root_rows(k, act, rstd, parts, width, banks):
    for n, (t0, t1) in enumerate(parts):
        k.act_chain(act, act.activation(rstd[:, t0:t1], k.psum[:, banks[n], 0:t1 - t0], ACT.Ln,
                                        bias=k.eps[:], scale=1.0 / width))
    for n, (t0, t1) in enumerate(parts):
        k.act_chain(act, act.activation(rstd[:, t0:t1], rstd[:, t0:t1], ACT.Exp, scale=-0.5))


def pre_norm(k, block, x, a, parts, coef, shift, temp, banks=(0, 1), part_ready=None, then=None,
             at_end=None, after_sums=None):
    squares = k.at("squares", temp, [P, 2, S])
    rstd = k.at("rstd", temp + 8 * S, [P, x.shape[2]])
    h = k.at("h", temp + 8 * S + 4 * x.shape[2], [P, 4, S])
    work = [(c, n, t0, t1) for n, (t0, t1) in enumerate(parts) for c in range(KC)]
    sq, summed = k.sem_named("square_ready"), k.sem_named("square_summed")
    ready, scaled, high = k.sem_named("rstd_ready"), k.sem_named("h_scaled"), k.sem_named("h_high")
    split_at = {}

    def root(act, n):
        act.wait_ge(summed.sem, summed.at(KC * (n + 1)))
        root_rows(k, act, rstd, parts[n:n + 1], D, banks[n:n + 1])
        act.nop().then_inc(ready.sem, 1)

    @block.scalar
    def _(act):
        for i, (c, n, t0, t1) in enumerate(work):
            if part_ready is not None:
                act.wait_ge(part_ready.sem, part_ready.at(i + 1))
            if i >= 2:
                act.wait_ge(summed.sem, summed.at(i - 1))
            act.activation(squares[:, i % 2, 0:t1 - t0], x[:, c, t0:t1], ACT.Square).then_inc(sq.sem, 1)
            if i == KC:
                root(act, 0)
        if then is not None:
            then(act)
        if len(parts) == 1:
            root(act, 0)

    @block.tensor
    def _(pe):
        for i, (c, n, t0, t1) in enumerate(work):
            pe.wait_ge(sq.sem, sq.at(i + 1))
            pe.matmul(k.psum[:, banks[n], 0:t1 - t0], k.cst("ones"), squares[:, i % 2, 0:t1 - t0],
                      start=c == 0, stop=c == KC - 1).then_inc(summed.sem, 1)

    if after_sums is not None:
        after_sums()

    @block.vector
    def _(dve):
        def low(i):
            c, n, t0, t1 = work[i]
            dve.wait_ge(high.sem, high.at(i + 1))
            dve.scalar_tensor_tensor(a[1][:, c, t0:t1], h[:, i % 4, 0:t1 - t0], shift(n, c),
                                     a[0][:, c, t0:t1].bitcast(F32), ALU.add, ALU.subtract) \
                .then_inc(k.dve_chain.sem, 1)
            k.dve_chain.count += 1
            split_at[c, n] = k.dve_chain.count

        for i, (c, n, t0, t1) in enumerate(work):
            if c == 0:
                dve.wait_ge(ready.sem, ready.at(n + 1))
            if i >= 4:
                dve.wait_ge(k.dve_chain.sem, k.dve_chain.count - 1)
            dve.scalar_tensor_tensor(h[:, i % 4, 0:t1 - t0], x[:, c, t0:t1], coef(n, c), rstd[:, t0:t1],
                                     ALU.mult, ALU.mult).then_inc(scaled.sem, 1)
            if i >= 2:
                low(i - 2)
        for i in range(len(work) - 2, len(work)):
            low(i)

    @block.scalar
    def _(act):
        for i, (c, n, t0, t1) in enumerate(work):
            if i == KC:
                root(act, 1)
            act.wait_ge(scaled.sem, scaled.at(i + 1))
            act.activation(a[0][:, c, t0:t1], h[:, i % 4, 0:t1 - t0], ACT.Identity, bias=shift(n, c)) \
                .then_inc(high.sem, 1)
        act.wait_ge(k.dve_chain.sem, split_at[KC - 1, len(parts) - 1])
        if at_end is not None:
            at_end(act)

    sq.stage_over(len(work))
    summed.stage_over(len(work))
    ready.stage_over(len(parts))
    scaled.stage_over(len(work))
    high.stage_over(len(work))
    k.rhs_ready = split_at



def ssd_branch(k, block, a, acc):
    B0 = k.ARENA + 49152
    z = k.at("z", B0, [P, 8, S])
    xbc = k.at("xbc", B0 + 16384, [P, 12, S])
    x_tok = k.at("x_tok", B0 + 40960, [P, 4, 1024])
    b_tok = k.at("b_tok", B0 + 57344, [P, 4, 256])
    h_prev = k.at("h_prev", B0 + 61440, [P, 3, 1024])
    small = B0 + 73728
    full = [(0, S)]

    ada = k.ada.group(16, B0 + 40960, k.ARENA + 32768, 3)
    dense(k, block, ["z"], feature_major(a, KC, full), ada=ada.of(8),
          act_tile=lambda act, i, t, ps: act.activation(z[:, t, :], ps, ACT.Silu))

    pad = k.at("pad", small, [P, 4, S + 3])
    conv = k.at("conv", small + 16 * (S + 3) + 32, [P, 2, S])

    @block.vector
    def _(dve):
        for t in range(4):
            dve.memset(pad[:, t, 0:3], 0.0)
        dve.nop().then_inc(k.dve_chain.sem, 1)
        k.dve_chain.count += 1

    def conv_tile(dve, i, t, ps):
        src, dst = pad[:, t % 4], conv[:, t % 2]
        tap = lambda j: k.col("conv_w", 12 * j + t)
        if t >= 2:
            dve.wait_ge(k.tile_free.sem, k.tile_free.at(t - 1))
        k.dve_chain(dve, dve.tensor_scalar(dst, src[:, 3:3 + S], tap(3), k.col("conv_b", t), ALU.mult, ALU.add))
        for j in (2, 1):
            k.dve_chain(dve, dve.scalar_tensor_tensor(dst, src[:, j:j + S], tap(j), dst, ALU.mult, ALU.add))
        return dve.scalar_tensor_tensor(dst, src[:, 0:S], tap(0), dst, ALU.mult, ALU.add)

    dense(k, block, ["xbc"], feature_major(a, KC, full),
          act_tile=lambda act, i, t, ps: act.activation(pad[:, t % 4, 3:3 + S], ps, ACT.Copy),
          dve_tile=conv_tile, ada=ada.of(8),
          act_last=lambda act, i, t: act.activation(xbc[:, t, :], conv[:, t % 2], ACT.Silu))

    dt = k.at("dt", small, [P, 9, 64])
    raw, e, u, dts, da, acum, nacum, wend, dec = (dt[:, j] for j in range(9))
    c4 = lambda x: x.rearrange("p (c h) -> p c h", c=4)
    bias = lambda name: k.row(name).unsqueeze(1).broadcast_to([P, 4, 16])

    dt_rows = k.at("dt_rows", small + 4096, [16, S])
    dense(k, block, ["dt"], few_rows(a, 16, full),
          act_tile=lambda act, i, t, ps: act.activation(dt_rows[:], ps[0:16, :], ACT.Copy))

    ssd_to_act, ssd_to_dve, ssd_to_pe = (k.sem_named(f"ssd_to_{x}") for x in ("act", "dve", "pe"))
    turned = k.sem_named("turned")

    @block.vector
    def _(dve):
        ch = k.dve_chain
        dve.wait_ge(turned.sem, turned.at(1))
        ch(dve, dve.tensor_tensor(c4(raw), c4(k.psum[:, 2, 0:64]), bias("dt_bias"), ALU.add))
        ch(dve, dve.tensor_scalar(e, raw, -1.0, None, ALU.mult))
        dve.tensor_tensor(e, raw, e, ALU.min).then_inc(ssd_to_act.sem, 1)
        dve.wait_ge(ssd_to_dve.sem, ssd_to_dve.at(1))
        ch(dve, dve.tensor_scalar(u, e, 1.0, None, ALU.add))
        dve.nop().then_inc(ssd_to_act.sem, 1)
        ch(dve, dve.scalar_tensor_tensor(dec, u, -1.0, e, ALU.add, ALU.subtract))
        ch(dve, dve.reciprocal(wend, u))
        ch(dve, dve.tensor_tensor(dec, dec, wend, ALU.mult))
        dve.wait_ge(ssd_to_dve.sem, ssd_to_dve.at(2))
        ch(dve, dve.tensor_tensor(dec, da, dec, ALU.subtract))
        ch(dve, dve.scalar_tensor_tensor(dts, raw, 0.0, dec, ALU.max, ALU.add))
        ch(dve, dve.scalar_tensor_tensor(c4(da), c4(dts), -1.0, bias("a_log"), ALU.mult, ALU.mult))
        dve.nop().then_inc(ssd_to_pe.sem, 1)
        dve.wait_ge(ssd_to_dve.sem, ssd_to_dve.at(3))
        ch(dve, dve.tensor_copy(acum, k.psum[:, 0, 0:64]))
        ch(dve, dve.tensor_scalar(nacum, acum, -1.0, None, ALU.mult))
        dve.tensor_tensor(wend, k.psum[:, 1, 0:64], acum, ALU.subtract).then_inc(ssd_to_act.sem, 1)

    @block.scalar
    def _(act):
        act.wait_ge(ssd_to_act.sem, ssd_to_act.at(1))
        k.act_chain(act, act.activation(e, e, ACT.Exp))
        act.activation(k.row("a_log"), k.row("a_log"), ACT.Exp).then_inc(ssd_to_dve.sem, 1)
        act.wait_ge(ssd_to_act.sem, ssd_to_act.at(2))
        act.activation(da, u, ACT.Ln).then_inc(ssd_to_dve.sem, 1)
        act.wait_ge(ssd_to_act.sem, ssd_to_act.at(3))
        act.activation(wend, wend, ACT.Exp)
        act.activation(dec, k.psum[:, 1, 0:64], ACT.Exp)

    @block.tensor
    def _(pe):
        for c in range(4):
            last = pe.transpose(k.psum[:, 2, 16 * c:16 * c + 16], dt_rows[:, c * P:(c + 1) * P],
                                k.cst("ident")[0:16, 0:16])
        last.then_inc(turned.sem, 1)
        pe.wait_ge(ssd_to_pe.sem, ssd_to_pe.at(1))
        pe.matmul(k.psum[:, 0, 0:64], k.cst("tri"), da, start=True, stop=True)
        pe.matmul(k.psum[:, 1, 0:64], k.cst("ones"), da, start=True, stop=True).then_inc(ssd_to_dve.sem, 1)

    turned.stage_over(1)
    ssd_to_act.stage_over(3)
    ssd_to_dve.stage_over(3)
    ssd_to_pe.stage_over(1)
    k.end_stage(block)

    turned, taken = k.sem_named("turned"), k.sem_named("turned_taken")
    groups = [(f0, c) for c in range(4) for f0 in (0, 4, 8)]

    @block.tensor
    def _(pe):
        for n, (f0, c) in enumerate(groups):
            if n >= 4:
                pe.wait_ge(taken.sem, taken.at(n - 3))
            for f in range(f0, min(f0 + 4, 10)):
                last = pe.transpose(k.psum[:, n % 4, (f - f0) * P:(f - f0 + 1) * P], xbc[:, f, c * P:(c + 1) * P],
                                    k.cst("ident"))
            last.then_inc(turned.sem, 1)

    @block.vector
    def _(dve):
        for n, (f0, c) in enumerate(groups):
            dve.wait_ge(turned.sem, turned.at(n + 1))
            if f0 == 8:
                dve.tensor_copy(b_tok[:, c, :], k.psum[:, n % 4, 0:256]).then_inc(taken.sem, 1)
            else:
                heads = c4(dts)[:, c, 2 * f0:2 * f0 + 8].unsqueeze(2).broadcast_to([P, 8, 64])
                dve.tensor_tensor(x_tok[:, c, f0 * P:f0 * P + 512].rearrange("p (h e) -> p h e", h=8),
                                  k.psum[:, n % 4, :].rearrange("p (h e) -> p h e", h=8), heads,
                                  ALU.mult).then_inc(taken.sem, 1)

    turned.stage_over(len(groups))
    taken.stage_over(len(groups))
    k.end_stage(block)

    xd = k.at("xd", small + 4096, [P, 2, 1024])
    ready, summed = k.sem_named("xd_ready"), k.sem_named("state_summed")

    @block.vector
    def _(dve):
        def scaled(c):
            w = c4(wend)[:, c, :].unsqueeze(2).broadcast_to([P, 16, 64])
            if c >= 2:
                dve.wait_ge(summed.sem, summed.at(c - 1))
            dve.tensor_tensor(xd[:, c % 2].rearrange("p (h e) -> p h e", h=16),
                              x_tok[:, c, :].rearrange("p (h e) -> p h e", h=16), w, ALU.mult).then_inc(ready.sem, 1)

        def state(c):
            dve.wait_ge(summed.sem, summed.at(c + 1))
            ps = k.psum[:, 2 * c:2 * c + 2, :].rearrange("p g n -> p (g n)")
            if c == 0:
                k.dve_chain(dve, dve.tensor_copy(h_prev[:, 0, :], ps))
            else:
                d = c4(dec)[:, c, :].unsqueeze(2).broadcast_to([P, 16, 64])
                k.dve_chain(dve, dve.tensor_tensor(h_prev[:, c, :].rearrange("p (h e) -> p h e", h=16),
                                                   h_prev[:, c - 1, :].rearrange("p (h e) -> p h e", h=16), d,
                                                   ALU.mult))
                k.dve_chain(dve, dve.tensor_tensor(h_prev[:, c, :], ps, h_prev[:, c, :], ALU.add))

        scaled(0)
        scaled(1)
        state(0)
        scaled(2)
        state(1)
        state(2)

    @block.tensor
    def _(pe):
        for c in range(3):
            pe.wait_ge(ready.sem, ready.at(c + 1))
            for g in range(2):
                last = pe.matmul(k.psum[:, 2 * c + g, :], b_tok[:, c, g * P:(g + 1) * P],
                                 xd[:, c % 2, g * 512:(g + 1) * 512], start=True, stop=True)
            last.then_inc(summed.sem, 1)
        for g in range(2):
            for c in range(4):
                last = pe.matmul(k.psum[:, 6 + g, c * P:(c + 1) * P], xbc[:, 8 + g, c * P:(c + 1) * P],
                                 xbc[:, 10 + g, c * P:(c + 1) * P], start=True, stop=True)

    ready.stage_over(3)
    summed.stage_over(3)
    k.end_stage(block)

    cb = k.at("cb", B0 + 57344, [P, 2, 512])
    o = small + 2560
    tri_a = k.at("tri_a", o, [P, 2, 512])
    seg = k.at("seg", o + 4096, [P, 3, 512])
    ea = k.at("ea", o + 10240, [P, 3, 512])
    cs = lambda x: x.rearrange("p (c l) -> p c l", c=4)
    rows_in, rows_out, seg_ready, dec_ready, m_ready, y_used = (
        k.sem_named(n) for n in ("ssd_rows_in", "ssd_rows_out", "ssd_seg_ready", "ssd_decay_ready",
                                 "ssd_m_ready", "ssd_y_used"))

    heads_out = k.sem_named("ssd_heads_out")

    @block.vector
    def _(dve):
        for g in range(2):
            k.dve_chain(dve, dve.tensor_copy(cb[:, g, :], k.psum[:, 6 + g, :]))
        tri = k.cst("tri").unsqueeze(1).broadcast_to([P, 4, P])
        mask = k.cst("mask_le").unsqueeze(1).broadcast_to([P, 4, P])

        def rows(h):
            if h >= 2:
                dve.wait_ge(rows_out.sem, rows_out.at(h - 1))
            d = c4(da)[:, :, h:h + 1].broadcast_to([P, 4, P])
            dve.tensor_tensor(cs(tri_a[:, h % 2]), tri, d, ALU.mult).then_inc(rows_in.sem, 1)

        def segment(h):
            dve.wait_ge(rows_out.sem, rows_out.at(h + 1))
            nac = c4(nacum)[:, :, h:h + 1].broadcast_to([P, 4, P])
            k.dve_chain(dve, dve.tensor_tensor(cs(seg[:, h % 3]), cs(k.psum[:, h % 2, :]), mask, ALU.add))
            dve.tensor_tensor(cs(seg[:, h % 3]), cs(seg[:, h % 3]), nac, ALU.add).then_inc(seg_ready.sem, 1)

        def combine(h):
            g = h // 8
            dve.wait_ge(dec_ready.sem, dec_ready.at(h + 1))
            dve.tensor_tensor(seg[:, h % 3], seg[:, h % 3], cb[:, g, :], ALU.mult)
            dve.tensor_tensor(ea[:, h % 3], ea[:, h % 3], xbc[:, 10 + g, :], ALU.mult).then_inc(m_ready.sem, 1)

        def finish(f):
            dve.wait_ge(heads_out.sem, heads_out.at(2 * f + 2))
            ps = k.psum[:, 2 + f % 2, :]
            k.dve_chain(dve, dve.scalar_tensor_tensor(xbc[:, f, :], xbc[:, f, :], k.col("d_skip", f), ps,
                                                      ALU.mult, ALU.add))
            dve.tensor_tensor(z[:, f, :], z[:, f, :], xbc[:, f, :], ALU.mult).then_inc(y_used.sem, 1)

        rows(0)
        rows(1)
        segment(0)
        for h in range(SSD_HEADS):
            if h + 2 < SSD_HEADS:
                rows(h + 2)
            if h + 1 < SSD_HEADS:
                if h >= 2:
                    dve.wait_ge(heads_out.sem, heads_out.at(h - 1))
                segment(h + 1)
            combine(h)
            if h % 2 == 1 and h >= 3:
                finish(h // 2 - 1)
        finish(7)

    @block.scalar
    def _(act):
        for h in range(SSD_HEADS):
            act.wait_ge(seg_ready.sem, seg_ready.at(h + 1))
            act.activation(seg[:, h % 3], seg[:, h % 3], ACT.Exp)
            act.activation(ea[:, h % 3], k.psum[:, h % 2, :], ACT.Exp).then_inc(dec_ready.sem, 1)

    @block.tensor
    def _(pe):
        def rows(h):
            if h >= 2:
                pe.wait_ge(dec_ready.sem, dec_ready.at(h - 1))
            pe.wait_ge(rows_in.sem, rows_in.at(h + 1))
            pe.matmul(k.psum[:, h % 2, :], k.cst("ones"), tri_a[:, h % 2], start=True, stop=True) \
                .then_inc(rows_out.sem, 1)

        rows(0)
        rows(1)
        for h in range(SSD_HEADS):
            f, off = h // 2, 64 * (h % 2)
            if h + 2 < SSD_HEADS:
                rows(h + 2)
            pe.wait_ge(m_ready.sem, m_ready.at(h + 1))
            if f >= 2 and off == 0:
                pe.wait_ge(y_used.sem, y_used.at(f - 1))
            for c in range(4):
                out = k.psum[off:off + 64, 2 + f % 2, c * P:(c + 1) * P]
                last = pe.matmul(out, x_tok[:, c, h * 64:(h + 1) * 64], seg[:, h % 3, c * P:(c + 1) * P],
                                 start=True, stop=c == 0)
                if c:
                    last = pe.matmul(out, h_prev[:, c - 1, h * 64:(h + 1) * 64], ea[:, h % 3, c * P:(c + 1) * P],
                                     start=False, stop=True)
            last.then_inc(heads_out.sem, 1)

    for s_, n in ((rows_in, 16), (rows_out, 16), (seg_ready, 16), (dec_ready, 16), (m_ready, 16),
                  (y_used, 8), (heads_out, 16)):
        s_.stage_over(n)
    k.end_stage(block)


def gated(k, block, a, b, sections, acc, temp, first):
    sig = k.at("sig", temp, [P, 2, S])
    start, staged = k.tile_free.base, k.staged.base

    def take(act, i, t, ps):
        if t >= 2:
            act.wait_ge(k.staged.sem, i * 4 + (staged + t))
            return act.nop()
        act.wait_ge(k.tile_free.sem, i * 4 + (start + t - 1))
        return act.activation(sig[:, t, :], ps, ACT.Sigmoid)

    def project(dve, i, t, ps):
        if t < 2:
            dve.wait_ge(k.tile_free.sem, i * 4 + (start + t))
            return dve.nop()
        chunk = acc[:, bass.ds(i * 2 + t - 2, 1), :].rearrange("p a n -> p (a n)")
        if first:
            return dve.tensor_tensor(chunk, ps, sig[:, t - 2, :], ALU.mult)
        k.dve_chain(dve, dve.tensor_tensor(sig[:, t - 2, :], ps, sig[:, t - 2, :], ALU.mult))
        return dve.tensor_tensor(chunk, chunk, sig[:, t - 2, :], ALU.add)

    dense(k, block, sections, lambda s, hi, lo: feature_major(b if s else a, KC, [(0, S)])(s, hi, lo),
          loop=True, dve_chained=0 if first else 2, act_tile=take, dve_tile=project)


def ssd_out(k, block, a, acc):
    B0 = k.ARENA + 49152
    z = k.at("z", B0, [P, 8, S])
    rstd = k.at("rstd", B0 + 73728, [P, 2, S])
    squares = k.at("squares", B0 + 73728 + 4096, [P, 2, S])
    y = (k.at("y_hi", B0 + 16384, [P, 8, S], F32R), k.at("y_lo", B0 + 32768, [P, 8, S], F32R))
    for g in range(2):
        rms_scale(k, block, z[:, 4 * g:4 * g + 4, :], 4, [(0, S)], 512, rstd[:, g], squares, banks=(g,))
    k.end_stage(block)

    @block.vector
    def _(dve):
        for f in range(8):
            k.dve_chain(dve, dve.scalar_tensor_tensor(z[:, f, :], z[:, f, :], k.col("ssd_norm_w", f),
                                                      rstd[:, f // 4], ALU.mult, ALU.mult))
            split(k, dve, y[0][:, f, :], y[1][:, f, :], z[:, f, :])

    k.end_stage(block)
    gated(k, block, a, y, [f"{x}{c}" for c in range(4) for x in ("g_ssd", "ssd_out")], acc, B0, True)


def attention(k, block, units, temp, width):
    scores_done, masked, exp_done, scaled, turned, copied, out_done, out_used = (
        k.sem_named(f"att_{x}") for x in ("scores_done", "max_ready", "exp_done", "scaled", "turned", "copied",
                                          "out_done", "out_used"))
    n = len(units)
    wide = 3 if width > 1024 else 2
    prob = k.at("prob", temp, [P, 3, width])
    prob_t = k.at("prob_t", temp + 12 * width, [P, 2, width])
    stat = k.at("stat", temp + 20 * width, [P, 3, 16])
    shared = wide == 3
    o_bank = 6

    def score(u):
        b = wide * (u % 2)
        return k.psum[:, b:b + wide, :].rearrange("p b n -> p (b n)")

    def turned_bank(u):
        return score(u) if shared else k.psum[:, 4:6, :].rearrange("p b n -> p (b n)")

    def out_bank(u):
        return k.psum[:, o_bank + u % 2, :]

    @block.tensor
    def _(pe):
        def scores(u):
            if u >= 2 and shared:
                pe.wait_ge(copied.sem, copied.at(u - 1))
            elif u >= 2:
                pe.wait_ge(exp_done.sem, exp_done.at(u - 1))
            ps = score(u)
            for col, cols, pairs in units[u]["qk"]:
                for j, (lhs, rhs) in enumerate(pairs):
                    last = pe.matmul(ps[:, col:col + cols], lhs, rhs, start=j == 0, stop=j == len(pairs) - 1)
            last.then_inc(scores_done.sem, 1)

        def turn(u):
            pe.wait_ge(scaled.sem, scaled.at(u + 1))
            if u and not shared:
                pe.wait_ge(copied.sem, copied.at(u))
            for j in range(len(units[u]["pv"])):
                last = pe.transpose(turned_bank(u)[:, j * P:(j + 1) * P], prob[:, u % 3, j * P:(j + 1) * P],
                                    k.cst("ident"))
            last.then_inc(turned.sem, 1)

        def values(u):
            pe.wait_ge(copied.sem, copied.at(u + 1))
            if u >= 2:
                pe.wait_ge(out_used.sem, out_used.at(u - 1))
            pv, r = units[u]["pv"], units[u]["rows"]
            for j, v in enumerate(pv):
                last = pe.matmul(out_bank(u)[r[0]:r[1], 0:P], v, prob_t[:, u % 2, j * P:(j + 1) * P],
                                 start=j == 0, stop=j == len(pv) - 1)
            last.then_inc(out_done.sem, 1)

        for u in range(n + 3):
            if u < n and not shared:
                scores(u)
            if 2 <= u < n + 2:
                turn(u - 2)
            if u >= 3 and not shared:
                values(u - 3)
            if u < n and shared:
                scores(u)
            if 2 <= u < n + 2 and shared:
                values(u - 2)

    @block.vector
    def _(dve):
        ch = k.dve_chain

        def step(u):
            new, old = u < n, 1 <= u <= n
            added = totalled = inverted = None
            if new:
                un, ps, st = units[u], score(u), stat[:, u % 3]
                if u >= 3:
                    dve.wait_ge(turned.sem, turned.at(u - 2))
                dve.wait_ge(scores_done.sem, scores_done.at(u + 1))
                for col, cols, mask in un["masks"]:
                    last = dve.tensor_tensor(ps[:, col:col + cols], ps[:, col:col + cols], mask, ALU.add)
                if un["masks"]:
                    added = ch.mark(last)
            if old:
                before, st_old = units[u - 1], stat[:, (u - 1) % 3]
                dve.wait_ge(exp_done.sem, exp_done.at(u))
                total = 8 + len(before["ranges"]) + (before["sink"] is not None)
                totalled = ch.mark(dve.tensor_reduce(st_old[:, 14:15], st_old[:, 8:total], AX.X, ALU.add))
            if new:
                if added:
                    dve.wait_ge(ch.sem, added)
                for j, (r0, r1) in enumerate(un["ranges"]):
                    last = dve.tensor_reduce(st[:, j:j + 1], ps[:, r0:r1], AX.X, ALU.max)
                largest = ch.mark(last)
            if old:
                dve.wait_ge(ch.sem, totalled)
                inverted = ch.mark(dve.reciprocal(st_old[:, 15:16], st_old[:, 14:15]))
            if new:
                dve.wait_ge(ch.sem, largest)
                m = st[:, 0:1]
                if len(un["ranges"]) > 1:
                    ch(dve, dve.tensor_reduce(st[:, 4:5], st[:, 0:len(un["ranges"])], AX.X, ALU.max))
                    m = st[:, 4:5]
                if un["sink"] is None:
                    dve.tensor_scalar(st[:, 5:6], m, -un["scale"], None, ALU.mult).then_inc(masked.sem, 1)
                else:
                    dve.tensor_scalar(st[:, 5:6], m, -un["scale"], un["neg_sink"], ALU.mult, ALU.min) \
                        .then_inc(masked.sem, 1)
            if old:
                dve.wait_ge(ch.sem, inverted)
                w = sum(r1 - r0 for r0, r1 in before["ranges"])
                dve.tensor_scalar(prob[:, (u - 1) % 3, 0:w], prob[:, (u - 1) % 3, 0:w], st_old[:, 15:16], None,
                                  ALU.mult).then_inc(scaled.sem, 1)

        for u in range(n + 6):
            if 5 <= u < n + 5 and "finish" in units[u - 5]:
                dve.wait_ge(out_used.sem, out_used.at(u - 4))
                units[u - 5]["finish"](dve)
            step(u)

    @block.scalar
    def _(act):
        def exps(u):
            un, ps, st = units[u], score(u), stat[:, u % 3]
            act.wait_ge(masked.sem, masked.at(u + 1))
            at = 0
            if un["sink"] is not None:
                act.activation(st[:, 8 + len(un["ranges"]):9 + len(un["ranges"])], un["sink"], ACT.Exp,
                               bias=st[:, 5:6])
            for j, (r0, r1) in enumerate(un["ranges"]):
                last = act.activation(prob[:, u % 3, at:at + r1 - r0], ps[:, r0:r1], ACT.Exp, bias=st[:, 5:6],
                                      scale=un["scale"], accum_out=st[:, 8 + j:9 + j])
                at += r1 - r0
            last.then_inc(exp_done.sem, 1)

        def copy(u):
            act.wait_ge(turned.sem, turned.at(u + 1))
            if u >= 2:
                act.wait_ge(out_done.sem, out_done.at(u - 1))
            w = P * len(units[u]["pv"])
            act.activation(prob_t[:, u % 2, 0:w], turned_bank(u)[:, 0:w], ACT.Copy).then_inc(copied.sem, 1)

        def take(u):
            act.wait_ge(out_done.sem, out_done.at(u + 1))
            r = units[u]["rows"]
            act.activation(units[u]["out"], out_bank(u)[r[0]:r[1], 0:P], ACT.Copy).then_inc(out_used.sem, 1)

        for u in range(n + 3):
            if 2 <= u < n + 2:
                copy(u - 2)
            if u < n:
                exps(u)
            if 2 <= u < n + 2 and shared:
                take(u - 2)
            if u >= 3 and not shared:
                take(u - 3)

    for s_ in (scores_done, masked, exp_done, scaled, turned, copied, out_done, out_used):
        s_.stage_over(n)
    k.end_stage(block)


def dilated_attention(k, block, a, acc):
    B0 = k.ARENA + 49152
    qkv = k.at("qkv", B0, [P, 9, S])
    v = qkv[:, 6:9, :].rearrange("p a n -> p (a n)").rearrange("p (b n) -> p b n", b=4)
    o = k.at("o", B0 + 18432, [P, 4, S])
    o_s = (k.at("o_hi", B0 + 26624, [P, 4, S], F32R), k.at("o_lo", B0 + 34816, [P, 4, S], F32R))
    tables = k.at("tables", B0 + 43008, [P, 4, 512])
    bias = k.at("bias", B0 + 51200, [P, 3, 512])
    temp = B0 + 57344
    squares = k.at("squares", temp, [P, 2, S])
    rstd = k.at("rstd", temp + 4096, [P, 6, S])
    v_rows = k.at("v_rows", temp + 33792, [P, S])
    turned = k.sem_named("turned")
    slopes = alibi_slopes(12)
    scale = float(P) ** -0.5
    loaded = k.sem_named("tables_loaded")
    normed, sq, summed = (k.sem_named(x) for x in ("qk_normed", "square_ready", "square_summed"))

    @block.scalar
    def _(act):
        n0 = CONST_AT["negd"]
        act.dma_start(tables[:], k.io["consts"][:, n0:n0 + 2048].rearrange("p (a n) -> p a n", a=4)) \
            .then_inc(loaded.sem, 16)

    for j in range(4):
        def tiles(s, hi, lo):
            if s < 3:
                return feature_major(a, KC, [(0, S)])(s, hi, lo)
            if s == 4:
                return feature_major(a, KC, [(0, S)], chunks=(0,))(s, hi, lo)
            hi = hi.rearrange("p (k n) -> p k n", k=KC)
            lo = lo.rearrange("p (k n) -> p k n", k=KC)
            return [(lambda bank: bank[:, 0:256],
                     [((a[0][:, c, b * P:(b + 1) * P], a[1][:, c, b * P:(b + 1) * P]),
                       (hi[:, c, :], lo[:, c, :])) for c in range(KC)]) for b in range(4)]

        def take(act, i, t, ps):
            if t < 6:
                return act.activation(qkv[:, t, :], ps, ACT.Copy)
            if t == 10:
                return act.activation(v_rows[:], ps, ACT.Copy)
            return act.activation(v[:, t - 6, 0:256], ps[:, 0:256], ACT.Copy)

        dense(k, block, [f"qkv{j}"], tiles, act_tile=take, ada=k.ada.group(4, temp, temp + 24576, 3).of(4))

        @block.scalar
        def _(act):
            for t in range(6):
                if t >= 2:
                    act.wait_ge(summed.sem, summed.at(t - 1))
                act.activation(squares[:, t % 2], qkv[:, t, :], ACT.Square).then_inc(sq.sem, 1)
            for t in range(6):
                act.wait_ge(summed.sem, summed.at(t + 1))
                last = act.activation(rstd[:, t], k.psum[:, t, :], ACT.Ln, bias=k.eps[:], scale=1.0 / P)
            k.act_chain(act, last)
            for t in range(6):
                act.activation(rstd[:, t], rstd[:, t], ACT.Exp, scale=-0.5).then_inc(normed.sem, 1)

        @block.tensor
        def _(pe):
            for b in range(4):
                last = pe.transpose(k.psum[:, 6, b * P:(b + 1) * P], v_rows[:, b * P:(b + 1) * P], k.cst("ident"))
            last.then_inc(turned.sem, 1)
            for t in range(6):
                pe.wait_ge(sq.sem, sq.at(t + 1))
                pe.matmul(k.psum[:, t, :], k.cst("ones"), squares[:, t % 2], start=True, stop=True) \
                    .then_inc(summed.sem, 1)

        @block.vector
        def _(dve):
            if j == 0:
                dve.wait_ge(loaded.sem, loaded.at(16))
            for g in range(3):
                dve.scalar_tensor_tensor(bias[:, g], tables[:, 0], slopes[4 * g + j] / scale, tables[:, 1 + g],
                                         ALU.mult, ALU.add)
            dve.wait_ge(turned.sem, turned.at(1))
            dve.tensor_copy(v[:, :, 256:384], k.psum[:, 6, :].rearrange("p (b n) -> p b n", b=4))
            for t in range(6):
                dve.wait_ge(normed.sem, normed.at(t + 1))
                dve.scalar_tensor_tensor(qkv[:, t, :], qkv[:, t, :], k.col("q_norm_w" if t < 3 else "k_norm_w"),
                                         rstd[:, t], ALU.mult, ALU.mult)

        turned.stage_over(1)
        sq.stage_over(6)
        summed.stage_over(6)
        normed.stage_over(6)
        if j == 0:
            loaded.stage_over(16)
        k.end_stage(block)

        units = []
        for b in (0, 3, 2, 1):
            q = lambda g: qkv[:, g, b * P:(b + 1) * P]
            lo0 = max(0, b - 1)
            k0s = [lo0, 0, 0]
            qk, masks, ranges, pv = [], [], [], []
            for g in range(3):
                n = (b + 1 - k0s[g]) * P
                qk.append((512 * g, n, [(q(g), qkv[:, 3 + g, k0s[g] * P:(b + 1) * P])]))
                masks.append((512 * g, n, bias[:, g, 512 - n:512]))
                ranges.append((512 * g, 512 * g + n))
                pv += [v[:, kb, g * P:(g + 1) * P] for kb in range(k0s[g], b + 1)]
            units.append(dict(qk=qk, masks=masks, ranges=ranges, scale=scale, sink=None, pv=pv, rows=(0, P),
                              out=o[:, j, b * P:(b + 1) * P]))
        attention(k, block, units, temp, 1280)

    @block.vector
    def _(dve):
        for j in range(4):
            split(k, dve, o_s[0][:, j, :], o_s[1][:, j, :], o[:, j, :])

    k.end_stage(block)
    gated_wide(k, block, a, o_s, acc, B0 + 43008)


def gated_wide(k, block, a, b, acc, temp):
    y = k.at("y_part", temp, [P, 4, S])
    sig = k.at("sig", temp + 8192, [P, 4, S])

    def tiles(s, hi, lo):
        if s % 3 == 0:
            return feature_major(b, 4, [(0, S)], chunks=range(4))(s, hi, lo)
        return feature_major(a, KC, [(0, S)])(s, hi, lo)

    def take(act, i, t, ps):
        c, n = divmod(t, 8)
        if n >= 4:
            return act.activation(sig[:, n - 4, :], ps, ACT.Sigmoid)
        if c:
            act.wait_ge(k.tile_free.sem, k.tile_free.at(n + 5))
        return act.activation(y[:, n, :], ps, ACT.Copy)

    def gate(dve, i, t, ps):
        c, n = divmod(t, 8)
        if n < 4:
            dve.wait_ge(k.tile_free.sem, k.tile_free.at(t))
            return dve.nop()
        s = sig[:, n - 4, :]
        k.dve_chain(dve, dve.tensor_tensor(s, s, y[:, n - 4, :], ALU.mult))
        return dve.tensor_tensor(acc[:, 4 * c + n - 4, :], acc[:, 4 * c + n - 4, :], s, ALU.add)

    dense(k, block, ["attn_out0", "g_attn0", "attn_out1", "g_attn1"], tiles, act_tile=take, dve_tile=gate)


def pool_branch(k, block, a, acc):
    B0 = k.ARENA + 49152
    PAD = 16
    u = k.at("u", B0, [P, 8, S + PAD])
    win = k.at("win", B0 + 17408, [P, 2, 2, S + PAD])
    m = (k.at("m_hi", B0 + 26112, [P, 8, S], F32R), k.at("m_lo", B0 + 42496, [P, 8, S], F32R))
    inv = k.at("inv", B0 + 58880, [P, 64])
    x = (k.at("x_hi", B0 + 59392, [P, 8, S], F32R), k.at("x_lo", B0, [P, 8, S], F32R))
    loaded = k.sem_named("tables_loaded")

    @block.vector
    def _(dve):
        k.dve_chain(dve, dve.memset(u[:, :, 0:PAD], 0.0))
        k.dve_chain(dve, dve.memset(win[:, :, :, 0:PAD], 0.0))

    @block.scalar
    def _(act):
        n0 = CONST_AT["pool_inv"]
        act.dma_start(inv[:], k.io["consts"][:, n0:n0 + 64]).then_inc(loaded.sem, 16)

    def pool_tile(dve, i, f, ps):
        ch = k.dve_chain
        if f == 0:
            dve.wait_ge(loaded.sem, loaded.at(16))
        g = f // 2
        w = 2 << g
        src = u[:, f]
        for d in range(g + 1):
            step = 1 << d
            dst = win[:, f % 2, d % 2]
            ch(dve, dve.tensor_tensor(dst[:, PAD:], src[:, PAD:], src[:, PAD - step:PAD + S - step], ALU.add))
            src = dst
        cur = u[:, f, PAD:]
        mean = win[:, f % 2, (g + 1) % 2]
        ch(dve, dve.tensor_tensor(mean[:, PAD:PAD + 16], src[:, PAD:PAD + 16], inv[:, 16 * g:16 * g + 16],
                                  ALU.mult))
        ch(dve, dve.tensor_scalar(mean[:, PAD + 16:], src[:, PAD + 16:], 1.0 / w, None, ALU.mult))
        ch(dve, dve.tensor_tensor(cur, mean[:, PAD:], cur, ALU.subtract))
        return split(k, dve, m[0][:, f, :], m[1][:, f, :], cur)

    dense(k, block, ["u"], feature_major(a, KC, [(0, S)]), dve_tile=pool_tile,
          act_tile=lambda act, i, t, ps: act.activation(u[:, t, PAD:], ps, ACT.Copy))
    loaded.stage_over(16)

    def mix_tiles(s, hi, lo):
        if s:
            return []
        hi = hi.rearrange("p (k n) -> p k n", k=KC)
        lo = lo.rearrange("p (k n) -> p k n", k=KC)
        return [(lambda bank: bank,
                 [((hi[:, 2 * g + j, c * P:(c + 1) * P], lo[:, 2 * g + j, c * P:(c + 1) * P]),
                   (m[0][:, 2 * g + j, :], m[1][:, 2 * g + j, :])) for j in range(2)])
                for g in range(4) for c in range(2)]

    mixed = k.at("mixed", B0 + 17408, [P, 4, S])

    def scaled(dve, i, t, ps):
        y = mixed[:, t % 4, :]
        k.dve_chain(dve, dve.tensor_scalar(y, ps, k.col("pool_scale", t), None, ALU.mult))
        return split(k, dve, x[0][:, t, :], x[1][:, t, :], y)

    dense(k, block, ["mix"], mix_tiles, dve_tile=scaled)
    gated(k, block, a, x, [f"{x_}{c}" for c in range(4) for x_ in ("g_pool", "pool_out")], acc, B0 + 26112,
          False)


def first_block(k, block, first_ada):
    A0 = k.ARENA
    B0 = A0 + 49152
    full = [(0, S)]
    a = (k.at("a_hi", A0, [P, KC, S], F32R), k.at("a_lo", A0 + 16384, [P, KC, S], F32R))
    acc = k.at("acc", A0 + 32768, [P, KC, S])
    x_in = k.io["xT"].rearrange("(c p) t -> p c t", p=P)
    x1 = k.at("x1", B0, [P, KC, S])
    loaded = k.sem_named("residual_loaded")
    last_load, finish = modulation_start(k, block, first_ada)
    last_load()

    @block.scalar
    def _(act):
        act.wait_ge(loaded.sem, loaded.at(16))

    pre_norm(k, block, x1, a, full, lambda n, c: k.coef[:, 0, c:c + 1],
             lambda n, c: k.mod1[:, c:c + 1], A0 + 122880, after_sums=finish)
    loaded.stage_over(16)
    ssd_branch(k, block, a, acc)
    ssd_out(k, block, a, acc)
    dilated_attention(k, block, a, acc)
    pool_branch(k, block, a, acc)

    m = (k.at("m_hi", B0, [P, KC, S], F32R), k.at("m_lo", B0 + 16384, [P, KC, S], F32R))
    both = k.at("x_in", B0 + 32768, [P, KC, T2])
    x = both[:, :, 0:S]

    @block.vector
    def _(dve):
        for c in range(KC):
            split(k, dve, m[0][:, c, :], m[1][:, c, :], acc[:, c, :])

    k.end_stage(block)
    loaded = k.sem_named("residual_loaded")

    @block.scalar
    def _(act):
        act.dma_start(x, x_in).then_inc(loaded.sem, 16)
        act.dma_start(both[:, :, S:T2], k.io["ctxT"].rearrange("(c p) t -> p c t", p=P)) \
            .then_inc(k.sem_named("context_loaded").sem, 16)

    @block.vector
    def _(dve):
        norm_coef(k, dve, 1, "norm2_w")
        dve.wait_ge(loaded.sem, loaded.at(16))

    def add(dve, i, t, ps):
        return dve.scalar_tensor_tensor(x[:, t, :], ps, k.mod1[:, 16 + t:17 + t], x[:, t, :], ALU.mult, ALU.add)

    dense(k, block, ["out"], feature_major(m, KC, full), dve_tile=add)
    loaded.stage_over(16)

    pre_norm(k, block, x, a, full, lambda n, c: k.coef[:, 1, c:c + 1],
             lambda n, c: k.mod1[:, 24 + c:25 + c], B0)

    hid = (k.at("hid_hi", B0, [P, KC, S], F32R), k.at("hid_lo", B0 + 16384, [P, KC, S], F32R))
    r = k.at("r", A0 + 32768, [P, 4, S])
    ada = k.ada.group(32, B0 + 57344, B0 + 81920, 3)
    for b in range(4):
        def square(dve, i, t, ps):
            y = r[:, t % 4, :]
            k.dve_chain(dve, dve.tensor_tensor(y, y, y, ALU.mult))
            return split(k, dve, hid[0][:, t, :], hid[1][:, t, :], y)

        dense(k, block, [f"ff1_{b}"], feature_major(a, KC, full),
              act_tile=lambda act, i, t, ps: act.activation(r[:, t % 4, :], ps, ACT.Relu), dve_tile=square,
              ada=ada.of(4))

        def add_ff(dve, i, t, ps):
            return dve.scalar_tensor_tensor(x[:, t, :], ps, k.mod1[:, 40 + t:41 + t], x[:, t, :], ALU.mult,
                                            ALU.add)

        dense(k, block, [f"ff2_{b}"], feature_major(hid, KC, full), dve_tile=add_ff, ada=ada.of(4))
    modulation_end(k, block)



LAT, CTX = (0, S), (S, T2)


def rotate(k, block, chunks, temp, cosines=None):
    t_sin = k.at("t_sin", temp, [P, 2, S])
    swapped, done = k.sem_named("swapped"), k.sem_named("swap_used")

    @block.tensor
    def _(pe):
        for n, c in enumerate(chunks):
            if n >= 2:
                pe.wait_ge(done.sem, done.at(n - 1))
            pe.matmul(k.psum[:, n % 2, :], k.cst("swap"), c, start=True, stop=True).then_inc(swapped.sem, 1)

    @block.vector
    def _(dve):
        for n, c in enumerate(chunks):
            dve.wait_ge(swapped.sem, swapped.at(n + 1))
            if cosines is None:
                dve.tensor_tensor(c, c, k.cst("cos"), ALU.mult)
            k.dve_chain(dve, dve.tensor_tensor(t_sin[:, n % 2], k.psum[:, n % 2, :], k.cst("sin"), ALU.mult))
            dve.tensor_tensor(c, c if cosines is None else cosines[n], t_sin[:, n % 2], ALU.add) \
                .then_inc(done.sem, 1)

    swapped.stage_over(len(chunks))
    done.stage_over(len(chunks))
    k.end_stage(block)


def token_major(a, blocks, slot_cols, width):
    def tiles(s, hi, lo):
        hi = hi.rearrange("p (k n) -> p k n", k=KC)
        lo = lo.rearrange("p (k n) -> p k n", k=KC)
        return [(lambda bank: bank[:, 0:slot_cols],
                 [((a[0][:, j, b * P:(b + 1) * P], a[1][:, j, b * P:(b + 1) * P]),
                   (hi[:, j, 0:slot_cols], lo[:, j, 0:slot_cols])) for j in range(KC)]) for b in blocks]
    return tiles


def layer_norm_in(k, block, l, a, x_at, temp, part_ready=None, banks=(0, 1)):
    x = k.at("x_in", x_at, [P, KC, T2])
    xres = k.io["xres"].rearrange("(c p) t -> p c t", p=P)
    stored = k.sem_named("stored")

    def save(act):
        act.dma_start(xres, x[:]).then_inc(stored.sem, 16)

    def saved(act):
        act.wait_ge(stored.sem, stored.at(16))

    pre_norm(k, block, x[:], a, [LAT, CTX], lambda n, c: k.coef2[:, l, c, n:n + 1],
             lambda n, c: k.mod2[:, l, c, n:n + 1], temp, banks, part_ready, save, saved)
    stored.stage_over(16)


def layer_out(k, block, l, section, b, parts, y_at, x_at, sum_at, temp, following=None):
    w = parts[-1][1]
    y = k.at("y", y_at, [P, KC, w])
    x = k.at("x_in", x_at, [P, KC, w])
    total = k.at("total", sum_at, [P, w])
    square = k.at("square", sum_at + 4 * w, [P, 2, S])
    rstd = k.at("rstd_y", temp, [P, w])
    n_parts = len(parts)
    loaded, part_ready = k.sem_named("residual_loaded"), k.sem_named("part_ready")
    ready, summed = k.sem_named("rstd_ready"), k.sem_named("square_summed")

    def chunk(i, t):
        t0, t1 = parts[t % n_parts]
        return y[:, bass.ds(i * 4 + t // n_parts, 1), t0:t1].rearrange("p a n -> p (a n)")

    @block.scalar
    def _(act):
        act.dma_start(x[:], k.io["xres"].rearrange("(c p) t -> p c t", p=P)[:, :, 0:w]).then_inc(loaded.sem, 16)

    @block.vector
    def _(dve):
        k.dve_chain(dve, dve.memset(total[:], 0.0))

    def add_square(dve, i, t, ps):
        t0, t1 = parts[t % n_parts]
        sq = square[:, t % 2, 0:t1 - t0]
        k.dve_chain(dve, dve.tensor_tensor(sq, chunk(i, t), chunk(i, t), ALU.mult))
        return dve.tensor_tensor(total[:, t0:t1], total[:, t0:t1], sq, ALU.add)

    dense(k, block, [section], feature_major(b, KC, parts), loop=True, dve_chained=4 * n_parts,
          act_tile=lambda act, i, t, ps: act.activation(chunk(i, t), ps[:, 0:parts[t % n_parts][1]
                                                                        - parts[t % n_parts][0]], ACT.Copy),
          dve_tile=add_square)

    @block.tensor
    def _(pe):
        for n, (t0, t1) in enumerate(parts):
            last = pe.matmul(k.psum[:, n, 0:t1 - t0], k.cst("ones"), total[:, t0:t1], start=True, stop=True)
        last.then_inc(summed.sem, 1)

    @block.scalar
    def _(act):
        act.wait_ge(summed.sem, summed.at(1))
        root_rows(k, act, rstd, parts, D, (0, 1))
        act.nop().then_inc(ready.sem, 1)

    @block.vector
    def _(dve):
        dve.wait_ge(loaded.sem, loaded.at(16))
        dve.wait_ge(ready.sem, ready.at(1))
        def gated(i):
            c, n, t0, t1 = work[i]
            return k.dve_chain.mark(dve.scalar_tensor_tensor(
                y[:, c, t0:t1], y[:, c, t0:t1], k.gate2[:, l, c, n:n + 1], rstd[:, t0:t1], ALU.mult, ALU.mult))

        work = [(c, n, t0, t1) for n, (t0, t1) in enumerate(parts) for c in range(KC)]
        done = gated(0)
        for i, (c, n, t0, t1) in enumerate(work):
            following_done = gated(i + 1) if i + 1 < len(work) else None
            dve.wait_ge(k.dve_chain.sem, done)
            dve.tensor_tensor(x[:, c, t0:t1], x[:, c, t0:t1], y[:, c, t0:t1], ALU.add).then_inc(part_ready.sem, 1)
            done = following_done

    summed.stage_over(1)
    ready.stage_over(1)
    loaded.stage_over(16)
    if following is not None:
        layer_norm_in(k, block, following[0], following[1], x_at, temp + 4 * w, part_ready, (2, 3))
        part_ready.stage_over(KC * n_parts)
        return
    stored = k.sem_named("stored")
    out = k.io["outT"].rearrange("(c p) t -> p c t", p=P)

    @block.scalar
    def _(act):
        for half in range(2):
            act.wait_ge(part_ready.sem, part_ready.at(4 * half + 4))
            if half:
                act.wait_ge(stored.sem, stored.at(16))
            act.dma_start(out[:, 4 * half:4 * half + 4, :], x[:, 4 * half:4 * half + 4, :]) \
                .then_inc(stored.sem, 16)
        act.wait_ge(stored.sem, stored.at(32))

    k.end_stage(block)


def finish_chunk(k, o, z, b, c, t0, t1):
    def finish(dve):
        k.dve_chain(dve, dve.tensor_tensor(o[:, c, t0:t1], o[:, c, t0:t1], z[:, c, t0:t1], ALU.mult))
        split(k, dve, b[0][:, c, t0:t1], b[1][:, c, t0:t1], o[:, c, t0:t1])
    return finish


def gqa_layer(k, block, l):
    A0, R0 = k.ARENA, k.ARENA + 49152
    a = (k.at("a2_hi", A0, [P, KC, T2], F32R), k.at("a2_lo", A0 + 24576, [P, KC, T2], F32R))
    both = l < 3
    if l == 0:
        k.context_in(block)
        layer_norm_in(k, block, l, a, R0 + 32768, R0)
    parts = [LAT, CTX] if both else [LAT]
    w = parts[-1][1]
    np_ = len(parts)
    q = k.at("gq", R0, [P, 8, T2])
    kk = k.at("gk", R0 + 24576, [P, 2, T2])
    v = k.at("gv", R0 + 30720, [P, 6, 256])
    z = k.at("gz", R0 + 36864, [P, 8, T2])
    temp = R0 + 61440

    def into(dst, func, parts):
        n = len(parts)
        return lambda act, i, t, ps: act.activation(
            dst[:, bass.ds(i * 4 + t // n, 1), parts[t % n][0]:parts[t % n][1]].rearrange("p a n -> p (a n)"),
            ps[:, 0:parts[t % n][1] - parts[t % n][0]], func)

    dense(k, block, [f"A{l}q"], feature_major(a, KC, parts), loop=True, act_tile=into(q, ACT.Copy, parts))
    dense(k, block, [f"A{l}k"], feature_major(a, KC, [LAT, CTX]), act_tile=into(kk, ACT.Copy, [LAT, CTX]))
    dense(k, block, [f"A{l}v"], token_major(a, range(6), 256, 256),
          act_tile=lambda act, i, t, ps: act.activation(v[:, t, :], ps[:, 0:256], ACT.Copy))
    chunks = [q[:, c, 0:S] for c in range(8)] + [kk[:, c, 0:S] for c in range(2)]
    cos_part = k.at("cos_part", temp + 4096, [P, 10, S])

    @block.vector
    def _(dve):
        for n, c in enumerate(chunks):
            dve.tensor_tensor(cos_part[:, n], c, k.cst("cos"), ALU.mult)

    dense(k, block, [f"A{l}z"], feature_major(a, KC, parts), loop=True, act_tile=into(z, ACT.Silu, parts))
    rotate(k, block, chunks, temp, [cos_part[:, n] for n in range(10)])

    sinks = k.row(f"l{l}_sink_2")
    neg_sinks = k.at("neg_sinks", temp + 20 * 640 + 256, [P, 16])

    @block.vector
    def _(dve):
        k.dve_chain(dve, dve.tensor_scalar(neg_sinks[:], sinks, -1.0, None, ALU.mult))

    def unit_of(pos, b):
        h = HEAD_ORDER[pos]
        r0, kv = 64 * (pos % 2), h // 4
        ks = kk[r0:r0 + 64, kv // 2]
        vs = lambda kb: v[:, kb, kv * 64:kv * 64 + 64]
        qb = q[r0:r0 + 64, pos // 2, b * P:(b + 1) * P]
        unit = dict(qk=[(0, 256, [(qb, ks[:, S:T2])])], masks=[], scale=A_SCALE, sink=sinks[:, h:h + 1],
                    neg_sink=neg_sinks[:, h:h + 1], pv=[vs(4), vs(5)], rows=(r0, r0 + 64), out=qb)
        if b < 4:
            for n, kb in enumerate(range(max(0, b - 1), min(3, b + 1) + 1)):
                unit["qk"].append((256 + n * P, P, [(qb, ks[:, kb * P:(kb + 1) * P])]))
                if kb != b:
                    unit["masks"].append((256 + n * P, P, k.cst("mask_le" if kb < b else "mask_ge")))
                unit["pv"].append(vs(kb))
        unit["ranges"] = [(0, P * len(unit["pv"]))]
        if pos % 2 and b in (3, 5):
            unit["finish"] = finish_chunk(k, q, z, a, pos // 2, *(LAT if b == 3 else CTX))
        return unit

    units = [unit_of(pos, b) for pos in range(16) for b in range(4)]
    if both:
        units += [unit_of(pos, b) for pos in range(16) for b in (4, 5)]
    attention(k, block, units, temp, 640)
    layer_out(k, block, l, f"A{l}o", a, parts, R0, R0 + 24576, R0 + 49152, R0 + 56320,
              (1, a) if both else None)


def mla_layer(k, block):
    l = 1
    A0, R0 = k.ARENA, k.ARENA + 49152
    a = (k.at("a2_hi", A0, [P, KC, T2], F32R), k.at("a2_lo", A0 + 24576, [P, KC, T2], F32R))
    both = [LAT, CTX]
    z = k.at("mz", R0, [P, 8, T2])
    raw = k.at("m_raw", R0 + 24576, [P, 4, T2])
    low = (k.at("low_hi", R0 + 73728, [P, 3, T2], F32R), k.at("low_lo", R0 + 82944, [P, 3, T2], F32R))
    q = k.at("mq", A0, [P, 8, T2])
    qr = k.at("mqr", A0 + 24576, [P, 4, T2])
    kpe = k.at("kpe", A0 + 36864, [P, T2])
    kn = k.at("mk", R0 + 24576, [P, 8, T2])
    v = k.at("mv", R0 + 49152, [P, 6, 1024])

    def into(dst, func, base=0):
        return lambda act, i, t, ps: act.activation(
            dst[:, base + t // 2, both[t % 2][0]:both[t % 2][1]], ps[:, 0:both[t % 2][1] - both[t % 2][0]], func)

    dense(k, block, ["Bin"], feature_major(a, KC, both), act_tile=into(raw, ACT.Copy))
    dense(k, block, ["Bz"], feature_major(a, KC, both), act_tile=into(z, ACT.Silu))

    squares = k.at("squares", A0 + 40960, [P, 2, T2])
    rstd = k.at("rstd2", R0 + 36864, [P, 2, T2])
    rms_scale(k, block, raw[:, 0:2, :], 2, both, 256, rstd[:, 0], squares, banks=(0, 1))
    rms_scale(k, block, raw[:, 2:3, :], 1, both, 128, rstd[:, 1], squares, banks=(2, 3))
    k.end_stage(block)

    @block.vector
    def _(dve):
        for c in range(3):
            g = k.col("l1_g_qa_2", c) if c < 2 else k.col("l1_g_kva_2")
            k.dve_chain(dve, dve.scalar_tensor_tensor(raw[:, c, :], raw[:, c, :], g, rstd[:, c // 2], ALU.mult,
                                                      ALU.mult))
            split(k, dve, low[0][:, c, :], low[1][:, c, :], raw[:, c, :])
        dve.tensor_copy(kpe[:], raw[:, 3, :])

    k.end_stage(block)
    rotate(k, block, [kpe[:, 0:S]], A0 + 40960)

    dense(k, block, ["Bq"],
          lambda s, hi, lo: feature_major([x[:, 0:2, :] for x in low], 2, both,
                                          chunks=range(8 if s == 0 else 4))(s, hi, lo),
          act_tile=lambda act, i, t, ps: (into(q, ACT.Copy) if t < 16 else into(qr, ACT.Copy, -8))(act, i, t, ps))

    kv = [x[:, 2:3, :] for x in low]

    def kv_tiles(s, hi, lo):
        if s:
            return []
        out = feature_major(kv, 1, both, chunks=range(8))(s, hi, lo)
        for b in range(6):
            for c in range(2):
                cols = slice(1024 + 512 * c, 1536 + 512 * c)
                out.append((lambda bank: bank,
                            [((kv[0][:, 0, b * P:(b + 1) * P], kv[1][:, 0, b * P:(b + 1) * P]),
                              (hi[:, cols], lo[:, cols]))]))
        return out

    def take(act, i, t, ps):
        if t < 16:
            return into(kn, ACT.Copy)(act, i, t, ps)
        b, c = divmod(t - 16, 2)
        return act.activation(v[:, b, 512 * c:512 * c + 512], ps, ACT.Copy)

    dense(k, block, ["Bk"], kv_tiles, act_tile=take)
    rotate(k, block, [qr[:, c, 0:S] for c in range(4)], R0 + 73728)

    b2 = (k.at("b2_hi", R0 + 24576, [P, KC, T2], F32R), k.at("b2_lo", A0, [P, KC, T2], F32R))
    units = []
    for h in range(8):
        r0 = 64 * (h % 2)
        for b in range(6):
            t = slice(b * P, (b + 1) * P)
            keys = [LAT, CTX] if b < 4 else [CTX]
            qk = [(512 * n, k1 - k0, [(q[:, h, t], kn[:, h, k0:k1]), (qr[r0:r0 + 64, h // 2, t],
                                                                     kpe[r0:r0 + 64, k0:k1])])
                  for n, (k0, k1) in enumerate(keys)]
            blocks = range(6) if b < 4 else (4, 5)
            units.append(dict(qk=qk, masks=[], ranges=[(0, P * len(blocks))], scale=B_SCALE, sink=None,
                              pv=[v[:, kb, h * P:(h + 1) * P] for kb in blocks], rows=(0, P), out=q[:, h, t]))
        units[-1]["finish"] = finish_chunk(k, q, z, b2, h, 0, T2)
    attention(k, block, units, R0 + 73728, 768)
    layer_out(k, block, l, "Bo", b2, both, R0 + 49152, R0, R0 + 73728, R0 + 24576, (2, a))


def second_block(k, block):
    gqa_layer(k, block, 0)
    mla_layer(k, block)
    mlstm_layer(k, block)
    gqa_layer(k, block, 3)


def mlstm_layer(k, block):
    l = 2
    A0, R0 = k.ARENA, k.ARENA + 49152
    a = (k.at("a2_hi", A0, [P, KC, T2], F32R), k.at("a2_lo", A0 + 24576, [P, KC, T2], F32R))
    both = [LAT, CTX]
    H, KS = 4, P ** -0.5
    qk = k.at("cqk", R0, [P, 8, T2])
    v = k.at("cv", R0 + 24576, [P, 6, 1024])
    k_tok = k.at("ck_tok", R0 + 49152, [P, 6, 512])
    hsum = k.at("hsum", R0 + 61440, [P, 6, 1024])
    gates = k.at("c_gates", R0 + 86016, [P, 6, 16])

    pad = k.at("c_pad", R0 + 49152, [P, 8, S + 4])
    conv = k.at("c_conv", R0 + 49152 + 32 * (S + 4), [P, 2, S])

    @block.vector
    def _(dve):
        for t in range(8):
            n = S if t % 2 == 0 else SC
            dve.memset(pad[:, t, 0:2], 0.0)
            k.dve_chain(dve, dve.memset(pad[:, t, 2 + n:4 + n], 0.0))

    def conv_tile(dve, i, t, ps):
        c, n = t // 2, (S if t % 2 == 0 else SC)
        src, dst = pad[:, t % 8], conv[:, t % 2, 0:n]
        tap = lambda j: k.col("l2_conv_2", 8 * j + c)
        if t >= 2:
            dve.wait_ge(k.tile_free.sem, k.tile_free.at(t - 1))
        k.dve_chain(dve, dve.tensor_scalar(dst, src[:, 0:n], tap(0), None, ALU.mult))
        for j in (1, 2, 3):
            k.dve_chain(dve, dve.scalar_tensor_tensor(dst, src[:, j:j + n], tap(j), dst, ALU.mult, ALU.add))
        return dve.scalar_tensor_tensor(dst, src[:, 4:4 + n], tap(4), dst, ALU.mult, ALU.add)

    def span(t):
        n = S if t % 2 == 0 else SC
        return n, (S if t % 2 else 0)

    dense(k, block, ["Cqk"], feature_major(a, KC, both),
          act_tile=lambda act, i, t, ps: act.activation(pad[:, t % 8, 2:2 + span(t)[0]], ps[:, 0:span(t)[0]],
                                                        ACT.Copy),
          dve_tile=conv_tile,
          act_last=lambda act, i, t: act.activation(qk[:, t // 2, span(t)[1]:span(t)[1] + span(t)[0]],
                                                    conv[:, t % 2, 0:span(t)[0]], ACT.Silu))
    dense(k, block, ["Cv"], token_major(a, range(6), 256, 256),
          act_tile=lambda act, i, t, ps: act.activation(v[:, t % 6, 256 * (t // 6):256 * (t // 6) + 256],
                                                        ps[:, 0:256], ACT.Copy))
    gate_rows = k.at("c_gate_rows", R0 + 88064, [16, T2])
    dense(k, block, ["Cg"], few_rows(a, 16, both),
          act_tile=lambda act, i, t, ps: act.activation(gate_rows[:, both[t][0]:both[t][1]],
                                                        ps[0:16, 0:both[t][1] - both[t][0]], ACT.Copy))

    gate_part = k.at("gate_part", R0 + 49152, [P, 3, 6, 256])
    saved = [k.sem_named(f"gate_saved{n}") for n in range(3)]

    def save(act, slot):
        act.wait_ge(k.tile_free.sem, k.tile_free.at(6 * (slot % 4) + 6))
        act.dma_start(k.io["gates"][slot], gate_part[:, slot % 3].rearrange("p b n -> p (b n)")) \
            .then_inc(saved[slot % 3].sem, 16)

    for section, func, s0 in (("Cog", ACT.Sigmoid, 0), ("Cz", ACT.Silu, 4)):
        def take_gate(act, i, t, ps, func=func, s0=s0):
            slot, b = s0 + t // 6, t % 6
            if b == 0 and t:
                save(act, slot - 1)
            if b == 0 and slot >= 3:
                act.wait_ge(saved[slot % 3].sem, 16 * (slot // 3))
            return act.activation(gate_part[:, slot % 3, b, :], ps[:, 0:256], func)

        def times_g_head(dve, i, t, ps):
            cell = gate_part[:, (4 + t // 6) % 3, t % 6, :]
            g_head = k.row("l2_g_head_2")[:, 256 * (t // 6):256 * (t // 6) + 256]
            return dve.tensor_tensor(cell, cell, g_head, ALU.mult)

        dense(k, block, [section], token_major(a, range(6), 256, 256), act_tile=take_gate,
              dve_tile=times_g_head if s0 else None)

        @block.scalar
        def _(act):
            act.dma_start(k.io["gates"][s0 + 3], gate_part[:, (s0 + 3) % 3].rearrange("p b n -> p (b n)")) \
                .then_inc(saved[(s0 + 3) % 3].sem, 16)
            if s0:
                for n in range(3):
                    act.wait_ge(saved[n].sem, 16 * len(range(n, 8, 3)))

    k.end_stage(block)

    turned, taken = k.sem_named("turned"), k.sem_named("turned_taken")

    gates_turned = k.sem_named("c_gates_turned")

    @block.tensor
    def _(pe):
        for b in range(6):
            last = pe.transpose(k.psum[:, 4, 16 * b:16 * b + 16], gate_rows[:, b * P:(b + 1) * P],
                                k.cst("ident")[0:16, 0:16])
        last.then_inc(gates_turned.sem, 1)
        for b in range(6):
            if b >= 2:
                pe.wait_ge(taken.sem, taken.at(b - 1))
            for h in range(H):
                last = pe.transpose(k.psum[:, b % 2, h * P:(h + 1) * P], qk[:, 4 + h, b * P:(b + 1) * P],
                                    k.cst("ident"))
            last.then_inc(turned.sem, 1)

    o = A0
    g48 = lambda name, n: k.at(name, o + 192 * n, [P, 2, 6, H])
    ig, f, e, u, t1, cum, g = (g48(f"c_{x}", n) for n, x in enumerate(("ig", "f", "e", "u", "t1", "cum", "g")))
    tot = g48("c_tot", 7)
    flat = lambda x: x[:].rearrange("p d b h -> p (d b h)")
    to_act, to_dve, to_pe = (k.sem_named(f"ssd_to_{x}") for x in ("act", "dve", "pe"))

    @block.vector
    def _(dve):
        ch = k.dve_chain
        dve.wait_ge(gates_turned.sem, gates_turned.at(1))
        ch(dve, dve.tensor_tensor(gates[:], k.psum[:, 4, 0:96].rearrange("p (b g) -> p b g", b=6),
                                  k.row("l2_b_gate_2").unsqueeze(1).broadcast_to([P, 6, 16]), ALU.add))
        for b in range(6):
            dve.wait_ge(turned.sem, turned.at(b + 1))
            dve.tensor_scalar(k_tok[:, b, :], k.psum[:, b % 2, :], KS, None, ALU.mult).then_inc(taken.sem, 1)
        for d in range(2):
            dve.tensor_copy(ig[:, d], gates[:, :, 8 * d:8 * d + 4])
            ch(dve, dve.tensor_copy(f[:, d], gates[:, :, 8 * d + 4:8 * d + 8]))
        ch(dve, dve.tensor_scalar(flat(e), flat(f), -1.0, None, ALU.mult))
        dve.tensor_tensor(flat(e), flat(f), flat(e), ALU.min).then_inc(to_act.sem, 1)
        dve.wait_ge(to_dve.sem, to_dve.at(1))
        ch(dve, dve.tensor_scalar(flat(u), flat(e), 1.0, None, ALU.add))
        dve.nop().then_inc(to_act.sem, 1)
        ch(dve, dve.scalar_tensor_tensor(flat(g), flat(u), -1.0, flat(e), ALU.add, ALU.subtract))
        ch(dve, dve.reciprocal(flat(t1), flat(u)))
        ch(dve, dve.tensor_tensor(flat(g), flat(g), flat(t1), ALU.mult))
        dve.wait_ge(to_dve.sem, to_dve.at(2))
        ch(dve, dve.tensor_tensor(flat(g), flat(cum), flat(g), ALU.subtract))
        ch(dve, dve.scalar_tensor_tensor(flat(f), flat(f), 0.0, flat(g), ALU.min, ALU.subtract))
        dve.nop().then_inc(to_pe.sem, 1)
        dve.wait_ge(to_dve.sem, to_dve.at(3))
        ch(dve, dve.tensor_copy(flat(cum), k.psum[:, 2, 0:48]))
        dve.tensor_copy(flat(tot), k.psum[:, 3, 0:48])
        dve.tensor_tensor(flat(g), flat(ig), flat(cum), ALU.subtract)

    @block.scalar
    def _(act):
        act.wait_ge(to_act.sem, to_act.at(1))
        act.activation(flat(e), flat(e), ACT.Exp).then_inc(to_dve.sem, 1)
        act.wait_ge(to_act.sem, to_act.at(2))
        act.activation(flat(cum), flat(u), ACT.Ln).then_inc(to_dve.sem, 1)

    @block.tensor
    def _(pe):
        pe.wait_ge(to_pe.sem, to_pe.at(1))
        pe.matmul(k.psum[:, 2, 0:24], k.cst("tri"), f[:, 0].rearrange("p b h -> p (b h)"), start=True, stop=True)
        pe.matmul(k.psum[:, 2, 24:48], k.cst("triT"), f[:, 1].rearrange("p b h -> p (b h)"), start=True, stop=True)
        pe.matmul(k.psum[:, 3, 0:48], k.cst("ones"), flat(f), start=True, stop=True).then_inc(to_dve.sem, 1)

    turned.stage_over(6)
    taken.stage_over(6)
    to_act.stage_over(2)
    to_dve.stage_over(3)
    to_pe.stage_over(1)
    k.end_stage(block)

    o = A0 + 2048
    diag = k.at("c_diag", o, [P, 2, H, P])
    gm = k.at("c_gm", o + 4096, [P, 2, H, P])
    prob = k.at("c_prob", o + 8192, [P, 2, H, P])
    prob_t = k.at("c_prob_t", o + 12288, [P, 2, H * P])
    ke = k.at("c_ke", o + 16384, [P, 2, H, P])
    state = k.at("c_state", o + 20480, [P, 2, H, 256])
    norm = k.at("c_norm", o + 28672, [P, 2, H])
    m_st = k.at("c_m", o + 28704, [P, 2, H])
    st = k.at("c_small", o + 28736, [P, 2, 16, H])
    order = [[4, 5, 0, 1, 2, 3], [5, 4, 3, 2, 1, 0]]
    steps = [(j, d, order[d][j]) for j in range(6) for d in range(2)]
    N = len(steps)
    names = ("diag_in", "scores", "sub_in", "exp_out", "ke_in", "prob_in", "turn", "turn_copied", "num2", "num1",
             "outs_taken", "local", "state_new", "nq_read", "nq_done", "n2_taken")
    (diag_in, scores, sub_in, exp_out, ke_in, prob_in, turn, turn_copied, num2, num1, outs_taken, local,
     state_new, nq_read, nq_done, n2_taken) = (k.sem_named(f"c_{x}") for x in names)
    bc = lambda x: x.unsqueeze(2).broadcast_to([P, H, P])
    ident4 = k.cst("ident").unsqueeze(1).broadcast_to([P, H, P])
    heads = lambda x: x.rearrange("p (h n) -> p h n", h=H)
    n2 = lambda h: k.psum[:, 4 + h // 2, 256 * (h % 2):256 * (h % 2) + 256]
    n1 = lambda h: k.psum[:, 2 + h // 2, 256 * (h % 2):256 * (h % 2) + 256]
    lc = lambda h: k.psum[:, 6 + h // 2, 256 * (h % 2):256 * (h % 2) + 256]

    @block.tensor
    def _(pe):
        def values(s):
            b = steps[s][2]
            pe.wait_ge(turn_copied.sem, turn_copied.at(s + 1))
            if s:
                pe.wait_ge(outs_taken.sem, outs_taken.at(s))
            for h in range(H):
                last = pe.matmul(n1(h), prob_t[:, s % 2, h * P:(h + 1) * P], v[:, b, 256 * h:256 * h + 256],
                                 start=True, stop=True)
            last.then_inc(num1.sem, 1)

        for s, (j, d, b) in enumerate(steps):
            t = slice(b * P, (b + 1) * P)
            if s:
                pe.wait_ge(nq_read.sem, nq_read.at(s))
                pe.wait_ge(turn_copied.sem, turn_copied.at(s))
            for h in range(H):
                pe.matmul(k.psum[:, 0, h * P:(h + 1) * P], qk[:, h, t], qk[:, 4 + h, t], start=True, stop=True)
            pe.wait_ge(diag_in.sem, diag_in.at(s + 1))
            pe.matmul(k.psum[:, 1, :], k.cst("ones"), diag[:, s % 2].rearrange("p h n -> p (h n)"), start=True,
                      stop=True).then_inc(scores.sem, 1)
            if s:
                values(s - 1)
                pe.wait_ge(n2_taken.sem, n2_taken.at(s))
            if s >= 2:
                pe.wait_ge(state_new.sem, state_new.at(s - 1))
            for h in range(H):
                last = pe.matmul(n2(h), qk[:, h, t], state[:, d, h, :], start=True, stop=True)
            last.then_inc(num2.sem, 1)
            pe.wait_ge(prob_in.sem, prob_in.at(s + 1))
            for h in range(H):
                pe.matmul(k.psum[:, 0, h:h + 1], qk[:, h, t], norm[:, d, h:h + 1], start=True, stop=True)
            pe.wait_ge(ke_in.sem, ke_in.at(s + 1))
            for h in range(H):
                last = pe.matmul(k.psum[:, 0, 8 + h:9 + h], ke[:, s % 2, h, :], k.cst("ones")[:, 0:1], start=True,
                                 stop=True)
            last.then_inc(nq_done.sem, 1)
            for h in range(H):
                last = pe.transpose(k.psum[:, 1, h * P:(h + 1) * P], prob[:, s % 2, h, :], k.cst("ident"))
            last.then_inc(turn.sem, 1)
            if s:
                pe.wait_ge(state_new.sem, state_new.at(s))
            for h in range(H):
                last = pe.matmul(lc(h), ke[:, s % 2, h, :], v[:, b, 256 * h:256 * h + 256], start=True, stop=True)
            last.then_inc(local.sem, 1)
        values(N - 1)

    @block.scalar
    def _(act):
        for s, (j, d, b) in enumerate(steps):
            act.wait_ge(sub_in.sem, sub_in.at(s + 1))
            act.activation(gm[:, s % 2], gm[:, s % 2], ACT.Exp)
            act.activation(st[:, s % 2, 0:5], st[:, s % 2, 0:5], ACT.Exp).then_inc(exp_out.sem, 1)
            act.wait_ge(turn.sem, turn.at(s + 1))
            act.activation(prob_t[:, s % 2], k.psum[:, 1, :], ACT.Copy).then_inc(turn_copied.sem, 1)

    @block.vector
    def _(dve):
        ch = k.dve_chain
        ch(dve, dve.memset(m_st[:], NEG))
        ch(dve, dve.memset(norm[:], 0.0))
        ch(dve, dve.memset(state[:], 0.0))

        def diagonal(s):
            j, d, b = steps[s]
            if s >= 2:
                dve.wait_ge(scores.sem, scores.at(s - 1))
            dve.tensor_tensor(diag[:, s % 2], ident4, bc(g[:, d, b, :]), ALU.mult).then_inc(diag_in.sem, 1)

        def gates_of(s):
            j, d, b = steps[s]
            S_ = lambda n: st[:, s % 2, n]
            mask = k.cst("mask_ge" if d == 0 else "mask_le").unsqueeze(1).broadcast_to([P, H, P])
            dve.wait_ge(scores.sem, scores.at(s + 1))
            rows = heads(k.psum[:, 1, :])
            ch(dve, dve.tensor_tensor(gm[:, s % 2], rows, mask, ALU.add))
            dve.tensor_reduce(S_(8), gm[:, s % 2], AX.X, ALU.max)
            ch(dve, dve.tensor_reduce(S_(9), rows, AX.X, ALU.max))
            m = m_st[:, d, :]
            ch(dve, dve.tensor_tensor(S_(10), S_(8), m, ALU.max))
            ch(dve, dve.tensor_tensor(S_(11), S_(9), m, ALU.max))
            dve.tensor_tensor(gm[:, s % 2], gm[:, s % 2], bc(S_(10)), ALU.subtract)
            dve.tensor_tensor(S_(0), m, S_(10), ALU.subtract)
            dve.scalar_tensor_tensor(S_(1), cum[:, d, b, :], -1.0, S_(10), ALU.mult, ALU.subtract)
            dve.tensor_tensor(S_(2), g[:, d, b, :], S_(9), ALU.subtract)
            dve.tensor_tensor(S_(3), m, S_(11), ALU.subtract)
            ch(dve, dve.tensor_tensor(S_(4), S_(9), S_(11), ALU.subtract))
            ch(dve, dve.tensor_tensor(m, tot[:, d, b, :], S_(11), ALU.add))
            dve.nop().then_inc(sub_in.sem, 1)

        def weights_of(s):
            j, d, b = steps[s]
            S_ = lambda n: st[:, s % 2, n]
            dve.wait_ge(exp_out.sem, exp_out.at(s + 1))
            ch(dve, dve.scalar_tensor_tensor(prob[:, s % 2], heads(k.psum[:, 0, :]), KS, gm[:, s % 2], ALU.mult,
                                             ALU.mult))
            dve.nop().then_inc(prob_in.sem, 1)
            dve.tensor_tensor(ke[:, s % 2], heads(k_tok[:, b, :]), bc(S_(2)), ALU.mult).then_inc(ke_in.sem, 1)
            if s + 1 < N:
                diagonal(s + 1)
            ch(dve, dve.tensor_reduce(S_(12), prob[:, s % 2], AX.X, ALU.add))
            dve.wait_ge(nq_done.sem, nq_done.at(s + 1))
            dve.tensor_tensor(S_(13), k.psum[:, 0, 0:H], S_(0), ALU.mult)
            ch(dve, dve.tensor_tensor(S_(8), k.psum[:, 0, 8:8 + H], S_(4), ALU.mult))
            dve.nop().then_inc(nq_read.sem, 1)
            dve.tensor_tensor(norm[:, d, :], norm[:, d, :], S_(3), ALU.mult)
            ch(dve, dve.tensor_tensor(S_(12), S_(12), S_(13), ALU.add))
            dve.tensor_tensor(norm[:, d, :], norm[:, d, :], S_(8), ALU.add)
            ch(dve, dve.tensor_scalar(S_(13), S_(12), -1.0, None, ALU.mult))
            ch(dve, dve.tensor_tensor(S_(12), S_(12), S_(13), ALU.max))
            ch(dve, dve.tensor_tensor(S_(12), S_(12), S_(1), ALU.max))
            ch(dve, dve.reciprocal(S_(14), S_(12)))
            ch(dve, dve.tensor_tensor(S_(15), S_(14), S_(0), ALU.mult))
            dve.wait_ge(num2.sem, num2.at(s + 1))
            for h in range(H):
                last = dve.tensor_scalar(state[:, d, h, :], state[:, d, h, :], S_(3)[:, h:h + 1], None, ALU.mult)
            ch(dve, last)
            dve.wait_ge(local.sem, local.at(s + 1))
            for h in range(H):
                last = dve.scalar_tensor_tensor(state[:, d, h, :], lc(h), S_(4)[:, h:h + 1], state[:, d, h, :],
                                                ALU.mult, ALU.add)
            last.then_inc(state_new.sem, 1)

        def outputs_of(s, src, column, taken):
            b = steps[s][2]
            for h in range(H):
                hs = hsum[:, b, 256 * h:256 * h + 256]
                scale = st[:, s % 2, column, h:h + 1]
                if src is n2 and b not in [x[2] for x in steps[:s]]:
                    last = dve.tensor_scalar(hs, src(h), scale, None, ALU.mult)
                else:
                    last = dve.scalar_tensor_tensor(hs, src(h), scale, hs, ALU.mult, ALU.add)
            last.then_inc(taken.sem, 1)

        diagonal(0)
        gates_of(0)
        for s in range(N):
            weights_of(s)
            outputs_of(s, n2, 15, n2_taken)
            if s + 1 < N:
                gates_of(s + 1)
            dve.wait_ge(num1.sem, num1.at(s + 1))
            dve.wait_ge(n2_taken.sem, n2_taken.at(s + 1))
            outputs_of(s, n1, 14, outs_taken)

    for x in (diag_in, scores, sub_in, exp_out, ke_in, prob_in, turn, turn_copied, num2, num1, outs_taken, local,
              state_new, nq_read, nq_done, n2_taken):
        x.stage_over(N)
    k.end_stage(block)

    og = k.at("c_og", A0, [P, H, 6, 256])
    z = k.at("c_z", A0 + 24576, [P, H, 6, 256])
    ms = k.at("c_ms", R0 + 86400, [P, 24])
    squares = k.at("c_sq", R0 + 86528, [P, 2, 256])
    b2 = (k.at("b3_hi", R0, [P, KC, T2], F32R), k.at("b3_lo", R0 + 24576, [P, KC, T2], F32R))
    og_first, og_loaded, z_loaded, gated_h, rooted, normed, high = (
        k.sem_named(f"c_{x}") for x in ("og_first", "og_loaded", "z_loaded", "gated_h", "rooted", "normed", "high"))
    head = lambda h: hsum[:, :, 256 * h:256 * h + 256]
    saved_gates = k.io["gates"].rearrange("s p n -> p s n")
    cells = [(h, b) for h in range(H) for b in range(6)]

    @block.scalar
    def _(act):
        act.dma_start(og[:, 0].rearrange("p b n -> p (b n)"), k.io["gates"][0]).then_inc(og_first.sem, 16)
        act.dma_start(og[:, 1:4].rearrange("p h b n -> p h (b n)"), saved_gates[:, 1:4]) \
            .then_inc(og_loaded.sem, 16)
        act.dma_start(z[:].rearrange("p h b n -> p h (b n)"), saved_gates[:, 4:8]).then_inc(z_loaded.sem, 16)
        for n, (h, b) in enumerate(cells):
            if b == 0:
                act.wait_ge(gated_h.sem, gated_h.at(h + 1))
            if n >= 2:
                act.wait_ge(k.act_chain.sem, k.act_chain.count - 1)
            act.activation(squares[:, n % 2], hsum[:, b, 256 * h:256 * h + 256], ACT.Square,
                           accum_out=ms[:, n:n + 1]).then_inc(k.act_chain.sem, 1)
            k.act_chain.count += 1
        act.wait_ge(k.act_chain.sem, k.act_chain.count)
        k.act_chain(act, act.activation(ms[:], ms[:], ACT.Ln, bias=k.eps[:], scale=1.0 / 256))
        act.activation(ms[:], ms[:], ACT.Exp, scale=-0.5).then_inc(rooted.sem, 1)
        for n in range(16):
            t0, t1 = both[n % 2]
            act.wait_ge(turned.sem, turned.at(n + 1))
            act.activation(b2[0][:, n // 2, t0:t1], k.psum[:, n % 4, 0:t1 - t0], ACT.Copy).then_inc(high.sem, 1)

    @block.vector
    def _(dve):
        def low(n):
            t0, t1 = both[n % 2]
            dve.wait_ge(high.sem, high.at(n + 1))
            dve.tensor_tensor(b2[1][:, n // 2, t0:t1], k.psum[:, n % 4, 0:t1 - t0],
                              b2[0][:, n // 2, t0:t1].bitcast(F32), ALU.subtract).then_inc(taken.sem, 1)

        dve.wait_ge(og_first.sem, og_first.at(16))
        for h in range(H):
            if h == 1:
                dve.wait_ge(og_loaded.sem, og_loaded.at(16))
            dve.tensor_tensor(head(h), head(h), og[:, h], ALU.mult).then_inc(gated_h.sem, 1)
        dve.wait_ge(z_loaded.sem, z_loaded.at(16))
        dve.wait_ge(rooted.sem, rooted.at(1))
        for n, (h, b) in enumerate(cells):
            hs = hsum[:, b, 256 * h:256 * h + 256]
            ins = dve.scalar_tensor_tensor(hs, hs, ms[:, n:n + 1], z[:, h, b, :], ALU.mult, ALU.mult)
            if b == 5:
                ins.then_inc(normed.sem, 1)
                if h:
                    for m in range(4 * h - 4, 4 * h):
                        low(m)
        for m in range(12, 16):
            low(m)

    @block.tensor
    def _(pe):
        for n in range(16):
            c, half = divmod(n, 2)
            if n % 4 == 0:
                pe.wait_ge(normed.sem, normed.at(n // 4 + 1))
            if n >= 4:
                pe.wait_ge(taken.sem, taken.at(n - 3))
            for j, b in enumerate((0, 1, 2, 3) if half == 0 else (4, 5)):
                last = pe.transpose(k.psum[:, n % 4, j * P:(j + 1) * P], hsum[:, b, c * P:(c + 1) * P],
                                    k.cst("ident"))
            last.then_inc(turned.sem, 1)

    turned.stage_over(16)
    taken.stage_over(16)
    k.end_stage(block)
    a3 = (k.at("a2_hi", A0, [P, KC, T2], F32R), k.at("a2_lo", A0 + 24576, [P, KC, T2], F32R))
    layer_out(k, block, l, "Co", b2, both, A0, R0 + 49152, R0 + 73728, R0, (3, a3))


def build(nc, io):
    with ExitStack() as ctx:
        k = Kernel(nc, ctx, io)
        block = ctx.enter_context(nc.Block())
        weight_stream(k, block)
        k.ada = Modulation(k)
        first_ada = setup(k, block)
        first_block(k, block, first_ada)
        second_block(k, block)



def layout(inputs):
    f = lambda name: np.asarray(inputs[name])
    w = {}
    for name, _, _, _ in PLAN:
        if name not in w:
            w[name] = f("w_pool_mix").reshape(1024, 256) if name == "mix" else \
                f(name)[0] if f(name).ndim == 3 else f(name)
    for name in ("l0_w_out_2", "l3_w_out_2"):
        w[name] = w[name][np.asarray(HEAD_COLS)]
    stream = np.zeros((N_SLOTS, P, SLOT), np.float32)
    for s, (name, r0, r1, cols) in enumerate(PLAN):
        kc = (r1 - r0) // P
        part = w[name][r0:r1][:, np.asarray(cols)]
        if kc * len(cols) <= SLOT:
            width = SLOT // kc
            stream[s].reshape(P, kc, width)[:, :, :len(cols)] = part.reshape(kc, P, len(cols)).transpose(1, 0, 2)
    ada = np.zeros((72, P, SLOT), np.float32)
    for s, (name, c) in enumerate(ada_plan()):
        m = f(name)[0] if f(name).ndim == 3 else f(name)
        ada[s] = m[:, 256 * c:256 * c + 256].reshape(KC, P, 256).transpose(1, 0, 2).reshape(P, SLOT)
    cols = np.zeros((P, N_COLS), np.float32)
    for name, n in COLS.items():
        v = f(name)
        if name == "d_skip":
            v = np.repeat(v, SSD_P)
        if name == "l2_conv_2" or name == "conv_w":
            v = v.reshape(-1)
        cols[:, COL_AT[name]:COL_AT[name] + n] = v.reshape(n, P).T
    rows = np.zeros((P, N_ROWS), np.float32)
    for name, n in ROWS.items():
        rows[:, ROW_AT[name]:ROW_AT[name] + n] = f(name).reshape(1, n)
    return {"stream": stream, "ada": ada, "cols": cols, "rows": rows, "consts": constants(),
            "xT": np.ascontiguousarray(f("x")[0].T), "ctxT": np.ascontiguousarray(f("ctx_2")[0].T)}


def kernel(**inputs):
    import concourse.bacc as bacc
    from concourse.bass_utils import run_bass_kernel_spmd

    nc = bacc.Bacc("TRN2", target_bir_lowering=False, num_devices=1)
    arrays = layout(inputs)
    io = {name: nc.dram_tensor(name, a.shape, F32, kind="ExternalInput").ap() for name, a in arrays.items()}
    io["outT"] = nc.dram_tensor("outT", (D, S), F32, kind="ExternalOutput").ap()
    io["gates"] = nc.dram_tensor("gates", (8, P, 6 * 256), F32).ap()
    io["xres"] = nc.dram_tensor("xres", (D, T2), F32).ap()
    build(nc, io)
    result = run_bass_kernel_spmd(nc, [arrays], core_ids=[0])
    return np.ascontiguousarray(result.results[0]["outT"].T)[None]
```
